# Optimizing a Trainium2 kernel written in Bass

```python
import math
import jax, jax.numpy as jnp
from jax import lax
import numpy as np

D_MODEL = 2048
BATCH = 1
SEQ = 256
DEPTH = 1

CHUNK = 64

CONV_WIDTH = D_MODEL
CONV_K = 3
SSM_WIDTH = D_MODEL // 2
SSM_GROUP = 16
SSM_GROUPS = SSM_WIDTH // SSM_GROUP
SSM_STATE = 64
DT_MIN = 0.001
DT_MAX = 0.1
RMS_EPS = 1e-6

_SIZES = (CONV_WIDTH, CONV_WIDTH, CONV_WIDTH, CONV_WIDTH,
          SSM_WIDTH, SSM_WIDTH,
          D_MODEL, D_MODEL)
N_IN = int(sum(_SIZES))
SPLITS = tuple(int(s) for s in np.cumsum(_SIZES)[:-1])


def rmsnorm(x, g):
    x32 = x.astype(jnp.float32)
    y = x32 * lax.rsqrt(jnp.mean(x32 * x32, axis=-1, keepdims=True) + RMS_EPS)
    return (y * g.astype(jnp.float32)).astype(x.dtype)

def causal_depthwise_conv(v, w):
    L = v.shape[1]
    vp = jnp.pad(v, ((0, 0), (CONV_K - 1, 0), (0, 0)))
    out = w[0] * vp[:, 0:L]
    for k in range(1, CONV_K):
        out = out + w[k] * vp[:, k:k + L]
    return out

def s5_scan(u, a_re, a_im, log_dt, b_re, b_im, c_re, c_im, d_skip):
    bsz, L, _ = u.shape
    f32 = jnp.float32
    ug = u.astype(f32).reshape(bsz, L, SSM_GROUPS, SSM_GROUP)
    lam = lax.complex(a_re.astype(f32), a_im.astype(f32))
    dt = jnp.exp(log_dt.astype(f32))[:, None]
    lam_bar = jnp.exp(lam * dt)
    b = lax.complex(b_re.astype(f32), b_im.astype(f32))
    b_bar = ((lam_bar - 1.0) / lam)[..., None] * b
    bu = jnp.einsum('gpc,blgc->blgp', b_bar, ug.astype(jnp.complex64))
    a = jnp.broadcast_to(lam_bar, bu.shape)

    def combine(e1, e2):
        a1, h1 = e1
        a2, h2 = e2
        return a1 * a2, a2 * h1 + h2

    _, h = lax.associative_scan(combine, (a, bu), axis=1)
    c = lax.complex(c_re.astype(f32), c_im.astype(f32))
    y = jnp.einsum('gcp,blgp->blgc', c, h).real + d_skip.astype(f32) * ug
    return y.reshape(bsz, L, SSM_WIDTH)

def hybrid_layer(x, norm_g, w_in, conv_w, w_out_a, a_re, a_im, log_dt, b_re, b_im,
                 c_re, c_im, d_skip, w_glu, b_glu, w_out_b, w_o):
    h = rmsnorm(x, norm_g)
    proj = jnp.einsum('bld,dn->bln', h, w_in)
    v, bg, cg, za, u, zb, ga, gb = jnp.split(proj, SPLITS, axis=-1)
    ya = bg * causal_depthwise_conv(cg * v, conv_w)
    ya = jnp.einsum('blc,cd->bld', ya * jax.nn.silu(za), w_out_a)
    yb = jax.nn.gelu(s5_scan(u, a_re, a_im, log_dt, b_re, b_im, c_re, c_im, d_skip))
    yb = yb * jax.nn.sigmoid(jnp.einsum('blc,ce->ble', yb, w_glu.astype(jnp.float32))
                             + b_glu.astype(jnp.float32))
    yb = yb.astype(x.dtype)
    yb = jnp.einsum('blc,cd->bld', yb * jax.nn.silu(zb), w_out_b)
    m = jax.nn.sigmoid(ga) * ya + jax.nn.sigmoid(gb) * yb
    return x + jnp.einsum('bld,de->ble', m, w_o)

def first_inputs(seed: int = 0) -> dict:
    key = jax.random.key(seed)
    ks = jax.random.split(key, 20)
    f32 = jnp.float32
    n = lambda k, shape, s: jax.random.normal(k, shape, f32) * s
    res_scale = 1.0 / math.sqrt(2.0 * DEPTH)
    G, P, c = SSM_GROUPS, SSM_STATE, SSM_GROUP
    a_im_base = math.pi * jnp.arange(P, dtype=f32)
    return {
        "x": n(ks[0], (BATCH, SEQ, D_MODEL), 1.0),
        "norm_g": 1.0 + n(ks[1], (DEPTH, D_MODEL), 0.02),
        "w_in": n(ks[2], (DEPTH, D_MODEL, N_IN), D_MODEL ** -0.5),
        "conv_w": n(ks[3], (DEPTH, CONV_K, CONV_WIDTH), CONV_K ** -0.5),
        "w_out_a": n(ks[4], (DEPTH, CONV_WIDTH, D_MODEL), CONV_WIDTH ** -0.5),
        "a_re": -0.5 + n(ks[5], (DEPTH, G, P), 0.01),
        "a_im": a_im_base + n(ks[6], (DEPTH, G, P), 0.01),
        "log_dt": jax.random.uniform(ks[7], (DEPTH, G), f32,
                                     math.log(DT_MIN), math.log(DT_MAX)),
        "b_re": n(ks[8], (DEPTH, G, P, c), (2.0 * c) ** -0.5),
        "b_im": n(ks[9], (DEPTH, G, P, c), (2.0 * c) ** -0.5),
        "c_re": n(ks[10], (DEPTH, G, c, P), (2.0 * P) ** -0.5),
        "c_im": n(ks[11], (DEPTH, G, c, P), (2.0 * P) ** -0.5),
        "d_skip": n(ks[12], (DEPTH, G, c), 1.0),
        "w_glu": n(ks[13], (DEPTH, SSM_WIDTH, SSM_WIDTH), SSM_WIDTH ** -0.5),
        "b_glu": n(ks[14], (DEPTH, SSM_WIDTH), 0.02),
        "w_out_b": n(ks[15], (DEPTH, SSM_WIDTH, D_MODEL), SSM_WIDTH ** -0.5),
        "w_o": n(ks[16], (DEPTH, D_MODEL, D_MODEL), D_MODEL ** -0.5 * res_scale),
        "final_g": 1.0 + n(ks[17], (D_MODEL,), 0.02),
    }

def first_block(x, norm_g, w_in, conv_w, w_out_a, a_re, a_im, log_dt, b_re, b_im,
              c_re, c_im, d_skip, w_glu, b_glu, w_out_b, w_o, final_g):
    for i in range(DEPTH):
        x = hybrid_layer(x, norm_g[i], w_in[i], conv_w[i], w_out_a[i], a_re[i], a_im[i],
                         log_dt[i], b_re[i], b_im[i], c_re[i], c_im[i], d_skip[i],
                         w_glu[i], b_glu[i], w_out_b[i], w_o[i])
    return rmsnorm(x, final_g)


HEAD_DIM = 64
ATTN_WIDTH = D_MODEL // 2
RWKV_WIDTH = D_MODEL - ATTN_WIDTH
N_ATTN_HEADS = ATTN_WIDTH // HEAD_DIM
N_RWKV_HEADS = RWKV_WIDTH // HEAD_DIM
DILATED_PATTERNS = ((128, 1), (512, 4), (2048, 16))
REL_BUCKETS = 32
REL_MAX_DIST = 2048
RWKV_DECAY_RANK = max(32, int(round(1.8 * RWKV_WIDTH ** 0.5 / 32)) * 32)
RWKV_A_RANK = max(32, int(round(1.8 * RWKV_WIDTH ** 0.5 / 32)) * 32)
RWKV_GATE_RANK = max(32, int(round(0.6 * RWKV_WIDTH ** 0.8 / 32)) * 32)
RWKV_COLS = 3 * RWKV_WIDTH + RWKV_DECAY_RANK + RWKV_A_RANK + RWKV_GATE_RANK
RWKV_SPLITS = (RWKV_WIDTH, 2 * RWKV_WIDTH, 3 * RWKV_WIDTH,
               3 * RWKV_WIDTH + RWKV_DECAY_RANK,
               3 * RWKV_WIDTH + RWKV_DECAY_RANK + RWKV_A_RANK)
IN_COLS = 3 * ATTN_WIDTH + RWKV_COLS
FFN_HIDDEN = -(-(8 * D_MODEL) // (3 * 256)) * 256
GN_EPS = 64e-5
DECAY_SCALE = math.exp(-0.5)
ATTN_SCALE = HEAD_DIM ** -0.5


def rms_norm(x, g):
    xf = x.astype(jnp.float32)
    y = xf * lax.rsqrt(jnp.mean(xf * xf, axis=-1, keepdims=True) + RMS_EPS)
    return (y * g.astype(jnp.float32)).astype(x.dtype)

def t5_bucket(dist):
    exact = REL_BUCKETS // 2
    d_f = jnp.maximum(dist, 1).astype(jnp.float32)
    large = exact + (jnp.log(d_f / exact) / math.log(REL_MAX_DIST / exact)
                     * (REL_BUCKETS - exact)).astype(jnp.int32)
    large = jnp.minimum(large, REL_BUCKETS - 1)
    return jnp.where(dist < exact, dist, large)

def dilated_branch(q, k, v, bias_table, window, dilation):
    b, s, h, dh = q.shape
    blk = window // dilation
    span = blk * dilation
    sp = -(-s // span) * span
    nblk = sp // span

    def blocks(t):
        t = jnp.pad(t, ((0, 0), (0, sp - s), (0, 0), (0, 0)))
        return t.reshape(b, nblk, blk, dilation, h, dh)

    def with_prev(t):
        prev = jnp.pad(t, ((0, 0), (1, 0), (0, 0), (0, 0), (0, 0), (0, 0)))[:, :-1]
        return jnp.concatenate([prev, t], axis=2)

    qb = blocks(q)
    kc = with_prev(blocks(k))
    vc = with_prev(blocks(v))
    qi = jnp.arange(blk)[:, None]
    ki = jnp.arange(2 * blk)[None, :]
    rel = qi + blk - ki
    band = (rel >= 0) & (rel <= blk)
    bias = bias_table[t5_bucket(jnp.clip(rel, 0, blk) * dilation)]
    bias = jnp.transpose(bias, (2, 0, 1)).astype(jnp.float32)
    not_first = jnp.arange(nblk)[:, None, None] > 0
    valid = band[None] & (not_first | (ki >= blk)[None])
    logits = jnp.einsum('bnqrhd,bnkrhd->bnrhqk', qb, kc) * ATTN_SCALE + bias
    logits = jnp.where(valid[None, :, None, None], logits, -jnp.inf)
    m = jnp.max(logits, axis=-1, keepdims=True)
    p = jnp.exp(logits - m)
    l = jnp.sum(p, axis=-1, keepdims=True)
    o = jnp.einsum('bnrhqk,bnkrhd->bnqrhd', p / l, vc)
    lse = (m + jnp.log(l))[..., 0]
    o = o.reshape(b, sp, h, dh)[:, :s]
    lse = jnp.transpose(lse, (0, 1, 4, 2, 3)).reshape(b, sp, h)[:, :s]
    return o, lse

def dilated_attention(q, k, v, bias_table):
    outs, lses = [], []
    for window, dilation in DILATED_PATTERNS:
        o, lse = dilated_branch(q, k, v, bias_table, window, dilation)
        outs.append(o)
        lses.append(lse)
    wts = jax.nn.softmax(jnp.stack(lses), axis=0)
    return jnp.sum(wts[..., None] * jnp.stack(outs), axis=0)

def rwkv7_step(state, inp):
    r, w, k, v, a, bb = inp
    sa = jnp.einsum('bhij,bhj->bhi', state, a)
    state = (state * w[:, :, None, :] + sa[..., None] * bb[:, :, None, :]
             + v[..., None] * k[:, :, None, :])
    y = jnp.einsum('bhij,bhj->bhi', state, r)
    return state, y

def rwkv7_time_mix(z, shift_mix, w0, w_up, a0, a_up, g_up, k_k, k_a, r_k, ln_w, ln_b):
    b, s, _ = z.shape
    prev = jnp.pad(z, ((0, 0), (1, 0), (0, 0)))[:, :-1]
    z = z + (prev - z) * shift_mix
    r, k, v, w_lo, a_lo, g_lo = jnp.split(z, list(RWKV_SPLITS), axis=-1)
    decay = jnp.exp(-DECAY_SCALE * jax.nn.sigmoid(w0 + jnp.tanh(w_lo) @ w_up))
    a = jax.nn.sigmoid(a0 + a_lo @ a_up)
    g = jax.nn.sigmoid(g_lo) @ g_up

    def heads(t):
        return t.reshape(b, s, N_RWKV_HEADS, HEAD_DIM)

    kk = heads(k * k_k)
    kk = kk / jnp.maximum(jnp.sqrt(jnp.sum(kk * kk, axis=-1, keepdims=True)), 1e-12)
    k = k * (1.0 + (a - 1.0) * k_a)
    rh, kh, vh, wh, ah = heads(r), heads(k), heads(v), heads(decay), heads(a)
    xs = tuple(jnp.moveaxis(t, 1, 0) for t in (rh, wh, kh, vh, -kk, kk * ah))
    state0 = jnp.zeros((b, N_RWKV_HEADS, HEAD_DIM, HEAD_DIM), jnp.float32)
    _, y = lax.scan(rwkv7_step, state0, xs)
    y = jnp.moveaxis(y, 0, 1)
    mu = jnp.mean(y, axis=-1, keepdims=True)
    var = jnp.mean(jnp.square(y - mu), axis=-1, keepdims=True)
    y = ((y - mu) * lax.rsqrt(var + GN_EPS)).reshape(b, s, RWKV_WIDTH) * ln_w + ln_b
    bonus = jnp.sum(rh * kh * r_k, axis=-1, keepdims=True) * vh
    return (y + bonus.reshape(b, s, RWKV_WIDTH)) * g

def second_inputs(seed: int = 0) -> dict:
    key = jax.random.key(seed)
    ks = jax.random.split(key, 20)
    L = DEPTH

    def nrm(k, shape, scale):
        return scale * jax.random.normal(k, shape, jnp.float32)

    return {
        'x': nrm(ks[0], (BATCH, SEQ, D_MODEL), 1.0),
        'norm1_g': 1.0 + nrm(ks[1], (L, D_MODEL), 0.05),
        'w_in': nrm(ks[2], (L, D_MODEL, IN_COLS), D_MODEL ** -0.5),
        'rwkv_shift_mix': jax.random.uniform(ks[3], (L, RWKV_COLS), jnp.float32),
        'rwkv_w0': jnp.linspace(-4.0, 2.0, RWKV_WIDTH, dtype=jnp.float32) + nrm(ks[4], (L, RWKV_WIDTH), 0.1),
        'rwkv_w_up': nrm(ks[5], (L, RWKV_DECAY_RANK, RWKV_WIDTH), 0.5 * RWKV_DECAY_RANK ** -0.5),
        'rwkv_a0': nrm(ks[6], (L, RWKV_WIDTH), 0.1),
        'rwkv_a_up': nrm(ks[7], (L, RWKV_A_RANK, RWKV_WIDTH), RWKV_A_RANK ** -0.5),
        'rwkv_g_up': nrm(ks[8], (L, RWKV_GATE_RANK, RWKV_WIDTH), RWKV_GATE_RANK ** -0.5),
        'rwkv_k_k': 0.85 + nrm(ks[9], (L, RWKV_WIDTH), 0.05),
        'rwkv_k_a': 1.0 + nrm(ks[10], (L, RWKV_WIDTH), 0.05),
        'rwkv_r_k': nrm(ks[11], (L, N_RWKV_HEADS, HEAD_DIM), 0.1),
        'rwkv_ln_w': 1.0 + nrm(ks[12], (L, RWKV_WIDTH), 0.05),
        'rwkv_ln_b': nrm(ks[13], (L, RWKV_WIDTH), 0.02),
        'rel_bias_table': nrm(ks[14], (REL_BUCKETS, N_ATTN_HEADS), 0.5),
        'w_out': nrm(ks[15], (L, D_MODEL, D_MODEL), D_MODEL ** -0.5),
        'norm2_g': 1.0 + nrm(ks[16], (L, D_MODEL), 0.05),
        'w_gate_up': nrm(ks[17], (L, D_MODEL, 2 * FFN_HIDDEN), D_MODEL ** -0.5),
        'w_down': nrm(ks[18], (L, FFN_HIDDEN, D_MODEL), FFN_HIDDEN ** -0.5),
        'final_g': 1.0 + nrm(ks[19], (D_MODEL,), 0.05),
    }

def second_block(x, norm1_g, w_in, rwkv_shift_mix, rwkv_w0, rwkv_w_up, rwkv_a0, rwkv_a_up,
              rwkv_g_up, rwkv_k_k, rwkv_k_a, rwkv_r_k, rwkv_ln_w, rwkv_ln_b, rel_bias_table,
              w_out, norm2_g, w_gate_up, w_down, final_g):
    b, s, _ = x.shape
    h = x
    for l in range(DEPTH):
        u = rms_norm(h, norm1_g[l])
        proj = (u @ w_in[l]).astype(jnp.float32)
        q, k, v, z = jnp.split(proj, [ATTN_WIDTH, 2 * ATTN_WIDTH, 3 * ATTN_WIDTH], axis=-1)
        hd = (b, s, N_ATTN_HEADS, HEAD_DIM)
        attn = dilated_attention(q.reshape(hd), k.reshape(hd), v.reshape(hd),
                                 rel_bias_table.astype(jnp.float32))
        rw = rwkv7_time_mix(z, rwkv_shift_mix[l], rwkv_w0[l], rwkv_w_up[l], rwkv_a0[l],
                            rwkv_a_up[l], rwkv_g_up[l], rwkv_k_k[l], rwkv_k_a[l],
                            rwkv_r_k[l], rwkv_ln_w[l], rwkv_ln_b[l])
        mixed = jnp.concatenate([attn.reshape(b, s, ATTN_WIDTH), rw], axis=-1).astype(h.dtype)
        h = h + mixed @ w_out[l]
        u = rms_norm(h, norm2_g[l])
        gate, up = jnp.split(u @ w_gate_up[l], 2, axis=-1)
        h = h + (jax.nn.silu(gate) * up) @ w_down[l]
    return rms_norm(h, final_g)


def setup_inputs(seed=0):
    out = dict(first_inputs(seed))
    for name, value in second_inputs(seed + 1).items():
        if name != "x":
            out[name + "_2"] = value
    return out


def reference(
    x, norm_g, w_in, conv_w, w_out_a, a_re, a_im, log_dt, b_re, b_im, c_re, c_im, d_skip, w_glu,
    b_glu, w_out_b, w_o, final_g, norm1_g_2, w_in_2, rwkv_shift_mix_2, rwkv_w0_2, rwkv_w_up_2,
    rwkv_a0_2, rwkv_a_up_2, rwkv_g_up_2, rwkv_k_k_2, rwkv_k_a_2, rwkv_r_k_2, rwkv_ln_w_2,
    rwkv_ln_b_2, rel_bias_table_2, w_out_2, norm2_g_2, w_gate_up_2, w_down_2, final_g_2,
):
    x = first_block(
        x, norm_g, w_in, conv_w, w_out_a, a_re, a_im, log_dt, b_re, b_im, c_re, c_im, d_skip,
        w_glu, b_glu, w_out_b, w_o, final_g,
    )
    return second_block(
        x, norm1_g_2, w_in_2, rwkv_shift_mix_2, rwkv_w0_2, rwkv_w_up_2, rwkv_a0_2, rwkv_a_up_2,
        rwkv_g_up_2, rwkv_k_k_2, rwkv_k_a_2, rwkv_r_k_2, rwkv_ln_w_2, rwkv_ln_b_2,
        rel_bias_table_2, w_out_2, norm2_g_2, w_gate_up_2, w_down_2, final_g_2,
    )


_drawn_inputs = setup_inputs


def setup_inputs(seed=0):
    import zlib

    import numpy as np

    out = dict(_drawn_inputs(seed))
    spreads = {}
    factors = {'norm_g': 4.303,
     'a_re': 64.0,
     'a_im': 64.0,
     'log_dt': 64.0,
     'b_re': 64.0,
     'b_im': 64.0,
     'c_re': 64.0,
     'c_im': 64.0,
     'b_glu': 64.0,
     'rwkv_w_up_2': 2.884,
     'rwkv_a0_2': 3.196,
     'rwkv_k_k_2': 28.604,
     'rwkv_ln_w_2': 2.88,
     'rwkv_ln_b_2': 7.432}
    for name, (base, spread) in spreads.items():
        noise = np.random.default_rng([zlib.crc32(name.encode()), seed]).standard_normal(out[name].shape)
        drawn = base * np.exp(spread * noise) if base else spread * noise
        out[name] = __import__('jax').numpy.asarray(drawn.astype(out[name].dtype))
    for name, factor in factors.items():
        out[name] = (out[name] * factor).astype(out[name].dtype)
    return out
```

```python
import math
from contextlib import ExitStack

import numpy as np

import concourse.bass as bass
from concourse import mybir

F32 = mybir.dt.float32
F32R = mybir.dt.float32r
ALU = mybir.AluOpType
ACT = mybir.ActivationFunctionType
AX = mybir.AxisListType

P = 128
L = 256
D = 2048
KB = D // P
SSM = 1024
SB = SSM // P
STATE_TILES = 64 * 64 // P
TPB = STATE_TILES // SB
EPS = 1e-6
FFN = 5632
FB = FFN // P
HEADS = 16
PAIRS = HEADS // 2
CH = 64
NCH = L // CH
INV = 16
DECAY_SCALE = math.exp(-0.5)
GN_EPS = 64e-5
ATTN_SCALE = 64 ** -0.5
ROUND = 1.5 * 2.0 ** 23
TWO_PI = 2 * math.pi
SIN_SCALE = 6.283185
PI_A = 6.28125
PI_B = 0.0019350051879882812
PI_C = TWO_PI - PI_A - PI_B

U = 1024
RING = 4

STREAM = [("u", 8, 2), ("zb", 8, 2), ("conv", 64, 2), ("gb", 16, 2), ("gaa", 32, 2), ("glu", 8, 1),
          ("outb", 16, 1), ("wo", 16, 2), ("lora", 3, 2), ("rkv", 24, 2), ("qkv", 24, 2),
          ("wout", 16, 2), ("ffn", 88, 2), ("down", 16, 6)]
UNIT0, BLOCK0 = {}, {}
_u = _b = 0
for _n, _blk, _per in STREAM:
    UNIT0[_n], BLOCK0[_n] = _u, _b
    _u += _blk * _per
    _b += _blk
UNITS_MAIN = UNIT0["down"]
UNITS = _u

PCOLS = {}
_c = 0
for _n, _w in [("norm_g", 16), ("conv0", 16), ("conv1", 16), ("conv2", 16), ("final_g", 16),
               ("norm1", 16), ("norm2", 16), ("final2", 16), ("b_glu", 8), ("d_skip", 8),
               ("mix_rkv", 24), ("mix_lo", 3), ("w0", 8), ("a0", 8), ("k_k", 8), ("k_a", 8),
               ("r_k", 8), ("ln_w", 8), ("ln_b", 8), ("a_re", 32), ("a_im", 32), ("log_dt", 32)]:
    PCOLS[_n] = (_c, _w)
    _c += _w
NPAR = _c

CCOLS = {}
_c = 0
for _n, _w in [("iota", 256), ("inchunk", 256), ("ones", 128), ("hones", 128), ("ident", 128), ("maskg", 128),
               ("mdiag", 64), ("mdiagt", 64), ("moff", 64), ("eye64", 64), ("lncount", 384), ("halfpi", 1), ("eps", 1),
               ("gneps", 1), ("round", 1)]:
    CCOLS[_n] = (_c, _w)
    _c += _w
NCONST = _c


class At:

    def __init__(self, c, m=0, i=None):
        self.c, self.m, self.i = c, m, i

    def __add__(self, k):
        return At(self.c + k, self.m, self.i)

    def v(self, k=0):
        return self.c + k if self.i is None else self.i * self.m + (self.c + k)

    def turns(self, ring, k=0):
        assert self.m % ring == 0
        n = self.c // ring + k
        return n if self.i is None else self.i * (self.m // ring) + n


class Links:

    def __init__(self, eng, sem):
        self.eng, self.sem, self.base, self.k, self.per, self.i = eng, sem, 0, 0, 0, None

    def __call__(self, ins):
        self.k += 1
        ins.then_inc(self.sem, 1)
        self.wait()

    def wait(self):
        n = self.base + self.k
        self.eng.wait_ge(self.sem, n if self.i is None else self.i * self.per + n)

    def loop(self, i, per, start=0):
        self.turned = self.base + self.k
        self.base, self.k, self.i, self.per = self.turned - per * start, 0, i, per

    def done(self, turns):
        assert self.k == self.per, f"the loop's body has {self.k} links"
        self.base, self.k, self.i = self.turned + self.per * turns, 0, None


def hybrid_kernel(nc, wmain, wdown, bst_dram, cst_dram, par_dram, const_dram, x_dram, lora_dram,
                  gup_dram, bias_dram, out_dram):
    ctx = ExitStack()
    with ctx:
        base = -(-nc.sbuf_base // 64) * 64
        ctx.enter_context(nc.sbuf_tensor("arena", [P, nc.sbuf_usable_end // 4 - base // 4 - 32], F32))
        K = 1024

        def at(name, offset, shape, dtype=F32):
            return nc.alloc_sbuf_tensor_at(name, [P, *shape], dtype, offset=base + offset)

        def sem(name):
            return ctx.enter_context(nc.semaphore(name))

        raw = at("w_raw", 0, [RING, U])
        whi = at("w_hi", 16 * K, [RING, U], F32R)
        wlo = at("w_lo", 32 * K, [RING, U], F32R)
        x = at("x_res", 48 * K, [KB, L])
        par = at("par", 64 * K, [NPAR])
        const = at("const", 66 * K, [NCONST])
        small = 73 * K
        rstd = at("rstd", small, [L])
        rstd2 = at("rstd2", small + 1 * K, [L])
        acc = at("acc", small + 2 * K, [2, L])
        tz = at("tz", small + 4 * K, [2, L])
        gt = at("gt", small + 6 * K, [2, L])
        f = at("f_val", small + 8 * K, [2, L])
        tmp = at("tmp", small + 10 * K, [2, L])
        sq = at("sq", small + 12 * K, [2, L])
        gg = at("gg", small + 14 * K, [KB])
        phi = at("phi", small + 14 * K + 64, [STATE_TILES])
        rho = at("rho", small + 14 * K + 192, [STATE_TILES])
        work = small + 14 * K + 320

        def wk(name, kb, shape, dtype=F32):
            assert base + work + kb * K + 4 * int(np.prod(shape)) <= nc.sbuf_usable_end, name
            return at(name, work + int(kb * K), shape, dtype)

        xh, xl = wk("xh", 0, [KB, L], F32R), wk("xl", 16, [KB, L], F32R)
        yah, yal = wk("yah", 32, [KB, L], F32R), wk("yal", 48, [KB, L], F32R)
        szb = wk("silu_zb", 64, [SB, L])
        ug = wk("u_then_gelu", 72, [SB, L])
        sgb = wk("sig_gb", 80, [KB, L])
        mix = wk("mixed", 96, [KB, L])
        sqx = wk("sqx", 96, [KB, L])
        convv = sq[:, 0, :]
        convc = wk("conv_cgv", 119, [L + 2])
        cosi = wk("cos_t", 80, [TPB, L])
        sini = wk("sin_t", 84, [TPB, L])
        turn = wk("turns", 88, [TPB, L])
        frac = wk("turn_frac", 92, [TPB, L])
        bstage = wk("b_stage", 96, [TPB, 2, P])
        m1, m2 = wk("m1", 100, [2, L]), wk("m2", 102, [2, L])
        gs = [wk("g_scan", 104, [2, L]), acc]
        o1, o2 = turn[:, 0:2, :], turn[:, 2:4, :]
        hs = wk("h_state", 106, [2, 2, L])
        cstage = wk("c_stage", 110, [TPB, 2, 32])
        cp = wk("c_prime", 111, [SB, TPB, 2, 32])
        craw = wk("c_raw", 32, [2, STATE_TILES, 32])
        cw = wk("c_work", 40, [2, STATE_TILES, 32])
        sv = {n: wk("s_" + n, 48 + i / 8, [STATE_TILES]) for i, n in enumerate(
            ["dt", "theta", "kk", "t0", "t1", "t2", "abs", "sin", "cos", "er", "den", "lr", "li",
             "kre", "kim", "den2"])}
        ybh, ybl = wk("ybh", 32, [SB, L], F32R), wk("ybl", 40, [SB, L], F32R)
        yoh, yol = wk("yoh", 48, [SB, L], F32R), wk("yol", 56, [SB, L], F32R)
        mh, ml = wk("mh", 0, [KB, L], F32R), wk("ml", 16, [KB, L], F32R)
        nh, nl = wk("nh", 32, [KB, L], F32R), wk("nl", 48, [KB, L], F32R)

        lora = wk("lora_up", 88, [1024])
        zs = wk("z_shift", 92, [L + 2])
        lo = wk("lora_lo", 94, [L])
        sgl = sq
        zr = wk("rkv", 64, [24, L])
        qkv = wk("qkv", 88, [24, L])
        aa = wk("a_gate", 0, [8, L])
        sw = wk("sig_w", 8, [8, L])
        abr = wk("ar_hat", 16, [2, 8, L])
        ba, br = abr[:, 0, :, :], abr[:, 1, :, :]
        bb = wk("b_hat", 112, [8, L])
        rr, kr, vr = zr[:, 0:8, :], zr[:, 8:16, :], zr[:, 16:24, :]
        pc = at("chunk_decay", small + 8 * K + 256, [8, NCH])
        gup = wk("g_up", 88, [2, 1024])
        bkc = wk("bk_chunk", 4, [8, 2, CH])
        gm = wk("gm", 88, [2, 8, P])
        st = wk("stack", 100, [8, 2, CH])
        bkt = wk("bk_tokens", 104, [8, P])
        mat = {n: wk("m_" + n, o, [8, CH]) for n, o in [
            ("n", 108), ("f", 110), ("nt", 40), ("w", 42), ("n2", 44), ("n2t", 46), ("n4", 56),
            ("n4t", 58), ("md", 60)]}
        xv = at("x_chunk", small + 6 * K, [8, CH])
        state = wk("state", 62, [8, CH])
        gnt = wk("gn_tmp", 0, [8, L])
        qs, ks = at("q_st", small + 4 * K, [2, L]), at("k_st", small + 6 * K, [2, L])
        vs, vt = wk("v_st", 46, [2, L]), wk("v_tok", 62, [2, 2, P])
        pt = wk("p_t", 0, [2, 2, 384])
        biasb = wk("bias", 40, [2, 2, 384])
        eb = wk("e_val", 56, [2, 2, 384])
        mxs = at("row_max", small + 8 * K, [2, 2, 2, 4])
        x3h, x3l = wk("x3h", 0, [KB, L], F32R), wk("x3l", 16, [KB, L], F32R)
        mxh, mxl = wk("mxh", 32, [KB, L], F32R), wk("mxl", 48, [KB, L], F32R)
        ah, al = wk("act_h", 32, [FB, L], F32R), wk("act_l", 76, [FB, L], F32R)

        main = ctx.enter_context(nc.psum_tensor("ps_main", [P, 4, 512], F32))
        aux = ctx.enter_context(nc.psum_tensor("ps_aux", [P, 4, 512], F32))

        def par_c(name, j):
            c, w = PCOLS[name]
            if isinstance(j, int):
                return par[:, c + j:c + j + 1]
            return par[:, bass.ds(j + c, 1)]

        def cst(name):
            c, w = CCOLS[name]
            return const[:, c:c + w]

        w_loaded = [sem(f"w_loaded{s}") for s in range(RING)]
        hi_ready, lo_ready, unit_used = sem("hi_ready"), sem("lo_ready"), sem("unit_used")
        bank_free = [sem(f"bank_free{b}") for b in range(4)]
        x_loaded, par_loaded, const_loaded, c_loaded = sem("x_loaded"), sem("par_loaded"), sem("const_loaded"), sem("c_loaded")
        dve_link, act_link, pool_link = sem("dve_link"), sem("act_link"), sem("pool_link")
        xsq_ready, acc_ready, ssq_ready, root_ready = sem("xsq_ready"), sem("acc_ready"), sem("ssq_ready"), sem("root_ready")
        in_ready = sem("in_ready")
        rstd_ready = sem("rstd_ready")
        gate_out = sem("gate_out")
        s_act, s_dve = sem("scan_par_act"), sem("scan_par_dve")
        scan_const = sem("scan_const")
        b_loaded, c_staged, frac_ready, trig_ready = sem("b_loaded"), sem("c_staged"), sem("frac_ready"), sem("trig_ready")
        bu_ready, bu_used, h_ready, h_used, y_used = sem("bu_ready"), sem("bu_used"), sem("h_ready"), sem("h_used"), sem("y_used")
        gs_ready = sem("gs_ready")
        ya_ready, gelu_ready, yb_ready, glu_out, yo_ready, m_ready = (
            sem("ya_ready"), sem("gelu_ready"), sem("yb_ready"), sem("glu_out"), sem("yo_ready"), sem("m_ready"))
        res_ready, sq_ready = sem("res_ready"), sem("sq_ready")
        out_stored = sem("out_stored")
        norm_sum, norm_root, ms_ready = sem("norm_sum"), sem("norm_root"), sem("ms_ready")
        lora_loaded, gup_loaded, res_scaled = sem("lora_loaded"), sem("gup_loaded"), sem("res_scaled")
        lo_shifted, lo_act, up_mm, up_act = sem("lo_shifted"), sem("lo_act"), sem("up_mm"), sem("up_act")
        prep_dve, prep_act, head_mm = sem("prep_dve"), sem("prep_act"), sem("head_mm")
        staged, core_mm, core_act, core_dve = sem("staged"), sem("core_mm"), sem("core_act"), sem("core_dve")
        core_pre = sem("core_pre")
        fin_mm, fin_act, fin_dve, gu_mm = sem("fin_mm"), sem("fin_act"), sem("fin_dve"), sem("gu_mm")
        bias_loaded = [sem("bias_loaded0"), sem("bias_loaded1")]
        bias_ready, att_staged, sc_mm, vt_mm, vt_sb, e_ready, max_ready, p_ready, pn_ready, pt_mm, pt_sb, o_mm, att_ready = (
            sem(n) for n in ("bias_ready", "att_staged", "sc_mm", "vt_mm", "vt_sb", "e_ready", "max_ready", "p_ready",
                             "pn_ready", "pt_mm", "pt_sb", "o_mm", "att_ready"))
        rwkv_ready, act_ready = sem("rwkv_ready"), sem("act_ready")
        out_ready = sem("out_ready")

        def down_width(u):
            return U if u < 5 else U // 2

        def hrow(h):
            return slice(64 * h, 64 * h + 64)

        PREP_DVE = 12
        GO = 1
        SCAN_BU, SCAN_IN, SCAN_Y = (0, 0, 3, 3), (0, 1, 3, 4), (3, 4, 6, 7)
        MM = {n: k + 1 for k, n in enumerate(
            ["vt", "g", "n", "bkt", "n2", "n2t", "w2", "n4", "n4t", "w4", "n8", "w8", "qt", "q", "md", "q2", "g1",
             "mt", "x", "sa", "y", "s"])}
        DV = {n: k + 1 for k, n in enumerate(
            ["gm", "nf", "w1", "n2t", "w2", "n4t", "w4", "w8", "qt", "t1", "g1", "sa", "y", "s"])}
        AC = {n: k + 1 for k, n in enumerate(["vt", "bkt", "n2", "n4", "n8", "q", "md", "q2", "mt", "x"])}

        block = ctx.enter_context(nc.Block())

        @block.sync
        def _(sp):
            for s in range(RING):
                sp.dma_start(raw[:, s, :], wmain[s]).then_inc(w_loaded[s], 16)
            with sp.Fori(1, UNITS_MAIN // RING) as i:
                for s in range(RING):
                    sp.wait_ge(lo_ready, i * RING + (s - RING + 1))
                    sp.dma_start(raw[:, s, :], wmain[bass.ds(i * RING + s, 1)].rearrange("a p n -> p (a n)"))\
                      .then_inc(w_loaded[s], 16)
            for n in range(UNITS_MAIN // RING * RING, UNITS_MAIN):
                sp.wait_ge(lo_ready, n - RING + 1)
                sp.dma_start(raw[:, n % RING, :], wmain[n]).then_inc(w_loaded[n % RING], 16)
            with sp.Fori(0, KB // 4) as i:
                for b in range(4):
                    for u in range(6):
                        n = At(UNITS_MAIN + 6 * b + u, 24, i)
                        w = down_width(u)
                        sp.wait_ge(lo_ready, n.v(1 - RING))
                        sp.dma_start(raw[:, n.c % RING, 0:w],
                                     wdown[bass.ds(i * 4 + b, 1), :, u * U:u * U + w].rearrange("a p n -> p (a n)"))\
                          .then_inc(w_loaded[n.c % RING], 16)
            for c in range(4):
                sp.wait_ge(out_ready, c + 1)
                sp.dma_start(out_dram[:, 4 * c:4 * c + 4, :], x[:, 4 * c:4 * c + 4, :]).then_inc(out_stored, 16)
            sp.wait_ge(out_stored, 64)

        @block.gpsimd
        def _(pool):
            link = Links(pool, pool_link)
            pool.sem_inc(h_ready, GO)
            pool.wait_ge(const_loaded, 16)
            pool.wait_ge(scan_const, 3)

            def scan_angles(i):
                c, _ = CCOLS["iota"]
                ph = phi[:, bass.ds(i * TPB, TPB)] if not isinstance(i, int) else phi[:, i * TPB:(i + 1) * TPB]
                link(nc.gpsimd.tensor_tensor(turn[:, :, :], const[:, c:c + L].unsqueeze(1).to_broadcast([P, TPB, L]),
                                             ph.unsqueeze(2).to_broadcast([P, TPB, L]), ALU.mult))
                rnd = cst("round").unsqueeze(1).to_broadcast([P, TPB, L])
                link(nc.gpsimd.tensor_tensor(frac[:, :, :], turn[:, :, :], rnd, ALU.add))
                link(nc.gpsimd.tensor_tensor(frac[:, :, :], frac[:, :, :], rnd, ALU.subtract))
                nc.gpsimd.tensor_tensor(frac[:, :, :], turn[:, :, :], frac[:, :, :], ALU.subtract).then_inc(frac_ready, 1)

            def scan_b(i):
                src = bst_dram[0] if isinstance(i, int) else bst_dram[bass.ds(i, 1)].rearrange("a p n -> p (a n)")
                pool.dma_start(bstage[:, :, :, :], src).then_inc(b_loaded, 16)

            def scan_c(i):
                src = cp[:, 0, :, :, :].rearrange("p a b c -> p (a b c)") if isinstance(i, int) else (
                    cp[:, bass.ds(i, 1), :, :, :].rearrange("p z a b c -> p (z a b c)"))
                nc.gpsimd.tensor_copy(cstage[:, :, :, :].rearrange("p a b c -> p (a b c)"), src).then_inc(c_staged, 1)

            def scan_out(i, t):
                cb = cosi[:, t, :].unsqueeze(1).to_broadcast([P, 2, L])
                sb_ = sini[:, t, :].unsqueeze(1).to_broadcast([P, 2, L])
                pool.wait_ge(gs_ready, i * TPB + (t + 1))
                pool.wait_ge(h_ready, i * TPB + t + GO)
                nc.gpsimd.tensor_tensor(o1, gs[t % 2][:, :, :], cb, ALU.mult)
                link(nc.gpsimd.tensor_tensor(o2, gs[t % 2][:, :, :], sb_, ALU.mult))
                pool.wait_ge(h_used, (i * TPB if t < 2 else i * TPB + (t - 1)) + GO)
                nc.gpsimd.tensor_tensor(hs[:, t % 2, 0, :], o1[:, 0, :], o2[:, 1, :], ALU.subtract)
                nc.gpsimd.tensor_tensor(hs[:, t % 2, 1, :], o1[:, 1, :], o2[:, 0, :], ALU.add).then_inc(h_ready, 1)

            def scan_block(i, last=False):
                scan_out(i, 0)
                scan_out(i, 1)
                if not last:
                    pool.wait_ge(h_ready, i * TPB + 2 + GO)
                    pool.wait_ge(trig_ready, i + 1)
                    scan_angles(i + 1)
                    pool.wait_ge(frac_ready, i + 2)
                scan_out(i, 2)
                scan_out(i, 3)
                if not last:
                    pool.wait_ge(bu_ready, i * TPB + TPB)
                    scan_b(i + 1)
                    pool.wait_ge(h_used, i * TPB + TPB + GO)
                    scan_c(i + 1)

            scan_b(0)
            scan_angles(0)
            pool.wait_ge(frac_ready, 1)
            scan_c(0)
            with pool.Fori(0, SB - 1) as i:
                link.loop(i, 7)
                scan_block(i)
            link.done(SB - 1)
            scan_block(SB - 1, True)

            pool.wait_ge(m_ready, KB)
            pool.dma_start(lora[:, :], lora_dram).then_inc(lora_loaded, 16)
            pool.wait_ge(rstd_ready, 2)
            pool.wait_ge(sq_ready, KB)
            pool.wait_ge(in_ready, 2 * KB)
            c, _ = PCOLS["final_g"]
            link(nc.gpsimd.tensor_tensor(x[:, :, :], x[:, :, :], rstd2[:, :].unsqueeze(1).to_broadcast([P, KB, L]), ALU.mult))
            nc.gpsimd.tensor_tensor(x[:, :, :], x[:, :, :], par[:, c:c + KB].unsqueeze(2).to_broadcast([P, KB, L]),
                                    ALU.mult).then_inc(res_scaled, 1)

            pool.wait_ge(prep_dve, PREP_DVE)
            pool.wait_ge(bank_free[(BLOCK0["wout"] - 1) % 4], (BLOCK0["wout"] - 1) // 4 + 1)
            pool.wait_ge(unit_used, UNIT0["wout"])
            with pool.Fori(0, PAIRS // 2) as i:
                for s in range(2):
                    j = i * 2 + s
                    pool.wait_ge(e_ready, i * 4 + GO)
                    pool.wait_ge(vt_mm, i * 2 + GO)
                    pool.dma_start(biasb[:, s, :, :].rearrange("p h n -> p (h n)"),
                                   bias_dram[bass.ds(j, 1)].rearrange("a p n -> p (a n)")).then_inc(bias_loaded[s], 16)
                    for k, t in enumerate((qs, ks, vs)):
                        ins = nc.gpsimd.tensor_copy(t[:, s, :], qkv[:, bass.ds(i * 6 + (3 * s + k), 1), :]
                                                    .rearrange("p a n -> p (a n)"))
                    ins.then_inc(att_staged, 1)
                for s in range(2):
                    pool.wait_ge(bias_loaded[s], i * 16 + 16)
                    nc.gpsimd.tensor_tensor(biasb[:, s, :, :], biasb[:, s, :, :],
                                            cst("lncount").unsqueeze(1).to_broadcast([P, 2, 384]), ALU.add)\
                        .then_inc(bias_ready, 1)
            pool.wait_ge(core_mm, NCH * len(MM) + GO)
            pool.dma_start(gup[:, :, :].rearrange("p a n -> p (a n)"), gup_dram.rearrange("p a n -> p (a n)"))\
                .then_inc(gup_loaded, 16)
            pool.wait_ge(gup_loaded, 16)

        @block.scalar
        def _(act):
            def split_hi(n, width=U):
                s = n.c % RING
                act.wait_ge(w_loaded[s], n.turns(RING, 1) * 16)
                if n.i is not None or n.c >= RING:
                    act.wait_ge(unit_used, n.v(1 - RING))
                nc.scalar.activation(whi[:, s, 0:width], raw[:, s, 0:width], ACT.Copy).then_inc(hi_ready, 1)

            def gate(func, out, k, g, bias=0.0):
                act.wait_ge(bank_free[g.c % 4], g.turns(4, 1))
                nc.scalar.activation(out, tz[:, k.c % 2, :], func, bias=bias).then_inc(gate_out, 1)

            act.sem_inc(pt_sb, GO)
            act.dma_start(x[:, :, :], x_dram).then_inc(x_loaded, 16)
            act.dma_start(par[:, :], par_dram).then_inc(par_loaded, 16)
            act.dma_start(const[:, :], const_dram).then_inc(const_loaded, 16)
            act.dma_start(craw[:, :, :, :], cst_dram).then_inc(c_loaded, 16)
            for s in range(3):
                split_hi(At(s))
            act.wait_ge(x_loaded, 16)
            nc.scalar.activation(sqx[:, :, :], x[:, :, :], ACT.Square).then_inc(xsq_ready, 1)
            act.wait_ge(const_loaded, 16)
            act.wait_ge(ssq_ready, 1)
            nc.scalar.activation(tmp[:, 0, :], aux[:, 3, 0:L], ACT.Sqrt, bias=cst("eps"), scale=1.0 / D)\
                .then_inc(root_ready, 1)

            act.wait_ge(par_loaded, 16)
            c, w = PCOLS["log_dt"]
            nc.scalar.activation(sv["dt"][:, :], par[:, c:c + w], ACT.Exp).then_inc(s_act, 1)

            n0 = UNIT0["u"]
            for b in range(8):
                split_hi(At(n0 + 2 * b + 3))
                split_hi(At(n0 + 2 * b + 4))
                if b == 0:
                    act.wait_ge(s_dve, 1)
                    nc.scalar.activation(rho[:, :], sv["er"][:, :], ACT.Exp).then_inc(s_act, 1)
                if b == 1:
                    act.wait_ge(s_dve, 2)
                    nc.scalar.activation(sv["sin"][:, :], phi[:, :], ACT.Sin, scale=SIN_SCALE).then_inc(s_act, 1)
                    nc.scalar.activation(sv["abs"][:, :], phi[:, :], ACT.Abs).then_inc(act_link, 1)
                    act.wait_ge(act_link, 1)
                    nc.scalar.activation(sv["cos"][:, :], sv["abs"][:, :], ACT.Sin, scale=-SIN_SCALE,
                                         bias=cst("halfpi")).then_inc(s_act, 1)
            links = Links(act, act_link)
            links.base = 1
            n0 = UNIT0["zb"]
            for b in range(8):
                split_hi(At(n0 + 2 * b + 3))
                split_hi(At(n0 + 2 * b + 4))
                gate(ACT.Silu, szb[:, b, :], At(b), At(BLOCK0["zb"] + b))

            def trig(i):
                act.wait_ge(frac_ready, i + 1)
                act.wait_ge(h_ready, i * TPB + GO)
                nc.scalar.activation(sini[:, :, :], frac[:, :, :], ACT.Sin, scale=SIN_SCALE)
                links(nc.scalar.activation(cosi[:, :, :], frac[:, :, :], ACT.Abs))
                nc.scalar.activation(cosi[:, :, :], cosi[:, :, :], ACT.Sin, scale=-SIN_SCALE,
                                     bias=cst("halfpi")).then_inc(trig_ready, 1)

            n0 = UNIT0["conv"]

            def conv(i, last=False):
                for b in range(8):
                    split_hi(At(n0 + 2 * b + 3, 16, i))
                    split_hi(At(n0 + 2 * b + 4, 16, i))
                    if b % 4 == 0:
                        gate(ACT.Silu, gt[:, (b // 4) % 2, :], At(8 + b // 4, 2, i), At(BLOCK0["conv"] + b, 8, i))
                    if b == 6 and not last:
                        trig(i + 1)

            trig(0)
            with act.Fori(0, SB - 1) as i:
                links.loop(i, 1)
                conv(i)
            links.done(SB - 1)
            conv(SB - 1, True)
            act.wait_ge(y_used, SB + GO)
            nc.scalar.activation(ug[:, :, :], ug[:, :, :], ACT.Gelu_apprx_tanh).then_inc(gelu_ready, 1)

            n0 = UNIT0["gb"]
            with act.Fori(0, 4) as i:
                for b in range(4):
                    split_hi(At(n0 + 2 * b + 3, 8, i))
                    split_hi(At(n0 + 2 * b + 4, 8, i))
                    gate(ACT.Sigmoid, sgb[:, bass.ds(i * 4 + b, 1), :].rearrange("p a n -> p (a n)"), At(24 + b, 4, i),
                         At(BLOCK0["gb"] + b, 4, i))
            n0 = UNIT0["gaa"]
            with act.Fori(0, 8) as i:
                for b in range(4):
                    split_hi(At(n0 + 2 * b + 3, 8, i))
                    split_hi(At(n0 + 2 * b + 4, 8, i))
                    if b % 2 == 0:
                        gate(ACT.Sigmoid, gt[:, b // 2, :], At(40 + b // 2, 2, i), At(BLOCK0["gaa"] + b, 4, i))
            n0, g0 = UNIT0["glu"], BLOCK0["glu"]
            for b in range(8):
                split_hi(At(n0 + b + 3))
                act.wait_ge(unit_used, n0 + b + 1)
                if b >= 2:
                    act.wait_ge(yo_ready, b - 1)
                nc.scalar.activation(gt[:, b % 2, :], main[:, (g0 + b) % 4, 0:L], ACT.Sigmoid,
                                     bias=par_c("b_glu", b)).then_inc(glu_out, 1)
            n0 = UNIT0["outb"]
            with act.Fori(0, 4) as i:
                for b in range(4):
                    split_hi(At(n0 + b + 3, 4, i))
            n0 = UNIT0["wo"]
            with act.Fori(0, 4) as i:
                for b in range(4):
                    split_hi(At(n0 + 2 * b + 3, 8, i))
                    split_hi(At(n0 + 2 * b + 4, 8, i))
                    j = i * 4 + b
                    xj = x[:, bass.ds(j, 1), :].rearrange("p a n -> p (a n)")
                    act.wait_ge(res_ready, i * 4 + b + 1)
                    nc.scalar.activation(sq[:, 0, :], xj, ACT.Square)
                    nc.scalar.activation(sq[:, 1, :], xj, ACT.Square, scale=par_c("final_g", j)).then_inc(sq_ready, 1)

            def root(src, dst, count, scale, eps="eps"):
                nc.scalar.activation(dst, src, ACT.Sqrt, bias=cst(eps), scale=scale).then_inc(norm_root, 1)

            n0 = UNIT0["lora"]
            for b in range(3):
                split_hi(At(n0 + 2 * b + 3))
                split_hi(At(n0 + 2 * b + 4))
                if b == 0:
                    act.wait_ge(norm_sum, 1)
                    root(aux[:, 3, 0:L], tmp[:, 0, :], 1, 1.0 / D)
                    act.wait_ge(ms_ready, 1)
                    root(tmp[:, 1, :], tmp[:, 0, :], 2, 1.0 / D)
                act.wait_ge(lo_shifted, b + 1)
                if b == 0:
                    nc.scalar.activation(lo[0:64, :], lo[0:64, :], ACT.Tanh).then_inc(lo_act, 1)
                else:
                    nc.scalar.activation(sgl[:, b - 1, :], f[:, b - 1, :], ACT.Sigmoid).then_inc(lo_act, 1)
            for j in range(8):
                act.wait_ge(up_mm, j + 1)
                nc.scalar.activation(sw[:, j, :], aux[:, j % 2, 0:L], ACT.Sigmoid, bias=par_c("w0", j))
                nc.scalar.activation(aa[:, j, :], aux[:, 2 + j % 2, 0:L], ACT.Sigmoid, bias=par_c("a0", j))\
                    .then_inc(up_act, 1)
            n0 = UNIT0["rkv"]
            with act.Fori(0, 6) as i:
                for b in range(4):
                    split_hi(At(n0 + 2 * b + 3, 8, i))
                    split_hi(At(n0 + 2 * b + 4, 8, i))

            def aux_all(lo_, hi_):
                return aux[:, lo_:hi_, :].rearrange("p b n -> p (b n)").rearrange("p (j n) -> p j n", n=L)

            n0 = UNIT0["qkv"]
            for b in range(24):
                split_hi(At(n0 + 2 * b + 3))
                split_hi(At(n0 + 2 * b + 4))
                if b == 1:
                    act.wait_ge(prep_dve, 1)
                    nc.scalar.activation(ba[:, :, :], bb[:, :, :], ACT.Square).then_inc(prep_act, 1)
                if b == 5:
                    act.wait_ge(head_mm, 1)
                    for c in range(4):
                        ins = nc.scalar.activation(br[:, 2 * c:2 * c + 2, :].rearrange("p j n -> p (j n)"),
                                                   aux[:, c, :], ACT.Sqrt)
                    ins.then_inc(prep_act, 1)
                if b == 13:
                    act.wait_ge(prep_dve, 7)
                    nc.scalar.activation(br[:, :, :], aa[:, :, :], ACT.Exp, scale=-DECAY_SCALE).then_inc(prep_act, 1)
                    act.wait_ge(prep_dve, 8)
                    nc.scalar.activation(sw[:, :, :], sw[:, :, :], ACT.Exp, scale=-DECAY_SCALE).then_inc(prep_act, 1)
                if b == 14:
                    act.wait_ge(prep_act, 4)
                    nc.scalar.activation(aa[:, :, :], aa[:, :, :], ACT.Exp, scale=DECAY_SCALE).then_inc(prep_act, 1)

            with act.Fori(0, PAIRS // 2) as i:
                for s in range(2):
                    act.wait_ge(vt_mm, i * 2 + (s + 1) + GO)
                    nc.scalar.activation(vt[:, s, :, :].rearrange("p b n -> p (b n)"), aux[:, s, 0:L], ACT.Copy)\
                        .then_inc(vt_sb, 1)
                for s in range(2):
                    for h in range(2):
                        act.wait_ge(max_ready, i * 4 + (2 * s + h + 1))
                        for q, w in enumerate((slice(0, P), slice(P, 384))):
                            ins = nc.scalar.activation(eb[:, s, h, w], eb[:, s, h, w], ACT.Exp, bias=mxs[:, s, h, q, 1:2],
                                                       accum_out=mxs[:, s, h, q, 2:3])
                        ins.then_inc(p_ready, 1)
                for s in range(2):
                    act.wait_ge(pt_mm, i * 2 + (s + 1))
                    for h in range(2):
                        ins = nc.scalar.activation(pt[:, s, h, :], main[:, 2 + h, 0:384], ACT.Copy)
                    ins.then_inc(pt_sb, 1)

            with act.Fori(0, NCH) as i:
                def copy(name, after, banks, dst):
                    act.wait_ge(core_mm, i * len(MM) + MM[after] + GO)
                    for h in range(2):
                        ins = nc.scalar.activation(dst[hrow(h), :, :].rearrange("p j n -> p (j n)"),
                                                   banks[h][hrow(h), :], ACT.Copy)
                    ins.then_inc(core_act, 1)

                b0, b2, a0, a2 = ([main[:, 0], main[:, 1]], [main[:, 2], main[:, 3]],
                                  [aux[:, 0], aux[:, 1]], [aux[:, 2], aux[:, 3]])
                act.wait_ge(core_mm, i * len(MM) + MM["vt"] + GO)
                for h in range(2):
                    ins = nc.scalar.activation(st[hrow(1 - h), :, h, :], aux[hrow(1 - h), 2 + h, :]
                                               .rearrange("p (j n) -> p j n", n=CH), ACT.Copy)
                ins.then_inc(core_act, 1)
                act.wait_ge(core_mm, i * len(MM) + MM["bkt"] + GO)
                nc.scalar.activation(bkt[:, 0:4, :].rearrange("p j n -> p (j n)"), aux[:, 2, :], ACT.Copy)
                nc.scalar.activation(bkt[:, 4:8, :].rearrange("p j n -> p (j n)"), aux[:, 3, :], ACT.Copy).then_inc(core_act, 1)
                copy("n2", "n2", a0, mat["n2"])
                copy("n4", "n4", a0, mat["n4"])
                copy("n8", "n8", a0, mat["n2"])
                copy("q", "q", a0, mat["n"])
                copy("md", "md", a2, mat["md"])
                copy("q2", "q2", b0, mat["n4"])
                copy("mt", "mt", b2, mat["n2"])
                copy("x", "x", a2, xv)

            act.wait_ge(fin_dve, 1)
            nc.scalar.activation(gnt[:, :, :], vr, ACT.Square).then_inc(fin_act, 1)
            act.wait_ge(fin_mm, 2)
            for c in range(4):
                ins = nc.scalar.activation(gnt[:, 2 * c:2 * c + 2, :].rearrange("p j n -> p (j n)"), aux[:, c, :], ACT.Sqrt,
                                           bias=cst("gneps"), scale=1.0 / 64)
            ins.then_inc(fin_act, 1)

            n0 = UNIT0["wout"]
            with act.Fori(0, 4) as i:
                for b in range(4):
                    split_hi(At(n0 + 2 * b + 3, 8, i))
                    split_hi(At(n0 + 2 * b + 4, 8, i))
                    j = i * 4 + b
                    act.wait_ge(res_ready, j + (KB + 1))
                    nc.scalar.activation(sq[:, 0, :], x[:, bass.ds(j, 1), :].rearrange("p a n -> p (a n)"), ACT.Square)\
                        .then_inc(sq_ready, 1)
            n0 = UNIT0["ffn"]

            def ffn(i):
                for b in range(4):
                    split_hi(At(n0 + 2 * b + 3, 8, i))
                    split_hi(At(n0 + 2 * b + 4, 8, i))
                    if b == 0 and i is None:
                        act.wait_ge(norm_sum, 2)
                        root(aux[:, 3, 0:L], tmp[:, 0, :], 3, 1.0 / D)
                    if b % 2 == 0:
                        gate(ACT.Silu, gt[:, b // 2, :], At(56 + b // 2, 2, i), At(BLOCK0["ffn"] + b, 4, i))

            ffn(None)
            with act.Fori(1, FB // 2) as i:
                ffn(i)

            n0 = UNIT0["down"]

            def down(i, c=0, last=False):
                for b in range(4):
                    for u in range(6):
                        if not (last and 6 * b + u + 3 >= 24):
                            split_hi(At(n0 + 24 * c + 6 * b + u + 3, 24, i), down_width((u + 3) % 6))
                    j = c * 4 + b if i is None else i * 4 + b
                    act.wait_ge(res_ready, j + (2 * KB + 1))
                    xj = x[:, j, :] if i is None else x[:, bass.ds(j, 1), :].rearrange("p a n -> p (a n)")
                    nc.scalar.activation(sq[:, 0, :], xj, ACT.Square).then_inc(sq_ready, 1)

            with act.Fori(0, 3) as i:
                down(i)
            down(None, 3, True)
            act.wait_ge(norm_sum, 3)
            root(aux[:, 3, 0:L], tmp[:, 0, :], 4, 1.0 / D)

        @block.vector
        def _(dve):
            V = nc.vector
            link = Links(dve, dve_link)
            for counted in (bu_used, y_used, e_ready, att_ready):
                dve.sem_inc(counted, GO)

            def split_lo(n, width=U):
                s = n.c % RING
                dve.wait_ge(hi_ready, n.v(1))
                V.tensor_tensor(wlo[:, s, 0:width], raw[:, s, 0:width], whi[:, s, 0:width].bitcast(F32), ALU.subtract)\
                    .then_inc(lo_ready, 1)

            def bank(g):
                return main[:, g.c % 4, 0:L]

            def evac(ins, g):
                return ins.then_inc(bank_free[g.c % 4], 1)

            def to_gate(g, k):
                if k.i is not None or k.c >= 2:
                    dve.wait_ge(gate_out, k.v(-1))
                dve.wait_ge(rstd_ready, 1)
                evac(V.tensor_tensor(tz[:, k.c % 2, :], bank(g), rstd[:, :], ALU.mult), g)

            def split_value(val, hi, lo, ready):
                link(V.tensor_copy(hi, val))
                V.tensor_tensor(lo, val, hi.bitcast(F32), ALU.subtract).then_inc(ready, 1)

            def blk(t, j):
                if isinstance(j, int):
                    return t[:, j, :]
                return t[:, bass.ds(j, 1), :].rearrange("p a n -> p (a n)")

            for s in range(3):
                split_lo(At(s))
            dve.wait_ge(x_loaded, 16)
            dve.wait_ge(par_loaded, 16)
            for j in range(KB):
                link(V.tensor_scalar(xh[:, j, :], x[:, j, :], par_c("norm_g", j), None, ALU.mult))
                V.scalar_tensor_tensor(xl[:, j, :], x[:, j, :], par_c("norm_g", j), xh[:, j, :].bitcast(F32),
                                       ALU.mult, ALU.subtract).then_inc(in_ready, 1)
            dve.wait_ge(xsq_ready, 1)
            V.tensor_reduce(acc[:, 0, :], sqx[:, :, :].rearrange("p j t -> p t j"), AX.X, ALU.add).then_inc(acc_ready, 1)
            dve.wait_ge(root_ready, 1)
            link(V.reciprocal(rstd[:, :], tmp[:, 0, :]))
            V.tensor_tensor(rstd2[:, :], rstd[:, :], rstd[:, :], ALU.mult).then_inc(rstd_ready, 1)

            def pv(name):
                c, w = PCOLS[name]
                return par[:, c:c + w]

            s = {n: t[:, :] for n, t in sv.items()}
            dve.wait_ge(s_act, 1)
            V.tensor_tensor(s["er"], pv("a_re"), s["dt"], ALU.mult).then_inc(s_dve, 1)
            link(V.tensor_tensor(s["theta"], pv("a_im"), s["dt"], ALU.mult))
            link(V.tensor_scalar(s["kk"], s["theta"], 1.0 / TWO_PI, None, ALU.mult))
            link(V.tensor_scalar(s["kk"], s["kk"], ROUND, ROUND, ALU.add, ALU.subtract))
            link(V.scalar_tensor_tensor(s["t0"], s["kk"], -PI_A, s["theta"], ALU.mult, ALU.add))
            link(V.scalar_tensor_tensor(s["t1"], s["kk"], -PI_B, s["t0"], ALU.mult, ALU.add))
            link(V.scalar_tensor_tensor(s["t2"], s["kk"], -PI_C, s["t1"], ALU.mult, ALU.add))
            link(V.tensor_scalar(s["t2"], s["t2"], 1.0 / TWO_PI, 0.5, ALU.mult, ALU.min))
            V.tensor_scalar(phi[:, :], s["t2"], -0.5, None, ALU.max).then_inc(s_dve, 1)

            def step(n, b):
                split_lo(At(n.c + 2 * b + 3, n.m, n.i))
                split_lo(At(n.c + 2 * b + 4, n.m, n.i))
                dve.wait_ge(unit_used, At(n.c + 2 * b + 2, n.m, n.i).v())

            n0, g0 = At(UNIT0["u"]), BLOCK0["u"]
            for b in range(8):
                step(n0, b)
                evac(V.tensor_tensor(ug[:, b, :], bank(At(g0 + b)), rstd[:, :], ALU.mult), At(g0 + b))
                if b == 2:
                    dve.wait_ge(s_act, 4)
                    link(V.tensor_tensor(s["t0"], rho[:, :], s["cos"], ALU.mult))
                    link(V.tensor_scalar(s["t0"], s["t0"], 1.0, None, ALU.subtract))
                    link(V.tensor_tensor(s["t1"], rho[:, :], s["sin"], ALU.mult))
                    link(V.tensor_tensor(s["den"], pv("a_re"), pv("a_re"), ALU.mult))
                    link(V.tensor_tensor(s["den2"], pv("a_im"), pv("a_im"), ALU.mult))
                    link(V.tensor_tensor(s["den"], s["den"], s["den2"], ALU.add))
                    link(V.reciprocal(s["den"], s["den"]))
                    link(V.tensor_tensor(s["lr"], pv("a_re"), s["den"], ALU.mult))
                    link(V.tensor_tensor(s["li"], pv("a_im"), s["den"], ALU.mult))
                if b == 3:
                    link(V.tensor_tensor(s["kre"], s["t0"], s["lr"], ALU.mult))
                    link(V.tensor_tensor(s["t2"], s["t1"], s["li"], ALU.mult))
                    link(V.tensor_tensor(s["kre"], s["kre"], s["t2"], ALU.add))
                    link(V.tensor_tensor(s["kim"], s["t1"], s["lr"], ALU.mult))
                    link(V.tensor_tensor(s["t2"], s["t0"], s["li"], ALU.mult))
                    link(V.tensor_tensor(s["kim"], s["kim"], s["t2"], ALU.subtract))
                if b in (4, 5):
                    dve.wait_ge(c_loaded, 16)
                    if b == 5:
                        dve.wait_ge(scan_const, 1)
                    ka, kb_ = ("kre", "kim") if b == 4 else ("kim", "kre")
                    kav = s[ka].unsqueeze(2).to_broadcast([P, STATE_TILES, 32])
                    kbv = s[kb_].unsqueeze(2).to_broadcast([P, STATE_TILES, 32])
                    link(V.tensor_tensor(cw[:, 0, :, :], craw[:, 0, :, :], kav, ALU.mult))
                    link(V.tensor_tensor(cw[:, 1, :, :], craw[:, 1, :, :], kbv, ALU.mult))
                    dst = cp[:, :, :, b - 4, :].rearrange("p a b c -> p (a b) c")
                    if b == 4:
                        V.tensor_tensor(dst, cw[:, 0, :, :], cw[:, 1, :, :], ALU.subtract).then_inc(scan_const, 1)
                    else:
                        link(V.tensor_tensor(cw[:, 0, :, :], cw[:, 0, :, :], cw[:, 1, :, :], ALU.add))
                        V.tensor_scalar(dst, cw[:, 0, :, :], -1.0, None, ALU.mult).then_inc(scan_const, 1)
                if b == 6:
                    V.memset(convc[:, 0:2], 0.0).then_inc(scan_const, 1)

            n0, g0 = At(UNIT0["zb"]), BLOCK0["zb"]
            for b in range(8):
                step(n0, b)
                to_gate(At(g0 + b), At(b))

            def scan_in(i, t):
                if t == 0:
                    dve.wait_ge(trig_ready, i + 1)
                dve.wait_ge(bu_ready, i * TPB + (t + 1))
                cb = cosi[:, t, :].unsqueeze(1).to_broadcast([P, 2, L])
                sb_ = sini[:, t, :].unsqueeze(1).to_broadcast([P, 2, L])
                bu = aux[:, t % 2, :].rearrange("p (a n) -> p a n", a=2)
                V.tensor_tensor(m1[:, :, :], bu, cb, ALU.mult)
                V.tensor_tensor(m2[:, :, :], bu, sb_, ALU.mult).then_inc(bu_used, 1)
                dve.wait_ge(bu_used, i * TPB + (t + 1) + GO)
                dve.wait_ge(h_ready, i * TPB + max(t - 1, 0) + GO)
                g = gs[t % 2]
                V.tensor_tensor(g[:, 0, :], m1[:, 0, :], m2[:, 1, :], ALU.add)
                link(V.tensor_tensor(g[:, 1, :], m1[:, 1, :], m2[:, 0, :], ALU.subtract))
                r = rho[:, bass.ds(i * TPB + t, 1)].to_broadcast([P, L])
                V.tensor_tensor_scan(g[:, 0, :], r, g[:, 0, :], 0.0, ALU.mult, ALU.add)
                V.tensor_tensor_scan(g[:, 1, :], r, g[:, 1, :], 0.0, ALU.mult, ALU.add).then_inc(gs_ready, 1)

            n0, g0 = UNIT0["conv"], BLOCK0["conv"]
            CONV_LINKS = 16
            with dve.Fori(0, SB) as i:
                link.loop(i, CONV_LINKS)
                nn = At(n0, 16, i)
                for b in range(8):
                    step(nn, b)
                    g = At(g0 + b, 8, i)
                    q = b // 4
                    j = i * 2 + q
                    if b % 4 == 0:
                        to_gate(g, At(8 + q, 2, i))
                    elif b % 4 == 1:
                        evac(V.tensor_tensor(convv, bank(g), rstd2[:, :], ALU.mult), g)
                        dve.wait_ge(bank_free[g.c % 4], g.turns(4, 1))
                    elif b % 4 == 2:
                        evac(V.tensor_tensor(convc[:, 2:L + 2], bank(g), convv, ALU.mult), g)
                        dve.wait_ge(bank_free[g.c % 4], g.turns(4, 1))
                        link(V.tensor_scalar(tmp[:, 0, :], convc[:, 0:L], par_c("conv0", j), None, ALU.mult))
                        link(V.scalar_tensor_tensor(convv, convc[:, 1:L + 1], par_c("conv1", j), tmp[:, 0, :],
                                                    ALU.mult, ALU.add))
                        link(V.scalar_tensor_tensor(tmp[:, 0, :], convc[:, 2:L + 2], par_c("conv2", j), convv,
                                                    ALU.mult, ALU.add))
                    else:
                        evac(V.tensor_tensor(convv, bank(g), tmp[:, 0, :], ALU.mult), g)
                        dve.wait_ge(bank_free[g.c % 4], g.turns(4, 1))
                        link(V.tensor_tensor(convv, convv, rstd[:, :], ALU.mult))
                        dve.wait_ge(gate_out, i * 2 + (8 + q + 1))
                        link(V.tensor_tensor(f[:, 0, :], convv, gt[:, q % 2, :], ALU.mult))
                        split_value(f[:, 0, :], blk(yah, j), blk(yal, j), ya_ready)
                    if b in SCAN_IN:
                        scan_in(i, SCAN_IN.index(b))
                dve.wait_ge(h_used, i * TPB + TPB + GO)
                V.scalar_tensor_tensor(blk(ug, i), blk(ug, i), par_c("d_skip", i), aux[:, 2, 0:L], ALU.mult, ALU.add)\
                    .then_inc(y_used, 1)
            link.done(SB)

            n0, g0 = UNIT0["gb"], BLOCK0["gb"]
            with dve.Fori(0, 4) as i:
                for b in range(4):
                    step(At(n0, 8, i), b)
                    to_gate(At(g0 + b, 4, i), At(24 + b, 4, i))

            n0, g0 = UNIT0["gaa"], BLOCK0["gaa"]
            with dve.Fori(0, 8) as i:
                for b in range(4):
                    step(At(n0, 8, i), b)
                    g = At(g0 + b, 4, i)
                    if b % 2 == 0:
                        to_gate(g, At(40 + b // 2, 2, i))
                    else:
                        dve.wait_ge(gate_out, i * 2 + (40 + b // 2 + 1))
                        evac(V.tensor_tensor(blk(mix, i * 2 + b // 2), gt[:, b // 2, :], bank(g), ALU.mult), g)

            dve.wait_ge(gelu_ready, 1)
            dve.wait_ge(unit_used, UNIT0["glu"])
            for j in range(SB):
                split_value(ug[:, j, :], ybh[:, j, :], ybl[:, j, :], yb_ready)

            n0, g0 = UNIT0["glu"], BLOCK0["glu"]
            for b in range(8):
                split_lo(At(n0 + b + 3))
                dve.wait_ge(glu_out, b + 1)
                evac(V.tensor_tensor(tmp[:, 0, :], ug[:, b, :], gt[:, b % 2, :], ALU.mult), At(g0 + b))
                dve.wait_ge(bank_free[(g0 + b) % 4], (g0 + b) // 4 + 1)
                link(V.tensor_tensor(f[:, b % 2, :], tmp[:, 0, :], szb[:, b, :], ALU.mult))
                split_value(f[:, b % 2, :], yoh[:, b, :], yol[:, b, :], yo_ready)

            n0, g0 = UNIT0["outb"], BLOCK0["outb"]
            with dve.Fori(0, 4) as i:
                link.loop(i, 8)
                for b in range(4):
                    split_lo(At(n0 + b + 3, 4, i))
                    dve.wait_ge(unit_used, At(n0 + b + 1, 4, i).v())
                    g = At(g0 + b, 4, i)
                    j = i * 4 + b
                    evac(V.tensor_tensor(tmp[:, 0, :], bank(g), blk(sgb, j), ALU.mult), g)
                    dve.wait_ge(bank_free[g.c % 4], g.turns(4, 1))
                    link(V.tensor_tensor(f[:, b % 2, :], tmp[:, 0, :], blk(mix, j), ALU.add))
                    split_value(f[:, b % 2, :], blk(mh, j), blk(ml, j), m_ready)
            link.done(4)

            c1, _ = PCOLS["final_g"]
            c2, _ = PCOLS["norm1"]
            link(V.tensor_tensor(gg[:, :], par[:, c1:c1 + KB], par[:, c2:c2 + KB], ALU.mult))
            link(V.memset(acc[:, :, :], 0.0))
            n0, g0 = UNIT0["wo"], BLOCK0["wo"]
            with dve.Fori(0, 4) as i:
                link.loop(i, 4)
                for b in range(4):
                    step(At(n0, 8, i), b)
                    g = At(g0 + b, 4, i)
                    j = i * 4 + b
                    xj = blk(x, j)
                    evac(V.tensor_tensor(xj, xj, bank(g), ALU.add), g)
                    dve.wait_ge(bank_free[g.c % 4], g.turns(4, 1))
                    gj = gg[:, bass.ds(j, 1)]
                    V.tensor_scalar(blk(nh, j), xj, gj, None, ALU.mult).then_inc(res_ready, 1)
                    dve.wait_ge(res_ready, j + 1)
                    V.scalar_tensor_tensor(blk(nl, j), xj, gj, blk(nh, j).bitcast(F32), ALU.mult, ALU.subtract)\
                        .then_inc(in_ready, 1)
                    dve.wait_ge(sq_ready, j + 1)
                    link(V.tensor_tensor(acc[:, :, :], acc[:, :, :], sq[:, :, :], ALU.add))
            link.done(4)
            V.memset(tmp[:, 1, 0:1], 0.0).then_inc(acc_ready, 1)

            def wide(name, j0=0, n=8):
                c, _ = PCOLS[name]
                return par[:, c + j0:c + j0 + n].unsqueeze(2).to_broadcast([P, n, L])

            n0, g0 = UNIT0["lora"], BLOCK0["lora"]
            link(V.memset(zs[:, 0:1], 0.0))
            for b in range(3):
                step(At(n0), b)
                g = At(g0 + b)
                if b == 0:
                    dve.wait_ge(norm_root, 1)
                    link(V.reciprocal(rstd2[:, :], tmp[:, 0, :]))
                    link(V.tensor_tensor(tmp[:, 1, :], aux[:, 3, L:2 * L], rstd2[:, :], ALU.mult))
                    V.tensor_tensor(tmp[:, 1, :], tmp[:, 1, :], rstd2[:, :], ALU.mult).then_inc(ms_ready, 1)
                    dve.wait_ge(norm_root, 2)
                    link(V.reciprocal(rstd[:, :], tmp[:, 0, :]))
                    V.tensor_tensor(rstd[:, :], rstd[:, :], rstd2[:, :], ALU.mult).then_inc(rstd_ready, 1)
                    dve.wait_ge(rstd_ready, 2)
                evac(V.tensor_tensor(zs[:, 1:L + 1], bank(g), rstd[:, :], ALU.mult), g)
                dve.wait_ge(bank_free[g.c % 4], g.turns(4, 1))
                link(V.tensor_tensor(tmp[:, 0, :], zs[:, 0:L], zs[:, 1:L + 1], ALU.subtract))
                dst = lo[:, :] if b == 0 else f[:, b - 1, :]
                V.scalar_tensor_tensor(dst, tmp[:, 0, :], par_c("mix_lo", b), zs[:, 1:L + 1], ALU.mult, ALU.add)\
                    .then_inc(lo_shifted, 1)
                dve.wait_ge(lo_shifted, b + 1)
            n0, g0 = UNIT0["rkv"], BLOCK0["rkv"]
            with dve.Fori(0, 6) as i:
                link.loop(i, 8)
                for b in range(4):
                    step(At(n0, 8, i), b)
                    g = At(g0 + b, 4, i)
                    j = i * 4 + b
                    evac(V.tensor_tensor(zs[:, 1:L + 1], bank(g), rstd[:, :], ALU.mult), g)
                    dve.wait_ge(bank_free[g.c % 4], g.turns(4, 1))
                    link(V.tensor_tensor(tmp[:, 0, :], zs[:, 0:L], zs[:, 1:L + 1], ALU.subtract))
                    link(V.scalar_tensor_tensor(blk(zr, j), tmp[:, 0, :], par_c("mix_rkv", j), zs[:, 1:L + 1],
                                                ALU.mult, ALU.add))
            link.done(6)

            n0, g0 = UNIT0["qkv"], BLOCK0["qkv"]
            prepared = [0]

            def prep(ins):
                prepared[0] += 1
                ins.then_inc(prep_dve, 1)
                dve.wait_ge(prep_dve, prepared[0])

            c, _ = CCOLS["inchunk"]
            inchunk = const[:, c:c + L]
            for b in range(24):
                step(At(n0), b)
                g = At(g0 + b)
                evac(V.tensor_tensor(qkv[:, b, :], bank(g), rstd[:, :], ALU.mult), g)
                if b == 0:
                    prep(V.tensor_tensor(bb[:, :, :], kr, wide("k_k"), ALU.mult))
                if b == 2:
                    dve.wait_ge(up_act, 8)
                    dve.wait_ge(prep_act, 1)
                if b == 3:
                    pass
                if b == 7:
                    dve.wait_ge(prep_act, 2)
                    link(V.tensor_scalar(br[:, :, :], br[:, :, :], 1e-12, None, ALU.max))
                    prep(V.reciprocal(br[:, :, :], br[:, :, :]))
                if b == 8:
                    prep(V.tensor_tensor(bb[:, :, :], bb[:, :, :], br[:, :, :], ALU.mult))
                    link(V.scalar_tensor_tensor(ba[:, :, :], aa[:, :, :], -1.0, wide("k_a"), ALU.add, ALU.mult))
                if b == 9:
                    prep(V.scalar_tensor_tensor(kr, ba[:, :, :], 1.0, kr, ALU.add, ALU.mult))
                    link(V.tensor_scalar(ba[:, :, :], bb[:, :, :], -1.0, None, ALU.mult))
                if b == 10:
                    prep(V.tensor_tensor(bb[:, :, :], bb[:, :, :], aa[:, :, :], ALU.mult))
                if b == 11:
                    for j in range(4):
                        V.tensor_tensor_scan(aa[:, j, :], inchunk, sw[:, j, :], 0.0, ALU.mult, ALU.add)
                if b == 12:
                    for j in range(4, 8):
                        ins = V.tensor_tensor_scan(aa[:, j, :], inchunk, sw[:, j, :], 0.0, ALU.mult, ALU.add)
                    prep(ins)
                    prep(V.tensor_copy(tmp[:, 0, 0:1], aa[:, 0, 0:1]))
                    prep(V.tensor_tensor(sw[:, :, :], aa[:, :, :], sw[:, :, :], ALU.subtract))
                if b == 14:
                    dve.wait_ge(prep_act, 3)
                    V.tensor_copy(pc[:, :, :], br[:, :, :].rearrange("p j (c t) -> p j c t", t=CH)[:, :, :, CH - 1])
                    dve.wait_ge(prep_act, 4)
                    prep(V.tensor_tensor(ba[:, :, :], ba[:, :, :], sw[:, :, :], ALU.mult))
                if b == 15:
                    link(V.tensor_tensor(sw[:, :, :], rr, wide("r_k"), ALU.mult))
                if b == 16:
                    prep(V.tensor_tensor(sw[:, :, :], sw[:, :, :], kr, ALU.mult))
                if b == 17:
                    link(V.tensor_tensor(br[:, :, :], br[:, :, :], rr, ALU.mult))
                if b == 18:
                    dve.wait_ge(prep_act, 5)
                    link(V.tensor_tensor(bb[:, :, :], bb[:, :, :], aa[:, :, :], ALU.mult))
                if b == 19:
                    link(V.tensor_tensor(kr, kr, aa[:, :, :], ALU.mult))
                if b in (21, 22):
                    dve.wait_ge(head_mm, 2)
                    for c in range(2 * (b - 21), 2 * (b - 21) + 2):
                        ins = V.tensor_tensor(sw[:, 2 * c:2 * c + 2, :].rearrange("p j n -> p (j n)"), aux[:, c, :],
                                              vr[:, 2 * c:2 * c + 2, :].rearrange("p j n -> p (j n)"), ALU.mult)
                    prep(ins)
            assert prepared[0] == PREP_DVE

            with dve.Fori(0, PAIRS // 2) as i:
                link.loop(i, 10)
                for s in range(2):
                    for h in range(2):
                        n = 2 * s + h
                        dve.wait_ge(bias_ready, i * 2 + (s + 1))
                        dve.wait_ge(sc_mm, i * 2 + (s + 1))
                        V.scalar_tensor_tensor(eb[:, s, h, :], main[:, h, 0:384], ATTN_SCALE, biasb[:, s, h, :],
                                               ALU.mult, ALU.add).then_inc(e_ready, 1)
                        dve.wait_ge(e_ready, i * 4 + (n + 1) + GO)
                        V.tensor_reduce(mxs[:, s, h, 0, 0:1], eb[:, s, h, 0:P], AX.X, ALU.max)
                        link(V.tensor_reduce(mxs[:, s, h, 1, 0:1], eb[:, s, h, P:384], AX.X, ALU.max))
                        V.tensor_scalar(mxs[:, s, h, :, 1], mxs[:, s, h, :, 0], -1.0, None, ALU.mult).then_inc(max_ready, 1)
                for s in range(2):
                    for h in range(2):
                        n = 2 * s + h
                        dve.wait_ge(p_ready, i * 4 + (n + 1))
                        link(V.reciprocal(mxs[:, s, h, :, 3], mxs[:, s, h, :, 2]))
                        V.tensor_scalar(eb[:, s, h, 0:P], eb[:, s, h, 0:P], mxs[:, s, h, 0, 3:4], None, ALU.mult)
                        V.tensor_scalar(eb[:, s, h, P:384], eb[:, s, h, P:384], mxs[:, s, h, 1, 3:4], None, ALU.mult)\
                            .then_inc(pn_ready, 1)
                for s in range(2):
                    dve.wait_ge(o_mm, i * 2 + (s + 1))
                    o = aux[:, 2 + s, 0:L]
                    j = i * 2 + s
                    link(V.tensor_copy(blk(mxh, j), o))
                    V.tensor_tensor(blk(mxl, j), o, blk(mxh, j).bitcast(F32), ALU.subtract).then_inc(att_ready, 1)
            link.done(PAIRS // 2)

            link(V.memset(state[:, :, :], 0.0))
            b0, b2, a0, a2 = ([main[:, 0], main[:, 1]], [main[:, 2], main[:, 3]],
                              [aux[:, 0], aux[:, 1]], [aux[:, 2], aux[:, 3]])

            def mask(name, h, n=8):
                c, w = CCOLS[name]
                return const[hrow(h), c:c + w].unsqueeze(1).to_broadcast([64, n, w])

            def flat(t, h):
                return t[hrow(h), :, :].rearrange("p j n -> p (j n)")

            def heads(bank_, h):
                return bank_[h][hrow(h), :].rearrange("p (j n) -> p j n", n=CH)

            def stage(i):
                t = tokens(i)
                for h in range(2):
                    V.tensor_copy(bkc[hrow(h), :, h, :], bb[hrow(h), :, t])
                    ins = V.tensor_copy(bkc[hrow(h), :, 1 - h, :], kr[hrow(h), :, t])
                ins.then_inc(staged, 1)

            def tokens(i):
                return slice(i * CH, (i + 1) * CH) if isinstance(i, int) else bass.ds(i * CH, CH)

            dve.wait_ge(pt_sb, PAIRS + GO)
            dve.wait_ge(o_mm, PAIRS)
            stage(0)

            def chunk(i, last=False):
                def mm(name):
                    dve.wait_ge(core_mm, i * len(MM) + MM[name] + GO)

                def done(name, ins):
                    ins.then_inc(core_dve, 1)
                    dve.wait_ge(core_dve, i * len(DV) + DV[name])

                mm("g")
                for c in range(4):
                    cm, _ = CCOLS["maskg"]
                    ins = V.tensor_tensor(gm[:, c // 2, 4 * (c % 2):4 * (c % 2) + 4, :],
                                          main[:, c, :].rearrange("p (j n) -> p j n", n=P),
                                          const[:, cm:cm + P].unsqueeze(1).to_broadcast([P, 4, P]), ALU.mult)
                done("gm", ins)
                mm("n")
                for h in range(2):
                    V.tensor_tensor(mat["n"][hrow(h), :, :], heads(a0, h), mask("mdiag", h), ALU.mult)
                    V.tensor_tensor(mat["f"][hrow(h), :, :], heads(a0, h), mask("moff", h), ALU.mult)
                    ins = V.tensor_tensor(mat["nt"][hrow(h), :, :], gm[hrow(h), h, :, 0:CH], mask("mdiagt", h), ALU.mult)
                done("nf", ins)
                cm, _ = CCOLS["eye64"]
                eye = const[:, cm:cm + CH].unsqueeze(1).to_broadcast([P, 8, CH])
                done("w1", V.tensor_tensor(mat["w"][:, :, :], mat["nt"][:, :, :], eye, ALU.add))

                def take(name, banks, dst):
                    mm(name)
                    for h in range(2):
                        ins = V.tensor_copy(flat(dst, h), banks[h][hrow(h), :])
                    done(name, ins)

                def plus(name, banks, dst, old):
                    mm(name)
                    for h in range(2):
                        ins = V.tensor_tensor(flat(dst, h), flat(old, h), banks[h][hrow(h), :], ALU.add)
                    done(name, ins)

                for h in range(2):
                    V.memset(st[hrow(h), :, h, :], 0.0)
                take("n2t", b0, mat["n2t"])
                if not last:
                    stage(i + 1)
                plus("w2", b2, mat["w"], mat["w"])
                take("n4t", b0, mat["n4t"])
                plus("w4", b2, mat["w"], mat["w"])
                plus("w8", b2, mat["w"], mat["w"])
                take("qt", b0, mat["nt"])
                done("t1", V.tensor_tensor(mat["n2t"][:, :, :], mat["nt"][:, :, :], eye, ALU.add))
                plus("g1", a0, mat["n4t"], mat["n2t"])
                mm("sa")
                for h in range(2):
                    ins = V.tensor_copy(st[hrow(h), :, h, :], heads(b0, h))
                done("sa", ins)
                mm("y")
                for h in range(2):
                    ins = V.tensor_copy(vr[hrow(h), :, tokens(i)], heads(a0, h))
                done("y", ins)
                mm("s")
                link(V.tensor_tensor(state[:, :, :], state[:, :, :],
                                     aux[:, 2, :].rearrange("p (j n) -> p j n", n=CH), ALU.add))
                done("s", V.tensor_tensor(state[:, :, :], state[:, :, :], (pc[:, :, i:i + 1] if last else pc[:, :, bass.ds(i, 1)]).to_broadcast([P, 8, CH]),
                                          ALU.mult))

            with dve.Fori(0, NCH - 1) as i:
                link.loop(i, 1)
                chunk(i)
            link.done(NCH - 1)
            chunk(NCH - 1, True)

            def four(t, c):
                return t[:, 2 * c:2 * c + 2, :].rearrange("p j n -> p (j n)")

            dve.wait_ge(fin_mm, 1)
            for c in range(4):
                ins = V.scalar_tensor_tensor(four(vr, c), aux[:, c, :], -1.0 / 64, four(vr, c), ALU.mult, ALU.add)
            ins.then_inc(fin_dve, 1)
            dve.wait_ge(fin_act, 2)
            link(V.reciprocal(gnt[:, :, :], gnt[:, :, :]))
            link(V.tensor_tensor(vr, vr, gnt[:, :, :], ALU.mult))
            for j in range(8):
                ins = V.tensor_scalar(vr[:, j, :], vr[:, j, :], par_c("ln_w", j), par_c("ln_b", j), ALU.mult, ALU.add)
            link(ins)
            link(V.tensor_tensor(vr, vr, sw[:, :, :], ALU.add))
            for j in range(8):
                dve.wait_ge(gu_mm, j + 1)
                V.tensor_tensor(f[:, j % 2, :], vr[:, j, :], main[:, j % 4, 0:L], ALU.mult).then_inc(fin_dve, 1)
                dve.wait_ge(fin_dve, j + 2)
                split_value(f[:, j % 2, :], mxh[:, 8 + j, :], mxl[:, 8 + j, :], rwkv_ready)

            link(V.memset(acc[:, 0, :], 0.0))
            n0, g0 = UNIT0["wout"], BLOCK0["wout"]
            dve.wait_ge(res_scaled, 1)
            with dve.Fori(0, 4) as i:
                link.loop(i, 4)
                for b in range(4):
                    step(At(n0, 8, i), b)
                    g = At(g0 + b, 4, i)
                    j = i * 4 + b
                    xj = blk(x, j)
                    evac(V.tensor_tensor(xj, xj, bank(g), ALU.add), g)
                    dve.wait_ge(bank_free[g.c % 4], g.turns(4, 1))
                    V.tensor_scalar(blk(x3h, j), xj, par_c("norm2", j), None, ALU.mult).then_inc(res_ready, 1)
                    dve.wait_ge(res_ready, j + (KB + 1))
                    V.scalar_tensor_tensor(blk(x3l, j), xj, par_c("norm2", j), blk(x3h, j).bitcast(F32),
                                           ALU.mult, ALU.subtract).then_inc(in_ready, 1)
                    dve.wait_ge(sq_ready, j + (KB + 1))
                    link(V.tensor_tensor(acc[:, 0, :], acc[:, 0, :], sq[:, 0, :], ALU.add))
            link.done(4)
            V.memset(tmp[:, 1, 0:1], 0.0).then_inc(acc_ready, 1)

            n0, g0 = UNIT0["ffn"], BLOCK0["ffn"]

            def ffn(i):
                for b in range(4):
                    step(At(n0, 8, i), b)
                    g = At(g0 + b, 4, i)
                    if b == 0 and i is None:
                        dve.wait_ge(norm_root, 3)
                        V.reciprocal(rstd[:, :], tmp[:, 0, :]).then_inc(rstd_ready, 1)
                        dve.wait_ge(rstd_ready, 3)
                    if b % 2 == 0:
                        to_gate(g, At(56 + b // 2, 2, i))
                    else:
                        k = At(56 + b // 2, 2, i)
                        evac(V.tensor_tensor(tmp[:, 0, :], bank(g), rstd[:, :], ALU.mult), g)
                        dve.wait_ge(bank_free[g.c % 4], g.turns(4, 1))
                        dve.wait_ge(gate_out, k.v(1))
                        j = b // 2 if i is None else i * 2 + b // 2
                        link(V.tensor_tensor(f[:, b // 2, :], tmp[:, 0, :], gt[:, b // 2, :], ALU.mult))
                        split_value(f[:, b // 2, :], blk(ah, j), blk(al, j), act_ready)

            ffn(None)
            with dve.Fori(1, FB // 2) as i:
                link.loop(i, 4, 1)
                ffn(i)
            link.done(FB // 2 - 1)

            link(V.memset(acc[:, 0, :], 0.0))
            n0, g0 = UNIT0["down"], BLOCK0["down"]

            def down(i, c=0, last=False):
                for b in range(4):
                    for u in range(6):
                        if not (last and 6 * b + u + 3 >= 24):
                            split_lo(At(n0 + 24 * c + 6 * b + u + 3, 24, i), down_width((u + 3) % 6))
                    dve.wait_ge(unit_used, At(n0 + 24 * c + 6 * b + 6, 24, i).v())
                    g = At(g0 + 4 * c + b, 4, i)
                    j = c * 4 + b if i is None else i * 4 + b
                    xj = blk(x, j)
                    V.tensor_tensor(xj, xj, bank(g), ALU.add).then_inc(res_ready, 1)
                    dve.wait_ge(res_ready, j + (2 * KB + 1))
                    dve.wait_ge(sq_ready, j + (2 * KB + 1))
                    evac(V.tensor_tensor(acc[:, 0, :], acc[:, 0, :], sq[:, 0, :], ALU.add), g)
                    dve.wait_ge(bank_free[g.c % 4], g.turns(4, 1))

            with dve.Fori(0, 3) as i:
                down(i)
            down(None, 3, True)
            V.memset(tmp[:, 1, 0:1], 0.0).then_inc(acc_ready, 1)
            dve.wait_ge(norm_root, 4)
            link(V.reciprocal(rstd[:, :], tmp[:, 0, :]))
            for j in range(KB):
                ins = V.scalar_tensor_tensor(x[:, j, :], x[:, j, :], par_c("final2", j), rstd[:, :], ALU.mult, ALU.mult)
                if j % 4 == 3:
                    ins.then_inc(out_ready, 1)

        @block.tensor
        def _(pe):
            for counted in (h_used, vt_mm, core_mm):
                pe.sem_inc(counted, GO)

            def unit(n, g, xh_, xl_, kb0, kbs, first, last, width=8):
                s = n.c % RING
                pe.wait_ge(lo_ready, n.v(1))
                out = main[:, g.c % 4, 0:L]
                for kk in range(kbs):
                    w = slice(kk * P, (kk + 1) * P)
                    k = kb0 + kk
                    nc.tensor.matmul(out, whi[:, s, w], xh_[:, k, :], start=(first and kk == 0), stop=False)
                    nc.tensor.matmul(out, whi[:, s, w], xl_[:, k, :], start=False, stop=False)
                    ins = nc.tensor.matmul(out, wlo[:, s, w], xh_[:, k, :], start=False, stop=(last and kk == kbs - 1))
                ins.then_inc(unit_used, 1)

            def free(g):
                if g.i is not None or g.c >= 4:
                    pe.wait_ge(bank_free[g.c % 4], g.turns(4))

            def column(n, g, xh_, xl_):
                free(g)
                unit(n, g, xh_, xl_, 0, 8, True, False)
                unit(n + 1, g, xh_, xl_, 8, 8, False, True)

            def head_sum(out, w, v):
                return nc.tensor.matmul(out, w, v, start=True, stop=True)

            n0, g0 = UNIT0["u"], BLOCK0["u"]
            for b in range(8):
                if b == 0:
                    pe.wait_ge(in_ready, KB)
                column(At(n0 + 2 * b), At(g0 + b), xh, xl)
                if b == 0:
                    pe.wait_ge(acc_ready, 1)
                    pe.wait_ge(const_loaded, 16)
                    head_sum(aux[:, 3, 0:L], cst("ones"), acc[:, 0, :]).then_inc(ssq_ready, 1)
            n0, g0 = UNIT0["zb"], BLOCK0["zb"]
            for b in range(8):
                column(At(n0 + 2 * b), At(g0 + b), xh, xl)

            def scan_bu(i, t):
                if t == 0:
                    pe.wait_ge(b_loaded, i * 16 + 16)
                pe.wait_ge(bu_used, (i * TPB if t < 2 else i * TPB + (t - 1)) + GO)
                uj = ug[:, bass.ds(i, 1), :].rearrange("p a n -> p (a n)")
                nc.tensor.matmul(aux[:, t % 2, 0:L], bstage[:, t, 0, :], uj, start=True, stop=True)
                nc.tensor.matmul(aux[:, t % 2, L:2 * L], bstage[:, t, 1, :], uj, start=True, stop=True)\
                    .then_inc(bu_ready, 1)

            def scan_y(i, t):
                if t == 0:
                    pe.wait_ge(c_staged, i + 1)
                    pe.wait_ge(y_used, i + GO)
                pe.wait_ge(h_ready, i * TPB + (t + 1) + GO)
                out = aux[32 * t:32 * t + 32, 2, 0:L]
                nc.tensor.matmul(out, cstage[:, t, 0, :], hs[:, t % 2, 0, :], start=True, stop=False,
                                 tile_position=(0, 32 * t))
                nc.tensor.matmul(out, cstage[:, t, 1, :], hs[:, t % 2, 1, :], start=False, stop=True,
                                 tile_position=(0, 32 * t)).then_inc(h_used, 1)

            n0, g0 = UNIT0["conv"], BLOCK0["conv"]
            with pe.Fori(0, SB) as i:
                for b in range(8):
                    for t in range(TPB):
                        if SCAN_BU[t] == b:
                            scan_bu(i, t)
                        if SCAN_Y[t] == b:
                            scan_y(i, t)
                    column(At(n0 + 2 * b, 16, i), At(g0 + b, 8, i), xh, xl)
            n0, g0 = UNIT0["gb"], BLOCK0["gb"]
            with pe.Fori(0, 4) as i:
                for b in range(4):
                    column(At(n0 + 2 * b, 8, i), At(g0 + b, 4, i), xh, xl)
            n0, g0 = UNIT0["gaa"], BLOCK0["gaa"]
            pe.wait_ge(ya_ready, KB)
            with pe.Fori(0, 8) as i:
                for b in range(4):
                    column(At(n0 + 2 * b, 8, i), At(g0 + b, 4, i), *((xh, xl) if b % 2 == 0 else (yah, yal)))
            n0, g0 = UNIT0["glu"], BLOCK0["glu"]
            pe.wait_ge(yb_ready, SB)
            for b in range(8):
                free(At(g0 + b))
                unit(At(n0 + b), At(g0 + b), ybh, ybl, 0, 8, True, True)
            n0, g0 = UNIT0["outb"], BLOCK0["outb"]
            pe.wait_ge(yo_ready, SB)
            with pe.Fori(0, 4) as i:
                for b in range(4):
                    free(At(g0 + b, 4, i))
                    unit(At(n0 + b, 4, i), At(g0 + b, 4, i), yoh, yol, 0, 8, True, True)
            n0, g0 = UNIT0["wo"], BLOCK0["wo"]
            pe.wait_ge(m_ready, KB)
            with pe.Fori(0, 4) as i:
                for b in range(4):
                    column(At(n0 + 2 * b, 8, i), At(g0 + b, 4, i), mh, ml)

            def norm_total(n, w):
                pe.wait_ge(acc_ready, n)
                nc.tensor.matmul(aux[:, 3, 0:w], cst("ones"), acc[:, :, :].rearrange("p a n -> p (a n)")[:, 0:w],
                                 start=True, stop=True).then_inc(norm_sum, 1)

            n0, g0 = UNIT0["lora"], BLOCK0["lora"]
            pe.wait_ge(in_ready, 2 * KB)
            for b in range(3):
                column(At(n0 + 2 * b), At(g0 + b), nh, nl)
                if b == 0:
                    norm_total(2, 2 * L)
            pe.wait_ge(lora_loaded, 16)
            pe.wait_ge(lo_act, 3)
            for j in range(8):
                if j >= 2:
                    pe.wait_ge(up_act, j - 1)
                cols = slice(j * P, (j + 1) * P)
                nc.tensor.matmul(aux[:, j % 2, 0:L], lora[0:64, cols], lo[0:64, :], start=True, stop=True)
                nc.tensor.matmul(aux[:, 2 + j % 2, 0:L], lora[64:128, cols], lo[64:128, :], start=True, stop=True)\
                    .then_inc(up_mm, 1)
            n0, g0 = UNIT0["rkv"], BLOCK0["rkv"]
            with pe.Fori(0, 6) as i:
                for b in range(4):
                    column(At(n0 + 2 * b, 8, i), At(g0 + b, 4, i), nh, nl)
            n0, g0 = UNIT0["qkv"], BLOCK0["qkv"]

            def qkv_part(first, turns):
                with pe.Fori(0, turns) as i:
                    for b in range(4):
                        column(At(n0 + 8 * first + 2 * b, 8, i), At(g0 + 4 * first + b, 4, i), nh, nl)

            def over_heads(src):
                for c in range(4):
                    ins = nc.tensor.matmul(aux[:, c, :], cst("hones"), src[:, 2 * c:2 * c + 2, :]
                                           .rearrange("p j n -> p (j n)"), start=True, stop=True)
                return ins

            qkv_part(0, 1)
            pe.wait_ge(prep_act, 1)
            pe.wait_ge(up_act, 8)
            over_heads(ba).then_inc(head_mm, 1)
            qkv_part(1, 4)
            pe.wait_ge(prep_dve, 10)
            over_heads(sw).then_inc(head_mm, 1)
            qkv_part(5, 1)

            for g in range(BLOCK0["wout"] - 4, BLOCK0["wout"]):
                pe.wait_ge(bank_free[g % 4], g // 4 + 1)
            pe.wait_ge(prep_dve, PREP_DVE)
            with pe.Fori(0, PAIRS // 2) as i:
                for s in range(2):
                    pe.wait_ge(att_staged, i * 2 + (s + 1))
                    pe.wait_ge(e_ready, i * 4 + 2 * s + GO)
                    for h in range(2):
                        nc.tensor.matmul(main[:, h, 0:P], qs[hrow(h), s, 0:P], ks[hrow(h), s, 0:P], start=True, stop=True)
                        ins = nc.tensor.matmul(main[:, h, P:384], qs[hrow(h), s, P:L], ks[hrow(h), s, :], start=True, stop=True)
                    ins.then_inc(sc_mm, 1)
                    for b in range(2):
                        ins = nc.tensor.transpose(aux[:, s, b * P:(b + 1) * P], vs[:, s, b * P:(b + 1) * P], cst("ident"))
                    ins.then_inc(vt_mm, 1)
                for s in range(2):
                    pe.wait_ge(pn_ready, i * 4 + (2 * s + 2))
                    pe.wait_ge(pt_sb, i * 2 + s + GO)
                    for h in range(2):
                        for b in range(3):
                            ins = nc.tensor.transpose(main[:, 2 + h, b * P:(b + 1) * P],
                                                      eb[:, s, h, (0, P, 2 * P)[b]:(P, 2 * P, 3 * P)[b]], cst("ident"))
                    ins.then_inc(pt_mm, 1)
                for s in range(2):
                    pe.wait_ge(pt_sb, i * 2 + (s + 1) + GO)
                    pe.wait_ge(vt_sb, i * 2 + (s + 1))
                    pe.wait_ge(att_ready, i * 2 + s + GO)
                    for h in range(2):
                        nc.tensor.matmul(aux[hrow(h), 2 + s, 0:L], vt[:, s, 0, hrow(h)], pt[:, s, h, 0:L],
                                         start=True, stop=False)
                        ins = nc.tensor.matmul(aux[hrow(h), 2 + s, P:L], vt[:, s, 1, hrow(h)], pt[:, s, h, L:384],
                                               start=False, stop=True)
                    ins.then_inc(o_mm, 1)

            pe.wait_ge(att_ready, PAIRS + GO)
            b0, b2, a0, a2 = ([main[:, 0], main[:, 1]], [main[:, 2], main[:, 3]],
                              [aux[:, 0], aux[:, 1]], [aux[:, 2], aux[:, 3]])
            for i in range(NCH):
                def dv(name):
                    pe.wait_ge(core_dve, i * len(DV) + DV[name])

                def ac(name):
                    pe.wait_ge(core_act, i * len(AC) + AC[name])

                def each(banks, fn):
                    for j in range(8):
                        for h in range(2):
                            out = banks[h][hrow(h), j * CH:(j + 1) * CH]
                            parts = fn(j, h)
                            for k, (w, v) in enumerate(parts):
                                ins = nc.tensor.matmul(out, w, v, start=(k == 0), stop=(k == len(parts) - 1))
                    ins.then_inc(core_mm, 1)

                def prod(banks, w, v):
                    each(banks, lambda j, h: [(mat[w][hrow(h), j, :], mat[v][hrow(h), j, :])])

                t = slice(i * CH, (i + 1) * CH)
                cm, _ = CCOLS["eye64"]
                pe.wait_ge(core_dve, i * len(DV))
                for j in range(8):
                    for h in range(2):
                        ins = nc.tensor.matmul(aux[hrow(1 - h), 2 + h, j * CH:(j + 1) * CH], vr[hrow(h), j, t],
                                               const[hrow(h), cm:cm + CH], start=True, stop=True)
                ins.then_inc(core_mm, 1)
                pe.wait_ge(staged, i + 1)
                for h in range(2):
                    for j in range(8):
                        ins = nc.tensor.matmul(main[:, 2 * h + j // 4, (j % 4) * P:(j % 4 + 1) * P],
                                               bkc[hrow(h), j, :, :].rearrange("p a n -> p (a n)"),
                                               abr[hrow(h), :, j, t], start=True, stop=True)
                ins.then_inc(core_mm, 1)
                each(a0, lambda j, h: [(ba[hrow(h), j, t], bkc[hrow(h), j, h, :])])
                ac("vt")
                for j in range(8):
                    ins = nc.tensor.transpose(aux[:, 2 + j // 4, (j % 4) * P:(j % 4 + 1) * P],
                                              bkc[:, j, :, :].rearrange("p a n -> p (a n)"), cst("ident"))
                ins.then_inc(core_mm, 1)
                dv("w1")
                prod(a0, "nt", "n")
                prod(b0, "n", "nt")
                ac("n2")
                prod(b2, "n2", "w")
                dv("n2t")
                prod(a0, "n2t", "n2")
                prod(b0, "n2", "n2t")
                ac("n4")
                dv("w2")
                prod(b2, "n4", "w")
                dv("n4t")
                prod(a0, "n4t", "n4")
                ac("n8")
                dv("w4")
                prod(b2, "n2", "w")
                dv("w8")
                prod(b0, "f", "w")
                prod(a0, "w", "f")
                ac("bkt")
                each(a2, lambda j, h: [(mat["w"][hrow(h), j, :], const[hrow(h), cm:cm + CH])])
                dv("qt")
                ac("q")
                prod(b0, "nt", "n")
                ac("q2")
                dv("t1")
                prod(a0, "n4", "n2t")
                ac("md")
                dv("g1")
                prod(b2, "md", "n4t")
                each(a2, lambda j, h: [(ba[hrow(h), j, t], state[hrow(h), j, :]),
                                      (gm[:, h, j, 0:CH], st[:, j, h, :])])
                ac("x")
                each(b0, lambda j, h: [(mat["n2"][hrow(h), j, :], xv[hrow(h), j, :])])
                dv("sa")
                each(a0, lambda j, h: [(state[hrow(h), j, :], br[hrow(h), j, t]), (st[:, j, h, :], gm[:, h, j, CH:P])])
                for j in range(8):
                    for h in range(2):
                        ins = nc.tensor.matmul(aux[hrow(h), 2, j * CH:(j + 1) * CH], bkt[:, j, hrow(h)], st[:, j, h, :],
                                               start=True, stop=True)
                ins.then_inc(core_mm, 1)

            pe.wait_ge(core_dve, NCH * len(DV))
            over_heads(vr).then_inc(fin_mm, 1)
            pe.wait_ge(fin_act, 1)
            pe.wait_ge(fin_dve, 1)
            over_heads(gnt).then_inc(fin_mm, 1)
            pe.wait_ge(gup_loaded, 16)
            for j in range(8):
                if j >= 4:
                    pe.wait_ge(fin_dve, j - 2)
                cols = slice(j * P, (j + 1) * P)
                nc.tensor.matmul(main[:, j % 4, 0:L], gup[:, 0, cols], sgl[:, 0, :], start=True, stop=False)
                nc.tensor.matmul(main[:, j % 4, 0:L], gup[0:32, 1, cols], sgl[0:32, 1, :], start=False, stop=True)\
                    .then_inc(gu_mm, 1)
            pe.wait_ge(rwkv_ready, 8)
            n0, g0 = UNIT0["wout"], BLOCK0["wout"]
            with pe.Fori(0, 4) as i:
                for b in range(4):
                    column(At(n0 + 2 * b, 8, i), At(g0 + b, 4, i), mxh, mxl)
            n0, g0 = UNIT0["ffn"], BLOCK0["ffn"]
            pe.wait_ge(in_ready, 3 * KB)
            for b in range(4):
                column(At(n0 + 2 * b), At(g0 + b), x3h, x3l)
                if b == 0:
                    norm_total(3, L)
            with pe.Fori(1, FB // 2) as i:
                for b in range(4):
                    column(At(n0 + 2 * b, 8, i), At(g0 + b, 4, i), x3h, x3l)
            n0, g0 = UNIT0["down"], BLOCK0["down"]
            pe.wait_ge(act_ready, FB)
            with pe.Fori(0, KB // 4) as i:
                for b in range(4):
                    g = At(g0 + b, 4, i)
                    free(g)
                    for u in range(6):
                        unit(At(n0 + 6 * b + u, 24, i), g, ah, al, 8 * u, down_width(u) // P, u == 0, u == 5)
            norm_total(4, L)


def _columns(w, cols):
    k = w.shape[0] // P
    return w[:, cols].reshape(k, P, P).transpose(1, 0, 2).reshape(P, k * P)


def _units(w, cols):
    return list(_columns(w, cols).reshape(P, -1, U).transpose(1, 0, 2))


def _rows(v):
    return np.asarray(v).reshape(-1, P).T


def _stream(w_in, w_out_a, w_glu, w_out_b, w_o, w_in_2, w_out_2, w_gate_up):
    def blk(start, j):
        return slice(start + j * P, start + (j + 1) * P)

    v, bg, cg, za, u, zb, ga, gb = (0, 2048, 4096, 6144, 8192, 9216, 10240, 12288)
    out = []
    for j in range(8):
        out += _units(w_in, blk(u, j))
    for j in range(8):
        out += _units(w_in, blk(zb, j))
    for j in range(16):
        for start in (za, v, cg, bg):
            out += _units(w_in, blk(start, j))
    for j in range(16):
        out += _units(w_in, blk(gb, j))
    for j in range(16):
        out += _units(w_in, blk(ga, j)) + _units(w_out_a, blk(0, j))
    for j in range(8):
        out += _units(w_glu, blk(0, j))
    for j in range(16):
        out += _units(w_out_b, blk(0, j))
    for j in range(16):
        out += _units(w_o, blk(0, j))
    z = 3 * 1024
    lo = np.concatenate([w_in_2[:, z + 3072:z + 3360], np.zeros((D, 96), np.float32)], axis=1)
    for j in range(3):
        out += _units(lo, blk(0, j))
    for j in range(24):
        out += _units(w_in_2, blk(z, j))
    for j in range(8):
        for start in (0, 1024, 2048):
            out += _units(w_in_2, blk(start, j))
    for j in range(16):
        out += _units(w_out_2, blk(0, j))
    for j in range(FB):
        out += _units(w_gate_up, blk(0, j)) + _units(w_gate_up, blk(FFN, j))
    assert len(out) == UNITS_MAIN
    return np.stack(out)


def _bucket(dist):
    if dist < 16:
        return dist
    big = 16 + int(np.float32(np.log(np.float32(dist) / np.float32(16))) / np.float32(math.log(2048 / 16)) * np.float32(16))
    return min(big, 31)


def _spans():
    q = np.arange(P)[:, None]
    return np.concatenate([q - np.arange(P)[None, :], q + P - np.arange(L)[None, :]], axis=1)


def _constants():
    c = np.zeros((P, NCONST), np.float32)

    def put(name, a):
        at, w = CCOLS[name]
        c[:a.shape[0], at:at + w] = a

    n, m = np.arange(P)[:, None], np.arange(P)[None, :]
    put("iota", np.tile(np.arange(L, dtype=np.float32), (P, 1)))
    put("inchunk", np.tile((np.arange(L) % CH > 0).astype(np.float32), (P, 1)))
    put("round", np.full((P, 1), ROUND))
    put("ones", np.ones((P, P)))
    put("hones", (n // 64 == m // 64).astype(np.float32))
    put("ident", np.eye(P))
    s, t = n % CH, m % CH
    put("maskg", np.where(m < CH, s < t, s <= t).astype(np.float32))
    n, m = np.arange(CH)[:, None], np.arange(CH)[None, :]
    put("mdiag", np.tile(((m < n) & (m // INV == n // INV)).astype(np.float32), (2, 1)))
    put("mdiagt", np.tile(((m > n) & (m // INV == n // INV)).astype(np.float32), (2, 1)))
    put("moff", np.tile((m // INV < n // INV).astype(np.float32), (2, 1)))
    put("eye64", np.tile(np.eye(CH), (2, 1)))
    d = _spans()
    count = (d >= 0).astype(int) * ((d <= 128).astype(int) + (d % 4 == 0) + (d % 16 == 0))
    put("lncount", np.where(count > 0, np.log(np.maximum(count, 1)), -1e30))
    put("halfpi", np.full((P, 1), math.pi / 2))
    put("eps", np.full((P, 1), EPS))
    put("gneps", np.full((P, 1), GN_EPS))
    return c


def _layout(a):
    f = {k: np.asarray(v) for k, v in a.items()}
    arrays = {}
    arrays["wmain"] = _stream(f["w_in"][0], f["w_out_a"][0], f["w_glu"][0], f["w_out_b"][0], f["w_o"][0],
                              f["w_in_2"][0], f["w_out_2"][0], f["w_gate_up_2"][0])
    arrays["wdown"] = np.stack([_columns(f["w_down_2"][0], slice(j * P, j * P + P)) for j in range(KB)])
    arrays["xt"] = np.ascontiguousarray(f["x"][0].T.reshape(KB, P, L).transpose(1, 0, 2))
    bst = np.zeros((SB, P, TPB, 2, P), np.float32)
    cs = np.zeros((P, 2, STATE_TILES, 32), np.float32)
    for r, (b, c) in enumerate(((f["b_re"][0], f["c_re"][0]), (f["b_im"][0], f["c_im"][0]))):
        for g in range(64):
            j, t, h = g // 8, g % 8 // 2, g % 2
            bst[j, (g % 8) * 16:(g % 8) * 16 + 16, t, r, h * 64:h * 64 + 64] = b[g].T
            cs[h * 64:h * 64 + 64, r, g // 2, h * 16:h * 16 + 16] = c[g].T
    arrays["bst"] = bst.reshape(SB, P, TPB * 2 * P)
    arrays["cs"] = cs
    par = np.zeros((P, NPAR), np.float32)

    def put(name, v):
        at, w = PCOLS[name]
        par[:, at:at + w] = _rows(v)

    put("norm_g", f["norm_g"][0])
    for k in range(3):
        put(f"conv{k}", f["conv_w"][0, k])
    put("final_g", f["final_g"])
    put("norm1", f["norm1_g_2"][0])
    put("norm2", f["norm2_g_2"][0])
    put("final2", f["final_g_2"])
    put("b_glu", f["b_glu"][0])
    put("d_skip", f["d_skip"][0])
    mixv = f["rwkv_shift_mix_2"][0]
    put("mix_rkv", mixv[:3072])
    put("mix_lo", np.concatenate([mixv[3072:], np.zeros(96, np.float32)]))
    for name, key in [("w0", "rwkv_w0_2"), ("a0", "rwkv_a0_2"), ("k_k", "rwkv_k_k_2"), ("k_a", "rwkv_k_a_2"),
                      ("r_k", "rwkv_r_k_2"), ("ln_w", "rwkv_ln_w_2"), ("ln_b", "rwkv_ln_b_2"),
                      ("a_re", "a_re"), ("a_im", "a_im")]:
        put(name, f[key][0])
    put("log_dt", np.repeat(f["log_dt"][0], 64))
    arrays["par"] = par
    arrays["consts"] = _constants()
    arrays["lora"] = np.concatenate([f["rwkv_w_up_2"][0], f["rwkv_a_up_2"][0]], axis=0)
    gup = np.zeros((P, 2, 1024), np.float32)
    gup[:, 0] = f["rwkv_g_up_2"][0][:P]
    gup[:32, 1] = f["rwkv_g_up_2"][0][P:]
    arrays["gup"] = gup
    which = np.vectorize(_bucket)(np.maximum(_spans(), 0))
    table = f["rel_bias_table_2"]
    bias = table[which]
    arrays["bias"] = np.ascontiguousarray(bias.reshape(P, 384, PAIRS, 2).transpose(2, 0, 3, 1)).reshape(PAIRS, P, 768)
    return arrays


_ORDER = ["wmain", "wdown", "bst", "cs", "par", "consts", "xt", "lora", "gup", "bias"]


def kernel(**inputs):
    import concourse.bacc as _bacc
    from concourse.bass_utils import run_bass_kernel_spmd as _run

    arrays = _layout(inputs)
    nc = _bacc.Bacc("TRN2", target_bir_lowering=False, num_devices=1)
    args = [nc.dram_tensor(n, arrays[n].shape, F32, kind="ExternalInput").ap() for n in _ORDER]
    out = nc.dram_tensor("out", (P, KB, L), F32, kind="ExternalOutput").ap()
    hybrid_kernel(nc, *args, out)
    r = _run(nc, [arrays], core_ids=[0])
    return r.results[0]["out"].transpose(2, 1, 0).reshape(1, L, D)
```

```python
import math
from contextlib import ExitStack

import numpy as np

import concourse.bass as bass
from concourse import mybir

F32 = mybir.dt.float32
F32R = mybir.dt.float32r
ALU = mybir.AluOpType
ACT = mybir.ActivationFunctionType
AX = mybir.AxisListType

P = 128
L = 256
D = 2048
KB = D // P
SSM = 1024
SB = SSM // P
STATE_TILES = 64 * 64 // P
TPB = STATE_TILES // SB
EPS = 1e-6
FFN = 5632
FB = FFN // P
HEADS = 16
PAIRS = HEADS // 2
CH = 64
NCH = L // CH
INV = 16
DECAY_SCALE = math.exp(-0.5)
GN_EPS = 64e-5
ATTN_SCALE = 64 ** -0.5
ROUND = 1.5 * 2.0 ** 23
TWO_PI = 2 * math.pi
SIN_SCALE = 6.283185
PI_A = 6.28125
PI_B = 0.0019350051879882812
PI_C = TWO_PI - PI_A - PI_B

U = 1024
RING = 4

STREAM = [("u", 8, 2), ("zb", 8, 2), ("conv", 64, 2), ("gb", 16, 2), ("gaa", 32, 2), ("glu", 8, 1),
          ("outb", 16, 1), ("wo", 16, 2), ("lora", 3, 2), ("rkv", 24, 2), ("qkv", 24, 2),
          ("wout", 16, 2), ("ffn", 88, 2), ("down", 16, 6)]
UNIT0, BLOCK0 = {}, {}
_u = _b = 0
for _n, _blk, _per in STREAM:
    UNIT0[_n], BLOCK0[_n] = _u, _b
    _u += _blk * _per
    _b += _blk
UNITS_MAIN = UNIT0["down"]
UNITS = _u

PCOLS = {}
_c = 0
for _n, _w in [("norm_g", 16), ("conv0", 16), ("conv1", 16), ("conv2", 16), ("final_g", 16),
               ("norm1", 16), ("norm2", 16), ("final2", 16), ("b_glu", 8), ("d_skip", 8),
               ("mix_rkv", 24), ("mix_lo", 3), ("w0", 8), ("a0", 8), ("k_k", 8), ("k_a", 8),
               ("r_k", 8), ("ln_w", 8), ("ln_b", 8), ("a_re", 32), ("a_im", 32), ("log_dt", 32)]:
    PCOLS[_n] = (_c, _w)
    _c += _w
NPAR = _c

CCOLS = {}
_c = 0
for _n, _w in [("iota", 256), ("inchunk", 256), ("ones", 128), ("hones", 128), ("ident", 128), ("maskg", 128),
               ("mdiag", 64), ("mdiagt", 64), ("moff", 64), ("eye64", 64), ("lncount", 384), ("halfpi", 1), ("eps", 1),
               ("gneps", 1), ("round", 1)]:
    CCOLS[_n] = (_c, _w)
    _c += _w
NCONST = _c


class At:

    def __init__(self, c, m=0, i=None):
        self.c, self.m, self.i = c, m, i

    def __add__(self, k):
        return At(self.c + k, self.m, self.i)

    def v(self, k=0):
        return self.c + k if self.i is None else self.i * self.m + (self.c + k)

    def turns(self, ring, k=0):
        assert self.m % ring == 0
        n = self.c // ring + k
        return n if self.i is None else self.i * (self.m // ring) + n


class Links:

    def __init__(self, eng, sem):
        self.eng, self.sem, self.base, self.k, self.per, self.i = eng, sem, 0, 0, 0, None

    def __call__(self, ins):
        self.k += 1
        ins.then_inc(self.sem, 1)
        self.wait()

    def wait(self):
        n = self.base + self.k
        self.eng.wait_ge(self.sem, n if self.i is None else self.i * self.per + n)

    def loop(self, i, per, start=0):
        self.turned = self.base + self.k
        self.base, self.k, self.i, self.per = self.turned - per * start, 0, i, per

    def done(self, turns):
        assert self.k == self.per, f"the loop's body has {self.k} links"
        self.base, self.k, self.i = self.turned + self.per * turns, 0, None


def hybrid_kernel(nc, wmain, wdown, bst_dram, cst_dram, par_dram, const_dram, x_dram, lora_dram,
                  gup_dram, bias_dram, out_dram):
    ctx = ExitStack()
    with ctx:
        base = -(-nc.sbuf_base // 64) * 64
        ctx.enter_context(nc.sbuf_tensor("arena", [P, nc.sbuf_usable_end // 4 - base // 4 - 32], F32))
        K = 1024

        def at(name, offset, shape, dtype=F32):
            return nc.alloc_sbuf_tensor_at(name, [P, *shape], dtype, offset=base + offset)

        def sem(name):
            return ctx.enter_context(nc.semaphore(name))

        raw = at("w_raw", 0, [RING, U])
        whi = at("w_hi", 16 * K, [RING, U], F32R)
        wlo = at("w_lo", 32 * K, [RING, U], F32R)
        x = at("x_res", 48 * K, [KB, L])
        par = at("par", 64 * K, [NPAR])
        const = at("const", 66 * K, [NCONST])
        small = 73 * K
        rstd = at("rstd", small, [L])
        rstd2 = at("rstd2", small + 1 * K, [L])
        acc = at("acc", small + 2 * K, [2, L])
        tz = at("tz", small + 4 * K, [2, L])
        gt = at("gt", small + 6 * K, [2, L])
        f = at("f_val", small + 8 * K, [2, L])
        tmp = at("tmp", small + 10 * K, [2, L])
        sq = at("sq", small + 12 * K, [2, L])
        gg = at("gg", small + 14 * K, [KB])
        phi = at("phi", small + 14 * K + 64, [STATE_TILES])
        rho = at("rho", small + 14 * K + 192, [STATE_TILES])
        work = small + 14 * K + 320

        def wk(name, kb, shape, dtype=F32):
            assert base + work + kb * K + 4 * int(np.prod(shape)) <= nc.sbuf_usable_end, name
            return at(name, work + int(kb * K), shape, dtype)

        xh, xl = wk("xh", 0, [KB, L], F32R), wk("xl", 16, [KB, L], F32R)
        yah, yal = wk("yah", 32, [KB, L], F32R), wk("yal", 48, [KB, L], F32R)
        szb = wk("silu_zb", 64, [SB, L])
        ug = wk("u_then_gelu", 72, [SB, L])
        sgb = wk("sig_gb", 80, [KB, L])
        mix = wk("mixed", 96, [KB, L])
        sqx = wk("sqx", 96, [KB, L])
        convv = sq[:, 0, :]
        convc = wk("conv_cgv", 119, [L + 2])
        cosi = wk("cos_t", 80, [TPB, L])
        sini = wk("sin_t", 84, [TPB, L])
        turn = wk("turns", 88, [TPB, L])
        frac = wk("turn_frac", 92, [TPB, L])
        bstage = wk("b_stage", 96, [TPB, 2, P])
        m1, m2 = wk("m1", 100, [2, L]), wk("m2", 102, [2, L])
        gs = [wk("g_scan", 104, [2, L]), acc]
        o1, o2 = turn[:, 0:2, :], turn[:, 2:4, :]
        hs = wk("h_state", 106, [2, 2, L])
        cstage = wk("c_stage", 110, [TPB, 2, 32])
        cp = wk("c_prime", 111, [SB, TPB, 2, 32])
        craw = wk("c_raw", 32, [2, STATE_TILES, 32])
        cw = wk("c_work", 40, [2, STATE_TILES, 32])
        sv = {n: wk("s_" + n, 48 + i / 8, [STATE_TILES]) for i, n in enumerate(
            ["dt", "theta", "kk", "t0", "t1", "t2", "abs", "sin", "cos", "er", "den", "lr", "li",
             "kre", "kim", "den2"])}
        ybh, ybl = wk("ybh", 32, [SB, L], F32R), wk("ybl", 40, [SB, L], F32R)
        yoh, yol = wk("yoh", 48, [SB, L], F32R), wk("yol", 56, [SB, L], F32R)
        mh, ml = wk("mh", 0, [KB, L], F32R), wk("ml", 16, [KB, L], F32R)
        nh, nl = wk("nh", 32, [KB, L], F32R), wk("nl", 48, [KB, L], F32R)

        lora = wk("lora_up", 88, [1024])
        zs = wk("z_shift", 92, [L + 2])
        lo = wk("lora_lo", 94, [L])
        sgl = sq
        zr = wk("rkv", 64, [24, L])
        qkv = wk("qkv", 88, [24, L])
        aa = wk("a_gate", 0, [8, L])
        sw = wk("sig_w", 8, [8, L])
        abr = wk("ar_hat", 16, [2, 8, L])
        ba, br = abr[:, 0, :, :], abr[:, 1, :, :]
        bb = wk("b_hat", 112, [8, L])
        rr, kr, vr = zr[:, 0:8, :], zr[:, 8:16, :], zr[:, 16:24, :]
        pc = at("chunk_decay", small + 8 * K + 256, [8, NCH])
        gup = wk("g_up", 0, [2, 1024])
        bkc = wk("bk_chunk", 4, [8, 2, CH])
        ga, gr, grn = (wk(n, o, [2, 8, CH]) for n, o in (("g_a", 88), ("g_r", 92), ("g_r_next", 0)))
        st = wk("stack", 100, [8, 2, CH])
        bkt = wk("bk_tokens", 104, [8, P])
        mat = {n: wk("m_" + n, o, [8, CH]) for n, o in [
            ("n", 108), ("f", 110), ("nt", 40), ("w", 42), ("n2", 44), ("n2t", 46), ("n4", 56),
            ("n4t", 58), ("md", 60)]}
        xv = at("x_chunk", small + 6 * K, [8, CH])
        state = wk("state", 62, [8, CH])
        gnt = wk("gn_tmp", 104, [8, L])
        gsb = wk("out_gate", 96, [8, L])
        vt = wk("v_tok", 62, [2, 2, P])
        pt = wk("p_t", 40, [2, 2, 384])
        biasb = at("bias", small + 2 * K, [2, 2, 384])
        eb = wk("e_val", 56, [2, 2, 384])
        mxs = at("row_max", small + 8 * K, [2, 2, 2, 4])
        x3h, x3l = wk("x3h", 0, [KB, L], F32R), wk("x3l", 16, [KB, L], F32R)
        mxh, mxl = wk("mxh", 32, [KB, L], F32R), wk("mxl", 48, [KB, L], F32R)
        ah, al = wk("act_h", 32, [FB, L], F32R), wk("act_l", 76, [FB, L], F32R)

        main = ctx.enter_context(nc.psum_tensor("ps_main", [P, 4, 512], F32))
        aux = ctx.enter_context(nc.psum_tensor("ps_aux", [P, 4, 512], F32))

        def par_c(name, j):
            c, w = PCOLS[name]
            if isinstance(j, int):
                return par[:, c + j:c + j + 1]
            return par[:, bass.ds(j + c, 1)]

        def cst(name):
            c, w = CCOLS[name]
            return const[:, c:c + w]

        w_loaded = [sem(f"w_loaded{s}") for s in range(RING)]
        hi_ready, lo_ready, unit_used = sem("hi_ready"), sem("lo_ready"), sem("unit_used")
        bank_free = [sem(f"bank_free{b}") for b in range(4)]
        x_loaded = [sem(f"x_loaded{c}") for c in range(4)]
        par_loaded, const_loaded, c_loaded = sem("par_loaded"), sem("const_loaded"), sem("c_loaded")
        dve_link, act_link, pool_link = sem("dve_link"), sem("act_link"), sem("pool_link")
        xsq_ready, acc_ready, ssq_ready, root_ready = sem("xsq_ready"), sem("acc_ready"), sem("ssq_ready"), sem("root_ready")
        in_ready = sem("in_ready")
        rstd_ready = sem("rstd_ready")
        gate_out = sem("gate_out")
        s_act, s_dve = sem("scan_par_act"), sem("scan_par_dve")
        scan_const = sem("scan_const")
        b_loaded, c_staged, frac_ready, trig_ready = sem("b_loaded"), sem("c_staged"), sem("frac_ready"), sem("trig_ready")
        bu_ready, bu_used, h_ready, h_used, y_used = sem("bu_ready"), sem("bu_used"), sem("h_ready"), sem("h_used"), sem("y_used")
        gs_ready = sem("gs_ready")
        ya_ready, gelu_ready, yb_ready, glu_out, yo_ready, m_ready = (
            sem("ya_ready"), sem("gelu_ready"), sem("yb_ready"), sem("glu_out"), sem("yo_ready"), sem("m_ready"))
        res_ready, sq_ready = sem("res_ready"), sem("sq_ready")
        out_stored = sem("out_stored")
        norm_sum, norm_root, ms_ready = sem("norm_sum"), sem("norm_root"), sem("ms_ready")
        lora_loaded, gup_loaded, res_scaled = sem("lora_loaded"), sem("gup_loaded"), sem("res_scaled")
        lo_shifted, lo_act, up_mm, up_act = sem("lo_shifted"), sem("lo_act"), sem("up_mm"), sem("up_act")
        prep_dve, prep_act, head_mm = sem("prep_dve"), sem("prep_act"), sem("head_mm")
        staged, core_mm, core_act, core_dve = sem("staged"), sem("core_mm"), sem("core_act"), sem("core_dve")
        core_pre, core_start = sem("core_pre"), sem("core_start")
        fin_mm, fin_act, fin_dve, gu_mm = sem("fin_mm"), sem("fin_act"), sem("fin_dve"), sem("gu_mm")
        gate_sb = sem("gate_sb")
        bias_loaded = [sem("bias_loaded0"), sem("bias_loaded1")]
        bias_ready, sc_mm, vt_mm, vt_sb, e_ready, max_ready, p_ready, pn_ready, pt_mm, pt_sb, o_mm, att_ready = (
            sem(n) for n in ("bias_ready", "sc_mm", "vt_mm", "vt_sb", "e_ready", "max_ready", "p_ready",
                             "pn_ready", "pt_mm", "pt_sb", "o_mm", "att_ready"))
        rwkv_ready, act_ready = sem("rwkv_ready"), sem("act_ready")
        out_ready = sem("out_ready")

        def down_width(u):
            return U if u < 5 else U // 2

        def hrow(h):
            return slice(64 * h, 64 * h + 64)

        PREP_DVE = 11
        GO = 1
        SCAN_BU, SCAN_IN, SCAN_Y = (0, 0, 3, 3), (0, 1, 3, 4), (3, 4, 6, 7)
        MM = {n: k + 1 for k, n in enumerate(
            ["n2", "n2t", "vt", "n4", "n4t", "w2", "n8", "w4", "bkt", "w8", "x", "qt", "q", "md", "q2", "g0", "g1",
             "g2", "mt", "n", "sa", "y", "s"])}
        DV = {n: k + 1 for k, n in enumerate(
            ["n2t", "n4t", "w2", "w4", "w8", "qt", "t1", "gm0", "g1", "gm1", "sa", "nf", "w1", "y", "s", "gr"])}
        AC = {n: k + 1 for k, n in enumerate(["n2", "vt", "n4", "n8", "bkt", "x", "q", "md", "q2", "mt"])}
        MM_NEXT, DV_NEXT = ("g0", "g2", "n", "s"), ("gm0", "gm1", "nf", "w1", "s", "gr")

        def steps(names, left_out, name, last):
            order = list(names)
            k, n = order.index(name), 1
            while last and k - n >= 0 and order[k - n] in left_out:
                n += 1
            return n

        block = ctx.enter_context(nc.Block())

        @block.sync
        def _(sp):
            for s in range(RING):
                sp.dma_start(raw[:, s, :], wmain[s]).then_inc(w_loaded[s], 16)
            with sp.Fori(1, UNITS_MAIN // RING) as i:
                for s in range(RING):
                    sp.wait_ge(lo_ready, i * RING + (s - RING + 1))
                    sp.dma_start(raw[:, s, :], wmain[bass.ds(i * RING + s, 1)].rearrange("a p n -> p (a n)"))\
                      .then_inc(w_loaded[s], 16)
            for n in range(UNITS_MAIN // RING * RING, UNITS_MAIN):
                sp.wait_ge(lo_ready, n - RING + 1)
                sp.dma_start(raw[:, n % RING, :], wmain[n]).then_inc(w_loaded[n % RING], 16)
            with sp.Fori(0, KB // 4) as i:
                for b in range(4):
                    for u in range(6):
                        n = At(UNITS_MAIN + 6 * b + u, 24, i)
                        w = down_width(u)
                        sp.wait_ge(lo_ready, n.v(1 - RING))
                        sp.dma_start(raw[:, n.c % RING, 0:w],
                                     wdown[bass.ds(i * 4 + b, 1), :, u * U:u * U + w].rearrange("a p n -> p (a n)"))\
                          .then_inc(w_loaded[n.c % RING], 16)
            for c in range(4):
                sp.wait_ge(out_ready, c + 1)
                sp.dma_start(out_dram[:, 4 * c:4 * c + 4, :], x[:, 4 * c:4 * c + 4, :]).then_inc(out_stored, 16)
            sp.wait_ge(out_stored, 64)

        @block.gpsimd
        def _(pool):
            link = Links(pool, pool_link)
            pool.sem_inc(h_ready, GO)
            pool.wait_ge(const_loaded, 16)
            pool.wait_ge(scan_const, 3)

            def scan_angles(i):
                c, _ = CCOLS["iota"]
                ph = phi[:, bass.ds(i * TPB, TPB)] if not isinstance(i, int) else phi[:, i * TPB:(i + 1) * TPB]
                link(nc.gpsimd.tensor_tensor(turn[:, :, :], const[:, c:c + L].unsqueeze(1).to_broadcast([P, TPB, L]),
                                             ph.unsqueeze(2).to_broadcast([P, TPB, L]), ALU.mult))
                rnd = cst("round").unsqueeze(1).to_broadcast([P, TPB, L])
                link(nc.gpsimd.tensor_tensor(frac[:, :, :], turn[:, :, :], rnd, ALU.add))
                link(nc.gpsimd.tensor_tensor(frac[:, :, :], frac[:, :, :], rnd, ALU.subtract))
                nc.gpsimd.tensor_tensor(frac[:, :, :], turn[:, :, :], frac[:, :, :], ALU.subtract).then_inc(frac_ready, 1)

            def scan_b(i):
                src = bst_dram[0] if isinstance(i, int) else bst_dram[bass.ds(i, 1)].rearrange("a p n -> p (a n)")
                pool.dma_start(bstage[:, :, :, :], src).then_inc(b_loaded, 16)

            def scan_c(i):
                src = cp[:, 0, :, :, :].rearrange("p a b c -> p (a b c)") if isinstance(i, int) else (
                    cp[:, bass.ds(i, 1), :, :, :].rearrange("p z a b c -> p (z a b c)"))
                nc.gpsimd.tensor_copy(cstage[:, :, :, :].rearrange("p a b c -> p (a b c)"), src).then_inc(c_staged, 1)

            def scan_out(i, t):
                cb = cosi[:, t, :].unsqueeze(1).to_broadcast([P, 2, L])
                sb_ = sini[:, t, :].unsqueeze(1).to_broadcast([P, 2, L])
                pool.wait_ge(gs_ready, i * TPB + (t + 1))
                pool.wait_ge(h_ready, i * TPB + t + GO)
                nc.gpsimd.tensor_tensor(o1, gs[t % 2][:, :, :], cb, ALU.mult)
                link(nc.gpsimd.tensor_tensor(o2, gs[t % 2][:, :, :], sb_, ALU.mult))
                pool.wait_ge(h_used, (i * TPB if t < 2 else i * TPB + (t - 1)) + GO)
                nc.gpsimd.tensor_tensor(hs[:, t % 2, 0, :], o1[:, 0, :], o2[:, 1, :], ALU.subtract)
                nc.gpsimd.tensor_tensor(hs[:, t % 2, 1, :], o1[:, 1, :], o2[:, 0, :], ALU.add).then_inc(h_ready, 1)

            def scan_block(i, last=False):
                scan_out(i, 0)
                scan_out(i, 1)
                if not last:
                    pool.wait_ge(h_ready, i * TPB + 2 + GO)
                    pool.wait_ge(trig_ready, i + 1)
                    scan_angles(i + 1)
                    pool.wait_ge(frac_ready, i + 2)
                scan_out(i, 2)
                scan_out(i, 3)
                if not last:
                    pool.wait_ge(bu_ready, i * TPB + TPB)
                    scan_b(i + 1)
                    pool.wait_ge(h_used, i * TPB + TPB + GO)
                    scan_c(i + 1)

            scan_b(0)
            scan_angles(0)
            pool.wait_ge(frac_ready, 1)
            scan_c(0)
            with pool.Fori(0, SB - 1) as i:
                link.loop(i, 7)
                scan_block(i)
            link.done(SB - 1)
            scan_block(SB - 1, True)

            pool.wait_ge(m_ready, KB)
            pool.dma_start(lora[:, :], lora_dram).then_inc(lora_loaded, 16)
            pool.wait_ge(rstd_ready, 2)
            pool.wait_ge(sq_ready, KB)
            pool.wait_ge(in_ready, 2 * KB)
            c, _ = PCOLS["final_g"]
            link(nc.gpsimd.tensor_tensor(x[:, :, :], x[:, :, :], rstd2[:, :].unsqueeze(1).to_broadcast([P, KB, L]), ALU.mult))
            nc.gpsimd.tensor_tensor(x[:, :, :], x[:, :, :], par[:, c:c + KB].unsqueeze(2).to_broadcast([P, KB, L]),
                                    ALU.mult).then_inc(res_scaled, 1)

            def load_bias(s, src):
                pool.dma_start(biasb[:, s, :, :].rearrange("p h n -> p (h n)"), src).then_inc(bias_loaded[s], 16)

            def add_count(i, s):
                pool.wait_ge(bias_loaded[s], i * 16 + 16)
                nc.gpsimd.tensor_tensor(biasb[:, s, :, :], biasb[:, s, :, :],
                                        cst("lncount").unsqueeze(1).to_broadcast([P, 2, 384]), ALU.add)\
                    .then_inc(bias_ready, 1)

            pool.wait_ge(prep_dve, 1)
            for s in range(2):
                load_bias(s, bias_dram[s])
            for s in range(2):
                add_count(0, s)
            with pool.Fori(1, PAIRS // 2) as i:
                for s in range(2):
                    pool.wait_ge(e_ready, i * 4 + (2 * s - 2 + GO))
                    load_bias(s, bias_dram[bass.ds(i * 2 + s, 1)].rearrange("a p n -> p (a n)"))
                    add_count(i, s)

            pool.wait_ge(core_mm, (NCH - 1) * len(MM) + MM["bkt"] + GO)
            pool.wait_ge(core_dve, (NCH - 1) * len(DV))
            pool.dma_start(gup[:, :, :].rearrange("p a n -> p (a n)"), gup_dram.rearrange("p a n -> p (a n)"))\
                .then_inc(gup_loaded, 16)
            pool.wait_ge(gup_loaded, 16)

        @block.scalar
        def _(act):
            def split_hi(n, width=U):
                s = n.c % RING
                act.wait_ge(w_loaded[s], n.turns(RING, 1) * 16)
                if n.i is not None or n.c >= RING:
                    act.wait_ge(unit_used, n.v(1 - RING))
                nc.scalar.activation(whi[:, s, 0:width], raw[:, s, 0:width], ACT.Copy).then_inc(hi_ready, 1)

            def gate(func, out, k, g, bias=0.0):
                act.wait_ge(bank_free[g.c % 4], g.turns(4, 1))
                nc.scalar.activation(out, tz[:, k.c % 2, :], func, bias=bias).then_inc(gate_out, 1)

            act.sem_inc(pt_sb, GO)
            act.dma_start(par[:, :], par_dram).then_inc(par_loaded, 16)
            for c in range(4):
                act.dma_start(x[:, 4 * c:4 * c + 4, :], x_dram[:, 4 * c:4 * c + 4, :]).then_inc(x_loaded[c], 16)
            act.dma_start(const[:, :], const_dram).then_inc(const_loaded, 16)
            act.dma_start(craw[:, :, :, :], cst_dram).then_inc(c_loaded, 16)
            for s in range(3):
                split_hi(At(s))
            for c in range(4):
                act.wait_ge(x_loaded[c], 16)
                ins = nc.scalar.activation(sqx[:, 4 * c:4 * c + 4, :], x[:, 4 * c:4 * c + 4, :], ACT.Square)
            ins.then_inc(xsq_ready, 1)

            act.wait_ge(par_loaded, 16)
            c, w = PCOLS["log_dt"]
            nc.scalar.activation(sv["dt"][:, :], par[:, c:c + w], ACT.Exp).then_inc(s_act, 1)

            n0 = UNIT0["u"]
            for b in range(8):
                split_hi(At(n0 + 2 * b + 3))
                split_hi(At(n0 + 2 * b + 4))
                if b == 1:
                    act.wait_ge(const_loaded, 16)
                    act.wait_ge(ssq_ready, 1)
                    nc.scalar.activation(tmp[:, 0, :], aux[:, 3, 0:L], ACT.Sqrt, bias=cst("eps"), scale=1.0 / D)\
                        .then_inc(root_ready, 1)
                    act.wait_ge(s_dve, 1)
                    nc.scalar.activation(rho[:, :], sv["er"][:, :], ACT.Exp).then_inc(s_act, 1)
                if b == 2:
                    act.wait_ge(s_dve, 2)
                    nc.scalar.activation(sv["sin"][:, :], phi[:, :], ACT.Sin, scale=SIN_SCALE).then_inc(s_act, 1)
                    nc.scalar.activation(sv["abs"][:, :], phi[:, :], ACT.Abs).then_inc(act_link, 1)
                    act.wait_ge(act_link, 1)
                    nc.scalar.activation(sv["cos"][:, :], sv["abs"][:, :], ACT.Sin, scale=-SIN_SCALE,
                                         bias=cst("halfpi")).then_inc(s_act, 1)
            links = Links(act, act_link)
            links.base = 1
            n0 = UNIT0["zb"]
            for b in range(8):
                split_hi(At(n0 + 2 * b + 3))
                split_hi(At(n0 + 2 * b + 4))
                gate(ACT.Silu, szb[:, b, :], At(b), At(BLOCK0["zb"] + b))

            def trig(i):
                act.wait_ge(frac_ready, i + 1)
                act.wait_ge(h_ready, i * TPB + GO)
                nc.scalar.activation(sini[:, :, :], frac[:, :, :], ACT.Sin, scale=SIN_SCALE)
                links(nc.scalar.activation(cosi[:, :, :], frac[:, :, :], ACT.Abs))
                nc.scalar.activation(cosi[:, :, :], cosi[:, :, :], ACT.Sin, scale=-SIN_SCALE,
                                     bias=cst("halfpi")).then_inc(trig_ready, 1)

            n0 = UNIT0["conv"]

            def conv(i, last=False):
                for b in range(8):
                    split_hi(At(n0 + 2 * b + 3, 16, i))
                    split_hi(At(n0 + 2 * b + 4, 16, i))
                    if b % 4 == 0:
                        gate(ACT.Silu, gt[:, (b // 4) % 2, :], At(8 + b // 4, 2, i), At(BLOCK0["conv"] + b, 8, i))
                    if b == 6 and not last:
                        trig(i + 1)

            trig(0)
            with act.Fori(0, SB - 1) as i:
                links.loop(i, 1)
                conv(i)
            links.done(SB - 1)
            conv(SB - 1, True)
            act.wait_ge(y_used, SB + GO)
            nc.scalar.activation(ug[:, :, :], ug[:, :, :], ACT.Gelu_apprx_tanh).then_inc(gelu_ready, 1)

            n0 = UNIT0["gb"]
            with act.Fori(0, 4) as i:
                for b in range(4):
                    split_hi(At(n0 + 2 * b + 3, 8, i))
                    split_hi(At(n0 + 2 * b + 4, 8, i))
                    gate(ACT.Sigmoid, sgb[:, bass.ds(i * 4 + b, 1), :].rearrange("p a n -> p (a n)"), At(24 + b, 4, i),
                         At(BLOCK0["gb"] + b, 4, i))
            n0 = UNIT0["gaa"]
            with act.Fori(0, 8) as i:
                for b in range(4):
                    split_hi(At(n0 + 2 * b + 3, 8, i))
                    split_hi(At(n0 + 2 * b + 4, 8, i))
                    if b % 2 == 0:
                        gate(ACT.Sigmoid, gt[:, b // 2, :], At(40 + b // 2, 2, i), At(BLOCK0["gaa"] + b, 4, i))
            n0, g0 = UNIT0["glu"], BLOCK0["glu"]
            for b in range(8):
                split_hi(At(n0 + b + 3))
                act.wait_ge(unit_used, n0 + b + 1)
                if b >= 2:
                    act.wait_ge(yo_ready, b - 1)
                nc.scalar.activation(gt[:, b % 2, :], main[:, (g0 + b) % 4, 0:L], ACT.Sigmoid,
                                     bias=par_c("b_glu", b)).then_inc(glu_out, 1)
            n0 = UNIT0["outb"]
            with act.Fori(0, 4) as i:
                for b in range(4):
                    split_hi(At(n0 + b + 3, 4, i))
            n0 = UNIT0["wo"]
            with act.Fori(0, 4) as i:
                for b in range(4):
                    split_hi(At(n0 + 2 * b + 3, 8, i))
                    split_hi(At(n0 + 2 * b + 4, 8, i))
                    j = i * 4 + b
                    xj = x[:, bass.ds(j, 1), :].rearrange("p a n -> p (a n)")
                    act.wait_ge(res_ready, i * 4 + b + 1)
                    nc.scalar.activation(sq[:, 0, :], xj, ACT.Square)
                    nc.scalar.activation(sq[:, 1, :], xj, ACT.Square, scale=par_c("final_g", j)).then_inc(sq_ready, 1)

            def root(src, dst, scale, eps="eps"):
                nc.scalar.activation(dst, src, ACT.Sqrt, bias=cst(eps), scale=scale).then_inc(norm_root, 1)

            n0 = UNIT0["lora"]
            for b in range(3):
                split_hi(At(n0 + 2 * b + 3))
                split_hi(At(n0 + 2 * b + 4))
                if b == 0:
                    act.wait_ge(norm_sum, 1)
                    root(aux[:, 3, 0:L], tmp[:, 0, :], 1.0 / D)
                    act.wait_ge(ms_ready, 1)
                    root(tmp[:, 1, :], tmp[:, 0, :], 1.0 / D)
                act.wait_ge(lo_shifted, b + 1)
                if b == 0:
                    nc.scalar.activation(lo[0:64, :], lo[0:64, :], ACT.Tanh).then_inc(lo_act, 1)
                else:
                    nc.scalar.activation(sgl[:, b - 1, :], f[:, b - 1, :], ACT.Sigmoid).then_inc(lo_act, 1)
            for j in range(8):
                act.wait_ge(up_mm, j + 1)
                nc.scalar.activation(sw[:, j, :], aux[:, j % 2, 0:L], ACT.Sigmoid, bias=par_c("w0", j))
                nc.scalar.activation(aa[:, j, :], aux[:, 2 + j % 2, 0:L], ACT.Sigmoid, bias=par_c("a0", j))\
                    .then_inc(up_act, 1)
            n0 = UNIT0["rkv"]
            with act.Fori(0, 6) as i:
                for b in range(4):
                    split_hi(At(n0 + 2 * b + 3, 8, i))
                    split_hi(At(n0 + 2 * b + 4, 8, i))

            def aux_all(lo_, hi_):
                return aux[:, lo_:hi_, :].rearrange("p b n -> p (b n)").rearrange("p (j n) -> p j n", n=L)

            n0 = UNIT0["qkv"]
            for b in range(24):
                split_hi(At(n0 + 2 * b + 3))
                split_hi(At(n0 + 2 * b + 4))
                if b == 1:
                    act.wait_ge(prep_dve, 1)
                    nc.scalar.activation(ba[:, :, :], bb[:, :, :], ACT.Square).then_inc(prep_act, 1)
                if b == 5:
                    act.wait_ge(head_mm, 1)
                    for c in range(4):
                        ins = nc.scalar.activation(br[:, 2 * c:2 * c + 2, :].rearrange("p j n -> p (j n)"),
                                                   aux[:, c, :], ACT.Sqrt)
                    ins.then_inc(prep_act, 1)
                if b == 15:
                    act.wait_ge(prep_dve, 6)
                    nc.scalar.activation(br[:, :, :], aa[:, :, :], ACT.Exp, scale=-DECAY_SCALE).then_inc(prep_act, 1)
                    act.wait_ge(prep_dve, 7)
                    nc.scalar.activation(sw[:, :, :], sw[:, :, :], ACT.Exp, scale=-DECAY_SCALE).then_inc(prep_act, 1)
                if b == 16:
                    act.wait_ge(prep_act, 4)
                    nc.scalar.activation(aa[:, :, :], aa[:, :, :], ACT.Exp, scale=DECAY_SCALE).then_inc(prep_act, 1)

            def exps(i, s):
                for h in range(2):
                    act.wait_ge(max_ready, i * 4 + (2 * s + h + 1))
                    for q, w in enumerate((slice(0, P), slice(P, 384))):
                        ins = nc.scalar.activation(eb[:, s % 2, h, w], eb[:, s % 2, h, w], ACT.Exp,
                                                   bias=mxs[:, s % 2, h, q, 1:2], accum_out=mxs[:, s % 2, h, q, 2:3])
                    ins.then_inc(p_ready, 1)

            def values(i, s):
                act.wait_ge(vt_mm, i * 2 + (s + 1) + GO)
                nc.scalar.activation(vt[:, s % 2, :, :].rearrange("p b n -> p (b n)"), aux[:, 2 + s % 2, L:2 * L], ACT.Copy)\
                    .then_inc(vt_sb, 1)

            def probs(i, s):
                act.wait_ge(pt_mm, i * 2 + (s + 1))
                for h in range(2):
                    ins = nc.scalar.activation(pt[:, s % 2, h, :], aux[:, h, 0:384], ACT.Copy)
                ins.then_inc(pt_sb, 1)

            values(0, 0)
            exps(0, 0)
            exps(0, 1)
            probs(0, 0)
            values(0, 1)
            with act.Fori(0, PAIRS // 2 - 1) as i:
                for s in (1, 2):
                    exps(i, s + 1)
                    probs(i, s)
                    values(i, s + 1)
            probs(0, PAIRS - 1)

            with act.Fori(0, NCH) as i:
                def copy(name, after, banks, dst):
                    act.wait_ge(core_mm, i * len(MM) + MM[after] + GO)
                    for h in range(2):
                        ins = nc.scalar.activation(dst[hrow(h), :, :].rearrange("p j n -> p (j n)"),
                                                   banks[h][hrow(h), :], ACT.Copy)
                    ins.then_inc(core_act, 1)

                b0, b2, a0, a2 = ([main[:, 0], main[:, 1]], [main[:, 2], main[:, 3]],
                                  [aux[:, 0], aux[:, 1]], [aux[:, 2], aux[:, 3]])
                copy("n2", "n2", a0, mat["n2"])
                act.wait_ge(core_mm, i * len(MM) + MM["vt"] + GO)
                for h in range(2):
                    ins = nc.scalar.activation(st[hrow(1 - h), :, h, :], aux[hrow(1 - h), 2 + h, :]
                                               .rearrange("p (j n) -> p j n", n=CH), ACT.Copy)
                ins.then_inc(core_act, 1)
                copy("n4", "n4", a0, mat["n4"])
                copy("n8", "n8", a0, mat["n2"])
                act.wait_ge(core_mm, i * len(MM) + MM["bkt"] + GO)
                nc.scalar.activation(bkt[:, 0:4, :].rearrange("p j n -> p (j n)"), aux[:, 2, :], ACT.Copy)
                nc.scalar.activation(bkt[:, 4:8, :].rearrange("p j n -> p (j n)"), aux[:, 3, :], ACT.Copy).then_inc(core_act, 1)
                copy("x", "x", a2, xv)
                copy("q", "q", a0, mat["n"])
                copy("md", "md", b2, mat["md"])
                copy("q2", "q2", b0, mat["n4"])
                copy("mt", "mt", b2, mat["n2"])

            def four(t, c):
                return t[:, 2 * c:2 * c + 2, :].rearrange("p j n -> p (j n)")

            for c in range(4):
                act.wait_ge(fin_dve, c + 1)
                nc.scalar.activation(four(gnt, c), four(vr, c), ACT.Square).then_inc(fin_act, 1)
            for c in range(4):
                act.wait_ge(fin_mm, 4 + c + 1)
                nc.scalar.activation(four(gnt, c), aux[:, c, :], ACT.Ln, bias=cst("gneps"), scale=1.0 / 64)\
                    .then_inc(fin_act, 1)
            for c in range(4):
                act.wait_ge(fin_act, 4 + c + 1)
                nc.scalar.activation(four(gnt, c), four(gnt, c), ACT.Exp, scale=-0.5).then_inc(fin_act, 1)
                act.wait_ge(gu_mm, 2 * c + 2)
                nc.scalar.activation(four(gsb, c), main[:, c, :], ACT.Copy).then_inc(gate_sb, 1)

            n0 = UNIT0["wout"]
            with act.Fori(0, 4) as i:
                for b in range(4):
                    split_hi(At(n0 + 2 * b + 3, 8, i))
                    split_hi(At(n0 + 2 * b + 4, 8, i))
                    j = i * 4 + b
                    act.wait_ge(res_ready, j + (KB + 1))
                    nc.scalar.activation(sq[:, 0, :], x[:, bass.ds(j, 1), :].rearrange("p a n -> p (a n)"), ACT.Square)\
                        .then_inc(sq_ready, 1)
            n0 = UNIT0["ffn"]

            def ffn(i):
                for b in range(4):
                    split_hi(At(n0 + 2 * b + 3, 8, i))
                    split_hi(At(n0 + 2 * b + 4, 8, i))
                    if b == 0 and i is None:
                        act.wait_ge(norm_sum, 2)
                        root(aux[:, 3, 0:L], tmp[:, 0, :], 1.0 / D)
                    if b % 2 == 0:
                        gate(ACT.Silu, gt[:, b // 2, :], At(56 + b // 2, 2, i), At(BLOCK0["ffn"] + b, 4, i))

            ffn(None)
            with act.Fori(1, FB // 2) as i:
                ffn(i)

            n0 = UNIT0["down"]

            def down(i, c=0, last=False):
                for b in range(4):
                    for u in range(6):
                        if not (last and 6 * b + u + 3 >= 24):
                            split_hi(At(n0 + 24 * c + 6 * b + u + 3, 24, i), down_width((u + 3) % 6))
                    j = c * 4 + b if i is None else i * 4 + b
                    act.wait_ge(res_ready, j + (2 * KB + 1))
                    xj = x[:, j, :] if i is None else x[:, bass.ds(j, 1), :].rearrange("p a n -> p (a n)")
                    nc.scalar.activation(sq[:, 0, :], xj, ACT.Square).then_inc(sq_ready, 1)

            with act.Fori(0, 3) as i:
                down(i)
            down(None, 3, True)
            act.wait_ge(norm_sum, 3)
            root(aux[:, 3, 0:L], tmp[:, 0, :], 1.0 / D)

        @block.vector
        def _(dve):
            V = nc.vector
            link = Links(dve, dve_link)
            for counted in (bu_used, y_used, e_ready, att_ready):
                dve.sem_inc(counted, GO)

            def split_lo(n, width=U):
                s = n.c % RING
                dve.wait_ge(hi_ready, n.v(1))
                V.tensor_tensor(wlo[:, s, 0:width], raw[:, s, 0:width], whi[:, s, 0:width].bitcast(F32), ALU.subtract)\
                    .then_inc(lo_ready, 1)

            def bank(g):
                return main[:, g.c % 4, 0:L]

            def evac(ins, g):
                return ins.then_inc(bank_free[g.c % 4], 1)

            def to_gate(g, k):
                if k.i is not None or k.c >= 2:
                    dve.wait_ge(gate_out, k.v(-1))
                dve.wait_ge(rstd_ready, 1)
                evac(V.tensor_tensor(tz[:, k.c % 2, :], bank(g), rstd[:, :], ALU.mult), g)

            def split_value(val, hi, lo, ready):
                link(V.tensor_copy(hi, val))
                V.tensor_tensor(lo, val, hi.bitcast(F32), ALU.subtract).then_inc(ready, 1)

            def blk(t, j):
                if isinstance(j, int):
                    return t[:, j, :]
                return t[:, bass.ds(j, 1), :].rearrange("p a n -> p (a n)")

            dve.wait_ge(par_loaded, 16)
            for half in range(2):
                split_lo(At(half))
                for j in range(8 * half, 8 * half + 8):
                    if j % 4 == 0:
                        dve.wait_ge(x_loaded[j // 4], 16)
                    link(V.tensor_scalar(xh[:, j, :], x[:, j, :], par_c("norm_g", j), None, ALU.mult))
                    V.scalar_tensor_tensor(xl[:, j, :], x[:, j, :], par_c("norm_g", j), xh[:, j, :].bitcast(F32),
                                           ALU.mult, ALU.subtract).then_inc(in_ready, 1)
            split_lo(At(2))
            def step(n, b):
                split_lo(At(n.c + 2 * b + 3, n.m, n.i))
                split_lo(At(n.c + 2 * b + 4, n.m, n.i))
                dve.wait_ge(unit_used, At(n.c + 2 * b + 2, n.m, n.i).v())

            def pv(name):
                c, w = PCOLS[name]
                return par[:, c:c + w]

            s = {n: t[:, :] for n, t in sv.items()}
            n0, g0 = At(UNIT0["u"]), BLOCK0["u"]
            for b in range(8):
                step(n0, b)
                if b == 0:
                    dve.wait_ge(xsq_ready, 1)
                    V.tensor_reduce(acc[:, 0, :], sqx[:, :, :].rearrange("p j t -> p t j"), AX.X, ALU.add)\
                        .then_inc(acc_ready, 1)
                    dve.wait_ge(s_act, 1)
                    V.tensor_tensor(s["er"], pv("a_re"), s["dt"], ALU.mult).then_inc(s_dve, 1)
                    link(V.tensor_tensor(s["theta"], pv("a_im"), s["dt"], ALU.mult))
                    link(V.tensor_scalar(s["kk"], s["theta"], 1.0 / TWO_PI, None, ALU.mult))
                    link(V.tensor_scalar(s["kk"], s["kk"], ROUND, ROUND, ALU.add, ALU.subtract))
                    link(V.scalar_tensor_tensor(s["t0"], s["kk"], -PI_A, s["theta"], ALU.mult, ALU.add))
                    link(V.scalar_tensor_tensor(s["t1"], s["kk"], -PI_B, s["t0"], ALU.mult, ALU.add))
                    link(V.scalar_tensor_tensor(s["t2"], s["kk"], -PI_C, s["t1"], ALU.mult, ALU.add))
                    link(V.tensor_scalar(s["t2"], s["t2"], 1.0 / TWO_PI, 0.5, ALU.mult, ALU.min))
                    V.tensor_scalar(phi[:, :], s["t2"], -0.5, None, ALU.max).then_inc(s_dve, 1)
                if b == 1:
                    dve.wait_ge(root_ready, 1)
                    link(V.reciprocal(rstd[:, :], tmp[:, 0, :]))
                    V.tensor_tensor(rstd2[:, :], rstd[:, :], rstd[:, :], ALU.mult).then_inc(rstd_ready, 1)
                for g in {0: (), 1: (0, 1)}.get(b, (b,)):
                    evac(V.tensor_tensor(ug[:, g, :], bank(At(g0 + g)), rstd[:, :], ALU.mult), At(g0 + g))
                if b == 3:
                    dve.wait_ge(s_act, 4)
                    link(V.tensor_tensor(s["t0"], rho[:, :], s["cos"], ALU.mult))
                    link(V.tensor_scalar(s["t0"], s["t0"], 1.0, None, ALU.subtract))
                    link(V.tensor_tensor(s["t1"], rho[:, :], s["sin"], ALU.mult))
                    link(V.tensor_tensor(s["den"], pv("a_re"), pv("a_re"), ALU.mult))
                    link(V.tensor_tensor(s["den2"], pv("a_im"), pv("a_im"), ALU.mult))
                    link(V.tensor_tensor(s["den"], s["den"], s["den2"], ALU.add))
                    link(V.reciprocal(s["den"], s["den"]))
                    link(V.tensor_tensor(s["lr"], pv("a_re"), s["den"], ALU.mult))
                    link(V.tensor_tensor(s["li"], pv("a_im"), s["den"], ALU.mult))
                if b == 3:
                    link(V.tensor_tensor(s["kre"], s["t0"], s["lr"], ALU.mult))
                    link(V.tensor_tensor(s["t2"], s["t1"], s["li"], ALU.mult))
                    link(V.tensor_tensor(s["kre"], s["kre"], s["t2"], ALU.add))
                    link(V.tensor_tensor(s["kim"], s["t1"], s["lr"], ALU.mult))
                    link(V.tensor_tensor(s["t2"], s["t0"], s["li"], ALU.mult))
                    link(V.tensor_tensor(s["kim"], s["kim"], s["t2"], ALU.subtract))
                if b in (4, 5):
                    dve.wait_ge(c_loaded, 16)
                    if b == 5:
                        dve.wait_ge(scan_const, 1)
                    ka, kb_ = ("kre", "kim") if b == 4 else ("kim", "kre")
                    kav = s[ka].unsqueeze(2).to_broadcast([P, STATE_TILES, 32])
                    kbv = s[kb_].unsqueeze(2).to_broadcast([P, STATE_TILES, 32])
                    link(V.tensor_tensor(cw[:, 0, :, :], craw[:, 0, :, :], kav, ALU.mult))
                    link(V.tensor_tensor(cw[:, 1, :, :], craw[:, 1, :, :], kbv, ALU.mult))
                    dst = cp[:, :, :, b - 4, :].rearrange("p a b c -> p (a b) c")
                    if b == 4:
                        V.tensor_tensor(dst, cw[:, 0, :, :], cw[:, 1, :, :], ALU.subtract).then_inc(scan_const, 1)
                    else:
                        link(V.tensor_tensor(cw[:, 0, :, :], cw[:, 0, :, :], cw[:, 1, :, :], ALU.add))
                        V.tensor_scalar(dst, cw[:, 0, :, :], -1.0, None, ALU.mult).then_inc(scan_const, 1)
                if b == 6:
                    V.memset(convc[:, 0:2], 0.0).then_inc(scan_const, 1)

            n0, g0 = At(UNIT0["zb"]), BLOCK0["zb"]
            for b in range(8):
                step(n0, b)
                to_gate(At(g0 + b), At(b))

            def scan_in(i, t):
                if t == 0:
                    dve.wait_ge(trig_ready, i + 1)
                dve.wait_ge(bu_ready, i * TPB + (t + 1))
                cb = cosi[:, t, :].unsqueeze(1).to_broadcast([P, 2, L])
                sb_ = sini[:, t, :].unsqueeze(1).to_broadcast([P, 2, L])
                bu = aux[:, t % 2, :].rearrange("p (a n) -> p a n", a=2)
                V.tensor_tensor(m1[:, :, :], bu, cb, ALU.mult)
                V.tensor_tensor(m2[:, :, :], bu, sb_, ALU.mult).then_inc(bu_used, 1)
                dve.wait_ge(bu_used, i * TPB + (t + 1) + GO)
                dve.wait_ge(h_ready, i * TPB + max(t - 1, 0) + GO)
                g = gs[t % 2]
                V.tensor_tensor(g[:, 0, :], m1[:, 0, :], m2[:, 1, :], ALU.add)
                link(V.tensor_tensor(g[:, 1, :], m1[:, 1, :], m2[:, 0, :], ALU.subtract))
                r = rho[:, bass.ds(i * TPB + t, 1)].to_broadcast([P, L])
                V.tensor_tensor_scan(g[:, 0, :], r, g[:, 0, :], 0.0, ALU.mult, ALU.add)
                V.tensor_tensor_scan(g[:, 1, :], r, g[:, 1, :], 0.0, ALU.mult, ALU.add).then_inc(gs_ready, 1)

            n0, g0 = UNIT0["conv"], BLOCK0["conv"]
            CONV_LINKS = 16
            with dve.Fori(0, SB) as i:
                link.loop(i, CONV_LINKS)
                nn = At(n0, 16, i)
                for b in range(8):
                    step(nn, b)
                    g = At(g0 + b, 8, i)
                    q = b // 4
                    j = i * 2 + q
                    if b % 4 == 0:
                        to_gate(g, At(8 + q, 2, i))
                    elif b % 4 == 1:
                        evac(V.tensor_tensor(convv, bank(g), rstd2[:, :], ALU.mult), g)
                        dve.wait_ge(bank_free[g.c % 4], g.turns(4, 1))
                    elif b % 4 == 2:
                        evac(V.tensor_tensor(convc[:, 2:L + 2], bank(g), convv, ALU.mult), g)
                        dve.wait_ge(bank_free[g.c % 4], g.turns(4, 1))
                        link(V.tensor_scalar(tmp[:, 0, :], convc[:, 0:L], par_c("conv0", j), None, ALU.mult))
                        link(V.scalar_tensor_tensor(convv, convc[:, 1:L + 1], par_c("conv1", j), tmp[:, 0, :],
                                                    ALU.mult, ALU.add))
                        link(V.scalar_tensor_tensor(tmp[:, 0, :], convc[:, 2:L + 2], par_c("conv2", j), convv,
                                                    ALU.mult, ALU.add))
                    else:
                        evac(V.tensor_tensor(convv, bank(g), tmp[:, 0, :], ALU.mult), g)
                        dve.wait_ge(bank_free[g.c % 4], g.turns(4, 1))
                        link(V.tensor_tensor(convv, convv, rstd[:, :], ALU.mult))
                        dve.wait_ge(gate_out, i * 2 + (8 + q + 1))
                        link(V.tensor_tensor(f[:, 0, :], convv, gt[:, q % 2, :], ALU.mult))
                        split_value(f[:, 0, :], blk(yah, j), blk(yal, j), ya_ready)
                    if b in SCAN_IN:
                        scan_in(i, SCAN_IN.index(b))
                dve.wait_ge(h_used, i * TPB + TPB + GO)
                V.scalar_tensor_tensor(blk(ug, i), blk(ug, i), par_c("d_skip", i), aux[:, 2, 0:L], ALU.mult, ALU.add)\
                    .then_inc(y_used, 1)
            link.done(SB)

            n0, g0 = UNIT0["gb"], BLOCK0["gb"]
            with dve.Fori(0, 4) as i:
                for b in range(4):
                    step(At(n0, 8, i), b)
                    to_gate(At(g0 + b, 4, i), At(24 + b, 4, i))

            n0, g0 = UNIT0["gaa"], BLOCK0["gaa"]
            with dve.Fori(0, 8) as i:
                for b in range(4):
                    step(At(n0, 8, i), b)
                    g = At(g0 + b, 4, i)
                    if b % 2 == 0:
                        to_gate(g, At(40 + b // 2, 2, i))
                    else:
                        dve.wait_ge(gate_out, i * 2 + (40 + b // 2 + 1))
                        evac(V.tensor_tensor(blk(mix, i * 2 + b // 2), gt[:, b // 2, :], bank(g), ALU.mult), g)

            dve.wait_ge(gelu_ready, 1)
            dve.wait_ge(unit_used, UNIT0["glu"])
            for j in range(SB):
                split_value(ug[:, j, :], ybh[:, j, :], ybl[:, j, :], yb_ready)

            n0, g0 = UNIT0["glu"], BLOCK0["glu"]
            for b in range(8):
                split_lo(At(n0 + b + 3))
                dve.wait_ge(glu_out, b + 1)
                evac(V.tensor_tensor(tmp[:, 0, :], ug[:, b, :], gt[:, b % 2, :], ALU.mult), At(g0 + b))
                dve.wait_ge(bank_free[(g0 + b) % 4], (g0 + b) // 4 + 1)
                link(V.tensor_tensor(f[:, b % 2, :], tmp[:, 0, :], szb[:, b, :], ALU.mult))
                split_value(f[:, b % 2, :], yoh[:, b, :], yol[:, b, :], yo_ready)

            n0, g0 = UNIT0["outb"], BLOCK0["outb"]
            with dve.Fori(0, 4) as i:
                link.loop(i, 8)
                for b in range(4):
                    split_lo(At(n0 + b + 3, 4, i))
                    dve.wait_ge(unit_used, At(n0 + b + 1, 4, i).v())
                    g = At(g0 + b, 4, i)
                    j = i * 4 + b
                    evac(V.tensor_tensor(tmp[:, 0, :], bank(g), blk(sgb, j), ALU.mult), g)
                    dve.wait_ge(bank_free[g.c % 4], g.turns(4, 1))
                    link(V.tensor_tensor(f[:, b % 2, :], tmp[:, 0, :], blk(mix, j), ALU.add))
                    split_value(f[:, b % 2, :], blk(mh, j), blk(ml, j), m_ready)
            link.done(4)

            c1, _ = PCOLS["final_g"]
            c2, _ = PCOLS["norm1"]
            link(V.tensor_tensor(gg[:, :], par[:, c1:c1 + KB], par[:, c2:c2 + KB], ALU.mult))
            link(V.memset(acc[:, :, :], 0.0))
            n0, g0 = UNIT0["wo"], BLOCK0["wo"]
            with dve.Fori(0, 4) as i:
                link.loop(i, 4)
                for b in range(4):
                    step(At(n0, 8, i), b)
                    g = At(g0 + b, 4, i)
                    j = i * 4 + b
                    xj = blk(x, j)
                    evac(V.tensor_tensor(xj, xj, bank(g), ALU.add), g)
                    dve.wait_ge(bank_free[g.c % 4], g.turns(4, 1))
                    gj = gg[:, bass.ds(j, 1)]
                    V.tensor_scalar(blk(nh, j), xj, gj, None, ALU.mult).then_inc(res_ready, 1)
                    dve.wait_ge(res_ready, j + 1)
                    V.scalar_tensor_tensor(blk(nl, j), xj, gj, blk(nh, j).bitcast(F32), ALU.mult, ALU.subtract)\
                        .then_inc(in_ready, 1)
                    dve.wait_ge(sq_ready, j + 1)
                    link(V.tensor_tensor(acc[:, :, :], acc[:, :, :], sq[:, :, :], ALU.add))
            link.done(4)
            V.memset(tmp[:, 1, 0:1], 0.0).then_inc(acc_ready, 1)

            def wide(name, j0=0, n=8):
                c, _ = PCOLS[name]
                return par[:, c + j0:c + j0 + n].unsqueeze(2).to_broadcast([P, n, L])

            n0, g0 = UNIT0["lora"], BLOCK0["lora"]
            link(V.memset(zs[:, 0:1], 0.0))
            for b in range(3):
                step(At(n0), b)
                g = At(g0 + b)
                if b == 0:
                    dve.wait_ge(norm_root, 1)
                    link(V.reciprocal(rstd2[:, :], tmp[:, 0, :]))
                    link(V.tensor_tensor(tmp[:, 1, :], aux[:, 3, L:2 * L], rstd2[:, :], ALU.mult))
                    V.tensor_tensor(tmp[:, 1, :], tmp[:, 1, :], rstd2[:, :], ALU.mult).then_inc(ms_ready, 1)
                    dve.wait_ge(norm_root, 2)
                    link(V.reciprocal(rstd[:, :], tmp[:, 0, :]))
                    V.tensor_tensor(rstd[:, :], rstd[:, :], rstd2[:, :], ALU.mult).then_inc(rstd_ready, 1)
                    dve.wait_ge(rstd_ready, 2)
                evac(V.tensor_tensor(zs[:, 1:L + 1], bank(g), rstd[:, :], ALU.mult), g)
                dve.wait_ge(bank_free[g.c % 4], g.turns(4, 1))
                link(V.tensor_tensor(tmp[:, 0, :], zs[:, 0:L], zs[:, 1:L + 1], ALU.subtract))
                dst = lo[:, :] if b == 0 else f[:, b - 1, :]
                V.scalar_tensor_tensor(dst, tmp[:, 0, :], par_c("mix_lo", b), zs[:, 1:L + 1], ALU.mult, ALU.add)\
                    .then_inc(lo_shifted, 1)
                dve.wait_ge(lo_shifted, b + 1)
            n0, g0 = UNIT0["rkv"], BLOCK0["rkv"]
            with dve.Fori(0, 6) as i:
                link.loop(i, 8)
                for b in range(4):
                    step(At(n0, 8, i), b)
                    g = At(g0 + b, 4, i)
                    j = i * 4 + b
                    evac(V.tensor_tensor(zs[:, 1:L + 1], bank(g), rstd[:, :], ALU.mult), g)
                    dve.wait_ge(bank_free[g.c % 4], g.turns(4, 1))
                    link(V.tensor_tensor(tmp[:, 0, :], zs[:, 0:L], zs[:, 1:L + 1], ALU.subtract))
                    link(V.scalar_tensor_tensor(blk(zr, j), tmp[:, 0, :], par_c("mix_rkv", j), zs[:, 1:L + 1],
                                                ALU.mult, ALU.add))
            link.done(6)

            def stage(i):
                t = tokens(i)
                for h in range(2):
                    V.tensor_copy(bkc[hrow(h), :, h, :], bb[hrow(h), :, t])
                    ins = V.tensor_copy(bkc[hrow(h), :, 1 - h, :], kr[hrow(h), :, t])
                ins.then_inc(staged, 1)

            def tokens(i):
                return slice(i * CH, (i + 1) * CH) if isinstance(i, int) else bass.ds(i * CH, CH)

            n0, g0 = UNIT0["qkv"], BLOCK0["qkv"]
            prepared = [0]

            def prep(ins):
                prepared[0] += 1
                ins.then_inc(prep_dve, 1)
                dve.wait_ge(prep_dve, prepared[0])

            c, _ = CCOLS["inchunk"]
            inchunk = const[:, c:c + L]
            for b in range(24):
                step(At(n0), b)
                g = At(g0 + b)
                evac(V.tensor_tensor(qkv[:, b, :], bank(g), rstd[:, :], ALU.mult), g)
                if b == 0:
                    prep(V.tensor_tensor(bb[:, :, :], kr, wide("k_k"), ALU.mult))
                if b == 2:
                    dve.wait_ge(up_act, 8)
                    dve.wait_ge(prep_act, 1)
                if b == 6:
                    dve.wait_ge(prep_act, 2)
                    link(V.tensor_scalar(br[:, :, :], br[:, :, :], 1e-12, None, ALU.max))
                if b in (6, 7, 8, 9):
                    ins = V.reciprocal(br[:, 2 * b - 12:2 * b - 10, :], br[:, 2 * b - 12:2 * b - 10, :])
                if b == 9:
                    prep(ins)
                if b == 10:
                    prep(V.tensor_tensor(bb[:, :, :], bb[:, :, :], br[:, :, :], ALU.mult))
                    link(V.scalar_tensor_tensor(ba[:, :, :], aa[:, :, :], -1.0, wide("k_a"), ALU.add, ALU.mult))
                if b == 11:
                    prep(V.scalar_tensor_tensor(kr, ba[:, :, :], 1.0, kr, ALU.add, ALU.mult))
                    link(V.tensor_scalar(ba[:, :, :], bb[:, :, :], -1.0, None, ALU.mult))
                if b == 12:
                    prep(V.tensor_tensor(bb[:, :, :], bb[:, :, :], aa[:, :, :], ALU.mult))
                if b == 13:
                    for j in range(4):
                        V.tensor_tensor_scan(aa[:, j, :], inchunk, sw[:, j, :], 0.0, ALU.mult, ALU.add)
                if b == 14:
                    for j in range(4, 8):
                        ins = V.tensor_tensor_scan(aa[:, j, :], inchunk, sw[:, j, :], 0.0, ALU.mult, ALU.add)
                    prep(ins)
                    prep(V.tensor_tensor(sw[:, :, :], aa[:, :, :], sw[:, :, :], ALU.subtract))
                if b == 16:
                    dve.wait_ge(prep_act, 3)
                    V.tensor_copy(pc[:, :, :], br[:, :, :].rearrange("p j (c t) -> p j c t", t=CH)[:, :, :, CH - 1])
                    dve.wait_ge(prep_act, 4)
                    prep(V.tensor_tensor(ba[:, :, :], ba[:, :, :], sw[:, :, :], ALU.mult))
                if b == 17:
                    link(V.tensor_tensor(sw[:, :, :], rr, wide("r_k"), ALU.mult))
                if b == 18:
                    prep(V.tensor_tensor(sw[:, :, :], sw[:, :, :], kr, ALU.mult))
                if b == 19:
                    link(V.tensor_tensor(br[:, :, :], br[:, :, :], rr, ALU.mult))
                if b == 20:
                    dve.wait_ge(prep_act, 5)
                    link(V.tensor_tensor(bb[:, :, :], bb[:, :, :], aa[:, :, :], ALU.mult))
                if b == 21:
                    link(V.tensor_tensor(kr, kr, aa[:, :, :], ALU.mult))
                if b in (22, 23):
                    dve.wait_ge(head_mm, 2)
                    for c in range(2 * (b - 22), 2 * (b - 22) + 2):
                        ins = V.tensor_tensor(sw[:, 2 * c:2 * c + 2, :].rearrange("p j n -> p (j n)"), aux[:, c, :],
                                              vr[:, 2 * c:2 * c + 2, :].rearrange("p j n -> p (j n)"), ALU.mult)
                    prep(ins)
                if b == 22:
                    stage(0)
            assert prepared[0] == PREP_DVE

            def scores(i, s):
                r = s % 2
                if not (isinstance(i, int) and s < 2):
                    dve.wait_ge(pt_mm, i * 2 + (s - 1))
                for h in range(2):
                    dve.wait_ge(bias_ready, i * 2 + (s + 1))
                    dve.wait_ge(sc_mm, i * 2 + (s + 1))
                    V.scalar_tensor_tensor(eb[:, r, h, :], main[:, 2 * r + h, 0:384], ATTN_SCALE, biasb[:, r, h, :],
                                           ALU.mult, ALU.add).then_inc(e_ready, 1)
                    dve.wait_ge(e_ready, i * 4 + (2 * s + h + 1) + GO)
                    V.tensor_reduce(mxs[:, r, h, 0, 0:1], eb[:, r, h, 0:P], AX.X, ALU.max)
                    link(V.tensor_reduce(mxs[:, r, h, 1, 0:1], eb[:, r, h, P:384], AX.X, ALU.max))
                    V.tensor_scalar(mxs[:, r, h, :, 1], mxs[:, r, h, :, 0], -1.0, None, ALU.mult).then_inc(max_ready, 1)

            def normalise(i, s):
                r = s % 2
                for h in range(2):
                    dve.wait_ge(p_ready, i * 4 + (2 * s + h + 1))
                    link(V.reciprocal(mxs[:, r, h, :, 3], mxs[:, r, h, :, 2]))
                    V.tensor_scalar(eb[:, r, h, 0:P], eb[:, r, h, 0:P], mxs[:, r, h, 0, 3:4], None, ALU.mult)
                    V.tensor_scalar(eb[:, r, h, P:384], eb[:, r, h, P:384], mxs[:, r, h, 1, 3:4], None, ALU.mult)\
                        .then_inc(pn_ready, 1)

            def outputs(i, s):
                dve.wait_ge(o_mm, i * 2 + (s + 1))
                o = aux[:, 2 + s % 2, 0:L]
                j = i * 2 + s
                link(V.tensor_copy(blk(mxh, j), o))
                V.tensor_tensor(blk(mxl, j), o, blk(mxh, j).bitcast(F32), ALU.subtract).then_inc(att_ready, 1)

            scores(0, 0)
            scores(0, 1)
            normalise(0, 0)
            with dve.Fori(0, PAIRS // 2 - 1) as i:
                link.loop(i, 10)
                for s in (1, 2):
                    scores(i, s + 1)
                    normalise(i, s)
                    outputs(i, s - 1)
            link.done(PAIRS // 2 - 1)
            b0, b2, a0, a2 = ([main[:, 0], main[:, 1]], [main[:, 2], main[:, 3]],
                              [aux[:, 0], aux[:, 1]], [aux[:, 2], aux[:, 3]])

            def mask(name, h):
                c, w = CCOLS[name]
                return const[hrow(h), c:c + w].unsqueeze(1).to_broadcast([64, 8, w])

            def flat(t, h):
                return t[hrow(h), :, :].rearrange("p j n -> p (j n)")

            def heads(bank_, h):
                return bank_[h][hrow(h), :].rearrange("p (j n) -> p j n", n=CH)

            def masked_products(h, banks, r):
                cm, _ = CCOLS["maskg"]
                both = banks.rearrange("p b (j n) -> p (b j) n", n=P)
                m = const[:, cm:cm + P].unsqueeze(1).to_broadcast([P, 8, P])
                V.tensor_tensor(ga[:, h, :, :], both[:, :, 0:CH], m[:, :, 0:CH], ALU.mult)
                return V.tensor_tensor(r[:, h, :, :], both[:, :, CH:P], m[:, :, CH:P], ALU.mult)

            def diagonal_and_rest(banks, which=(0, 1)):
                for h in which:
                    V.tensor_tensor(mat["n"][hrow(h), :, :], heads(banks, h), mask("mdiag", h), ALU.mult)
                    V.tensor_tensor(mat["f"][hrow(h), :, :], heads(banks, h), mask("moff", h), ALU.mult)
                    ins = V.tensor_tensor(mat["nt"][hrow(h), :, :], ga[hrow(h), h, :, :], mask("mdiagt", h), ALU.mult)
                return ins

            cm, _ = CCOLS["eye64"]
            eye = const[:, cm:cm + CH].unsqueeze(1).to_broadcast([P, 8, CH])
            normalise(0, PAIRS - 1)
            dve.wait_ge(core_pre, 1)
            masked_products(0, main[:, 0:2, :], gr)
            outputs(0, PAIRS - 2)
            dve.wait_ge(core_pre, 2)
            link(masked_products(1, main[:, 2:4, :], gr))
            outputs(0, PAIRS - 1)

            link(V.memset(state[:, :, :], 0.0))
            dve.wait_ge(core_pre, 3)
            link(diagonal_and_rest(a0))
            V.tensor_tensor(mat["w"][:, :, :], mat["nt"][:, :, :], eye, ALU.add).then_inc(core_start, 1)
            for j in range(8):
                ins = V.tensor_scalar(sw[:, j, :], sw[:, j, :], par_c("ln_b", j), None, ALU.add)
            link(ins)

            def chunk(i, last=False):
                def mm(name):
                    dve.wait_ge(core_mm, i * len(MM) + MM[name] + GO)

                def done(name, ins):
                    ins.then_inc(core_dve, steps(DV, DV_NEXT, name, last))
                    dve.wait_ge(core_dve, i * len(DV) + DV[name])

                def take(name, banks, dst):
                    mm(name)
                    for h in range(2):
                        ins = V.tensor_copy(flat(dst, h), banks[h][hrow(h), :])
                    done(name, ins)

                def plus(name, banks, dst, old):
                    mm(name)
                    for h in range(2):
                        ins = V.tensor_tensor(flat(dst, h), flat(old, h), banks[h][hrow(h), :], ALU.add)
                    done(name, ins)

                take("n2t", b0, mat["n2t"])
                take("n4t", b0, mat["n4t"])
                for h in range(2):
                    V.memset(st[hrow(h), :, h, :], 0.0)
                plus("w2", b2, mat["w"], mat["w"])
                plus("w4", b2, mat["w"], mat["w"])
                plus("w8", b2, mat["w"], mat["w"])
                if not last:
                    stage(i + 1)
                take("qt", b0, mat["nt"])
                done("t1", V.tensor_tensor(mat["n2t"][:, :, :], mat["nt"][:, :, :], eye, ALU.add))
                if not last:
                    mm("g0")
                    done("gm0", masked_products(0, aux[:, 2:4, :], grn))
                plus("g1", a0, mat["n4t"], mat["n2t"])
                if not last:
                    mm("g2")
                    done("gm1", masked_products(1, main[:, 0:2, :], grn))
                    mm("n")
                    diagonal_and_rest(a2, (0,))
                mm("sa")
                for h in range(2):
                    ins = V.tensor_copy(st[hrow(h), :, h, :], heads(a0, h))
                done("sa", ins)
                if not last:
                    done("nf", diagonal_and_rest(a2, (1,)))
                    done("w1", V.tensor_tensor(mat["w"][:, :, :], mat["nt"][:, :, :], eye, ALU.add))
                mm("y")
                for h in range(2):
                    ins = V.tensor_copy(vr[hrow(h), :, tokens(i)], heads(b2, h))
                done("y", ins)
                if not last:
                    mm("s")
                    link(V.tensor_tensor(state[:, :, :], state[:, :, :],
                                         aux[:, 2, :].rearrange("p (j n) -> p j n", n=CH), ALU.add))
                    done("s", V.tensor_tensor(state[:, :, :], state[:, :, :], pc[:, :, bass.ds(i, 1)].to_broadcast([P, 8, CH]),
                                              ALU.mult))
                    done("gr", V.tensor_copy(gr[:, :, :, :], grn[:, :, :, :]))

            with dve.Fori(0, NCH - 1) as i:
                link.loop(i, 1)
                chunk(i)
            link.done(NCH - 1)
            chunk(NCH - 1, True)

            def four(t, c):
                return t[:, 2 * c:2 * c + 2, :].rearrange("p j n -> p (j n)")

            for c in range(4):
                dve.wait_ge(fin_mm, c + 1)
                V.scalar_tensor_tensor(four(vr, c), aux[:, c, :], -1.0 / 64, four(vr, c), ALU.mult, ALU.add)\
                    .then_inc(fin_dve, 1)
            for c in range(4):
                dve.wait_ge(fin_act, 8 + c + 1)
                link(V.tensor_tensor(four(vr, c), four(vr, c), four(gnt, c), ALU.mult))
                for j in (2 * c, 2 * c + 1):
                    ins = V.scalar_tensor_tensor(vr[:, j, :], vr[:, j, :], par_c("ln_w", j), sw[:, j, :], ALU.mult, ALU.add)
                link(ins)
                dve.wait_ge(gate_sb, c + 1)
                link(V.tensor_tensor(four(vr, c), four(vr, c), four(gsb, c), ALU.mult))
                split_value(vr[:, 2 * c:2 * c + 2, :], mxh[:, 8 + 2 * c:10 + 2 * c, :], mxl[:, 8 + 2 * c:10 + 2 * c, :],
                            rwkv_ready)

            link(V.memset(acc[:, 0, :], 0.0))
            n0, g0 = UNIT0["wout"], BLOCK0["wout"]
            dve.wait_ge(res_scaled, 1)
            with dve.Fori(0, 4) as i:
                link.loop(i, 4)
                for b in range(4):
                    step(At(n0, 8, i), b)
                    g = At(g0 + b, 4, i)
                    j = i * 4 + b
                    xj = blk(x, j)
                    evac(V.tensor_tensor(xj, xj, bank(g), ALU.add), g)
                    dve.wait_ge(bank_free[g.c % 4], g.turns(4, 1))
                    V.tensor_scalar(blk(x3h, j), xj, par_c("norm2", j), None, ALU.mult).then_inc(res_ready, 1)
                    dve.wait_ge(res_ready, j + (KB + 1))
                    V.scalar_tensor_tensor(blk(x3l, j), xj, par_c("norm2", j), blk(x3h, j).bitcast(F32),
                                           ALU.mult, ALU.subtract).then_inc(in_ready, 1)
                    dve.wait_ge(sq_ready, j + (KB + 1))
                    link(V.tensor_tensor(acc[:, 0, :], acc[:, 0, :], sq[:, 0, :], ALU.add))
            link.done(4)
            V.memset(tmp[:, 1, 0:1], 0.0).then_inc(acc_ready, 1)

            n0, g0 = UNIT0["ffn"], BLOCK0["ffn"]

            def ffn(i):
                for b in range(4):
                    step(At(n0, 8, i), b)
                    g = At(g0 + b, 4, i)
                    if b == 0 and i is None:
                        dve.wait_ge(norm_root, 3)
                        V.reciprocal(rstd[:, :], tmp[:, 0, :]).then_inc(rstd_ready, 1)
                        dve.wait_ge(rstd_ready, 3)
                    if b % 2 == 0:
                        to_gate(g, At(56 + b // 2, 2, i))
                    else:
                        k = At(56 + b // 2, 2, i)
                        evac(V.tensor_tensor(tmp[:, 0, :], bank(g), rstd[:, :], ALU.mult), g)
                        dve.wait_ge(bank_free[g.c % 4], g.turns(4, 1))
                        dve.wait_ge(gate_out, k.v(1))
                        j = b // 2 if i is None else i * 2 + b // 2
                        link(V.tensor_tensor(f[:, b // 2, :], tmp[:, 0, :], gt[:, b // 2, :], ALU.mult))
                        split_value(f[:, b // 2, :], blk(ah, j), blk(al, j), act_ready)

            ffn(None)
            with dve.Fori(1, FB // 2) as i:
                link.loop(i, 4, 1)
                ffn(i)
            link.done(FB // 2 - 1)

            link(V.memset(acc[:, 0, :], 0.0))
            n0, g0 = UNIT0["down"], BLOCK0["down"]

            def down(i, c=0, last=False):
                for b in range(4):
                    for u in range(6):
                        if not (last and 6 * b + u + 3 >= 24):
                            split_lo(At(n0 + 24 * c + 6 * b + u + 3, 24, i), down_width((u + 3) % 6))
                    dve.wait_ge(unit_used, At(n0 + 24 * c + 6 * b + 6, 24, i).v())
                    g = At(g0 + 4 * c + b, 4, i)
                    j = c * 4 + b if i is None else i * 4 + b
                    xj = blk(x, j)
                    V.tensor_tensor(xj, xj, bank(g), ALU.add).then_inc(res_ready, 1)
                    dve.wait_ge(res_ready, j + (2 * KB + 1))
                    dve.wait_ge(sq_ready, j + (2 * KB + 1))
                    evac(V.tensor_tensor(acc[:, 0, :], acc[:, 0, :], sq[:, 0, :], ALU.add), g)
                    dve.wait_ge(bank_free[g.c % 4], g.turns(4, 1))

            with dve.Fori(0, 3) as i:
                down(i)
            down(None, 3, True)
            V.memset(tmp[:, 1, 0:1], 0.0).then_inc(acc_ready, 1)
            dve.wait_ge(norm_root, 4)
            link(V.reciprocal(rstd[:, :], tmp[:, 0, :]))
            for j in range(KB):
                ins = V.scalar_tensor_tensor(x[:, j, :], x[:, j, :], par_c("final2", j), rstd[:, :], ALU.mult, ALU.mult)
                if j % 4 == 3:
                    ins.then_inc(out_ready, 1)

        @block.tensor
        def _(pe):
            for counted in (h_used, vt_mm, core_mm):
                pe.sem_inc(counted, GO)

            def unit(n, g, xh_, xl_, kb0, kbs, first, last, split=None):
                s = n.c % RING
                pe.wait_ge(lo_ready, n.v(1))
                out = main[:, g.c % 4, 0:L]
                for kk in range(kbs):
                    w = slice(kk * P, (kk + 1) * P)
                    k = kb0 + kk
                    if split and k % (split[2:] or (1,))[0] == 0:
                        pe.wait_ge(split[0], split[1] + k // (split[2:] or (1,))[0] + 1)
                    nc.tensor.matmul(out, whi[:, s, w], xh_[:, k, :], start=(first and kk == 0), stop=False)
                    nc.tensor.matmul(out, whi[:, s, w], xl_[:, k, :], start=False, stop=False)
                    ins = nc.tensor.matmul(out, wlo[:, s, w], xh_[:, k, :], start=False, stop=(last and kk == kbs - 1))
                ins.then_inc(unit_used, 1)

            def free(g):
                if g.i is not None or g.c >= 4:
                    pe.wait_ge(bank_free[g.c % 4], g.turns(4))

            def column(n, g, xh_, xl_, split=None):
                free(g)
                unit(n, g, xh_, xl_, 0, 8, True, False, split)
                unit(n + 1, g, xh_, xl_, 8, 8, False, True, split)

            def head_sum(out, w, v):
                return nc.tensor.matmul(out, w, v, start=True, stop=True)

            n0, g0 = UNIT0["u"], BLOCK0["u"]
            for b in range(8):
                column(At(n0 + 2 * b), At(g0 + b), xh, xl, (in_ready, 0) if b == 0 else None)
                if b == 1:
                    pe.wait_ge(acc_ready, 1)
                    pe.wait_ge(const_loaded, 16)
                    head_sum(aux[:, 3, 0:L], cst("ones"), acc[:, 0, :]).then_inc(ssq_ready, 1)
            n0, g0 = UNIT0["zb"], BLOCK0["zb"]
            for b in range(8):
                column(At(n0 + 2 * b), At(g0 + b), xh, xl)

            def scan_bu(i, t):
                if t == 0:
                    pe.wait_ge(b_loaded, i * 16 + 16)
                pe.wait_ge(bu_used, (i * TPB if t < 2 else i * TPB + (t - 1)) + GO)
                uj = ug[:, bass.ds(i, 1), :].rearrange("p a n -> p (a n)")
                nc.tensor.matmul(aux[:, t % 2, 0:L], bstage[:, t, 0, :], uj, start=True, stop=True)
                nc.tensor.matmul(aux[:, t % 2, L:2 * L], bstage[:, t, 1, :], uj, start=True, stop=True)\
                    .then_inc(bu_ready, 1)

            def scan_y(i, t):
                if t == 0:
                    pe.wait_ge(c_staged, i + 1)
                    pe.wait_ge(y_used, i + GO)
                pe.wait_ge(h_ready, i * TPB + (t + 1) + GO)
                out = aux[32 * t:32 * t + 32, 2, 0:L]
                nc.tensor.matmul(out, cstage[:, t, 0, :], hs[:, t % 2, 0, :], start=True, stop=False,
                                 tile_position=(0, 32 * t))
                nc.tensor.matmul(out, cstage[:, t, 1, :], hs[:, t % 2, 1, :], start=False, stop=True,
                                 tile_position=(0, 32 * t)).then_inc(h_used, 1)

            n0, g0 = UNIT0["conv"], BLOCK0["conv"]
            with pe.Fori(0, SB) as i:
                for b in range(8):
                    for t in range(TPB):
                        if SCAN_BU[t] == b:
                            scan_bu(i, t)
                        if SCAN_Y[t] == b:
                            scan_y(i, t)
                    column(At(n0 + 2 * b, 16, i), At(g0 + b, 8, i), xh, xl)
            n0, g0 = UNIT0["gb"], BLOCK0["gb"]
            with pe.Fori(0, 4) as i:
                for b in range(4):
                    column(At(n0 + 2 * b, 8, i), At(g0 + b, 4, i), xh, xl)
            n0, g0 = UNIT0["gaa"], BLOCK0["gaa"]
            pe.wait_ge(ya_ready, KB)
            with pe.Fori(0, 8) as i:
                for b in range(4):
                    column(At(n0 + 2 * b, 8, i), At(g0 + b, 4, i), *((xh, xl) if b % 2 == 0 else (yah, yal)))
            n0, g0 = UNIT0["glu"], BLOCK0["glu"]
            for b in range(8):
                free(At(g0 + b))
                unit(At(n0 + b), At(g0 + b), ybh, ybl, 0, 8, True, True, (yb_ready, 0) if b == 0 else None)
            n0, g0 = UNIT0["outb"], BLOCK0["outb"]
            with pe.Fori(0, 4) as i:
                for b in range(4):
                    free(At(g0 + b, 4, i))
                    unit(At(n0 + b, 4, i), At(g0 + b, 4, i), yoh, yol, 0, 8, True, True, (yo_ready, 0) if b == 0 else None)
            n0, g0 = UNIT0["wo"], BLOCK0["wo"]
            with pe.Fori(0, 4) as i:
                for b in range(4):
                    column(At(n0 + 2 * b, 8, i), At(g0 + b, 4, i), mh, ml, (m_ready, 0) if b == 0 else None)

            def norm_total(n, w):
                pe.wait_ge(acc_ready, n)
                nc.tensor.matmul(aux[:, 3, 0:w], cst("ones"), acc[:, :, :].rearrange("p a n -> p (a n)")[:, 0:w],
                                 start=True, stop=True).then_inc(norm_sum, 1)

            n0, g0 = UNIT0["lora"], BLOCK0["lora"]
            for b in range(3):
                column(At(n0 + 2 * b), At(g0 + b), nh, nl, (in_ready, KB) if b == 0 else None)
                if b == 0:
                    norm_total(2, 2 * L)
            pe.wait_ge(lora_loaded, 16)
            pe.wait_ge(lo_act, 3)
            for j in range(8):
                if j >= 2:
                    pe.wait_ge(up_act, j - 1)
                cols = slice(j * P, (j + 1) * P)
                nc.tensor.matmul(aux[:, j % 2, 0:L], lora[0:64, cols], lo[0:64, :], start=True, stop=True)
                nc.tensor.matmul(aux[:, 2 + j % 2, 0:L], lora[64:128, cols], lo[64:128, :], start=True, stop=True)\
                    .then_inc(up_mm, 1)
            n0, g0 = UNIT0["rkv"], BLOCK0["rkv"]
            with pe.Fori(0, 6) as i:
                for b in range(4):
                    column(At(n0 + 2 * b, 8, i), At(g0 + b, 4, i), nh, nl)
            n0, g0 = UNIT0["qkv"], BLOCK0["qkv"]

            def qkv_part(first, turns):
                with pe.Fori(0, turns) as i:
                    for b in range(4):
                        column(At(n0 + 8 * first + 2 * b, 8, i), At(g0 + 4 * first + b, 4, i), nh, nl)

            def over_heads(src):
                for c in range(4):
                    ins = nc.tensor.matmul(aux[:, c, :], cst("hones"), src[:, 2 * c:2 * c + 2, :]
                                           .rearrange("p j n -> p (j n)"), start=True, stop=True)
                return ins

            qkv_part(0, 1)
            pe.wait_ge(prep_act, 1)
            pe.wait_ge(up_act, 8)
            over_heads(ba).then_inc(head_mm, 1)
            qkv_part(1, 4)
            pe.wait_ge(prep_dve, 9)
            over_heads(sw).then_inc(head_mm, 1)
            qkv_part(5, 1)

            for g in range(BLOCK0["wout"] - 4, BLOCK0["wout"]):
                pe.wait_ge(bank_free[g % 4], g // 4 + 1)
            pe.wait_ge(prep_dve, PREP_DVE)
            def pair_scores(p):
                q, k = qkv[:, 3 * p, :], qkv[:, 3 * p + 1, :]
                if p >= 2:
                    pe.wait_ge(e_ready, 2 * p - 2 + GO)
                for h in range(2):
                    out = main[:, 2 * (p % 2) + h, :]
                    nc.tensor.matmul(out[:, 0:P], q[hrow(h), 0:P], k[hrow(h), 0:P], start=True, stop=True)
                    ins = nc.tensor.matmul(out[:, P:384], q[hrow(h), P:L], k[hrow(h), :], start=True, stop=True)
                ins.then_inc(sc_mm, 1)

            def pair_values(p):
                if p >= 2:
                    pe.wait_ge(att_ready, p - 1 + GO)
                for b in range(2):
                    ins = nc.tensor.transpose(aux[:, 2 + p % 2, L + b * P:L + (b + 1) * P],
                                              qkv[:, 3 * p + 2, b * P:(b + 1) * P], cst("ident"))
                ins.then_inc(vt_mm, 1)

            def pair_probs(p):
                pe.wait_ge(pn_ready, 2 * p + 2)
                pe.wait_ge(pt_sb, p + GO)
                for h in range(2):
                    for b in range(3):
                        ins = nc.tensor.transpose(aux[:, h, b * P:(b + 1) * P], eb[:, p % 2, h, b * P:(b + 1) * P],
                                                  cst("ident"))
                ins.then_inc(pt_mm, 1)

            def pair_output(p):
                pe.wait_ge(pt_sb, p + 1 + GO)
                pe.wait_ge(vt_sb, p + 1)
                for h in range(2):
                    out = aux[hrow(h), 2 + p % 2, 0:L]
                    nc.tensor.matmul(out, vt[:, p % 2, 0, hrow(h)], pt[:, p % 2, h, 0:L], start=True, stop=False)
                    ins = nc.tensor.matmul(out[:, P:L], vt[:, p % 2, 1, hrow(h)], pt[:, p % 2, h, L:384],
                                           start=False, stop=True)
                ins.then_inc(o_mm, 1)

            b0, b2, a0, a2 = ([main[:, 0], main[:, 1]], [main[:, 2], main[:, 3]],
                              [aux[:, 0], aux[:, 1]], [aux[:, 2], aux[:, 3]])
            cm, _ = CCOLS["eye64"]

            def toks(i):
                return slice(i * CH, (i + 1) * CH)

            def every_head(banks, fn):
                for j in range(8):
                    for h in range(2):
                        ins = nc.tensor.matmul(banks[h][hrow(h), j * CH:(j + 1) * CH], *fn(j, h), start=True, stop=True)
                return ins

            def with_a_and_r(i, h, banks):
                for j in range(8):
                    ins = nc.tensor.matmul(banks[:, j // 4, (j % 4) * P:(j % 4 + 1) * P],
                                           bkc[hrow(h), j, :, :].rearrange("p a n -> p (a n)"),
                                           abr[hrow(h), :, j, toks(i)], start=True, stop=True)
                return ins

            def a_with_b(i, banks):
                return every_head(banks, lambda j, h: (ba[hrow(h), j, toks(i)], bkc[hrow(h), j, h, :]))

            pair_scores(0)
            pair_values(0)
            pair_scores(1)
            for p in range(PAIRS):
                if p + 2 < PAIRS:
                    pair_scores(p + 2)
                else:
                    h = p + 2 - PAIRS
                    pe.wait_ge(e_ready, 2 * p + 2 + GO)
                    pe.wait_ge(staged, 1)
                    with_a_and_r(0, h, main[:, 2 * h:2 * h + 2, :]).then_inc(core_pre, 1)
                pair_probs(p)
                pair_output(p)
                if p + 1 < PAIRS:
                    pair_values(p + 1)
            a_with_b(0, a0).then_inc(core_pre, 1)

            pe.wait_ge(att_ready, PAIRS + GO)
            for i in range(NCH):
                last = i == NCH - 1

                def dv(name, back=0):
                    pe.wait_ge(core_dve, (i - back) * len(DV) + DV[name])

                def ac(name):
                    pe.wait_ge(core_act, i * len(AC) + AC[name])

                def done(name, ins):
                    ins.then_inc(core_mm, steps(MM, MM_NEXT, name, last))

                def prod(name, banks, w, v):
                    done(name, every_head(banks, lambda j, h: (mat[w][hrow(h), j, :], mat[v][hrow(h), j, :])))

                if i:
                    dv("w1", 1)
                else:
                    pe.wait_ge(core_start, 1)
                prod("n2", a0, "nt", "n")
                prod("n2t", b0, "n", "nt")
                if i:
                    dv("s", 1)
                for j in range(8):
                    for h in range(2):
                        ins = nc.tensor.matmul(aux[hrow(1 - h), 2 + h, j * CH:(j + 1) * CH], vr[hrow(h), j, toks(i)],
                                               const[hrow(h), cm:cm + CH], start=True, stop=True)
                done("vt", ins)
                ac("n2")
                dv("n2t")
                prod("n4", a0, "n2t", "n2")
                prod("n4t", b0, "n2", "n2t")
                prod("w2", b2, "n2", "w")
                ac("n4")
                dv("n4t")
                prod("n8", a0, "n4t", "n4")
                dv("w2")
                prod("w4", b2, "n4", "w")
                ac("vt")
                for j in range(8):
                    ins = nc.tensor.transpose(aux[:, 2 + j // 4, (j % 4) * P:(j % 4 + 1) * P],
                                              bkc[:, j, :, :].rearrange("p a n -> p (a n)"), cst("ident"))
                done("bkt", ins)
                ac("n8")
                dv("w4")
                prod("w8", b2, "n2", "w")
                ac("bkt")
                for j in range(8):
                    for h in range(2):
                        out = a2[h][hrow(h), j * CH:(j + 1) * CH]
                        nc.tensor.matmul(out, ba[hrow(h), j, toks(i)], state[hrow(h), j, :], start=True, stop=False)
                        ins = nc.tensor.matmul(out, ga[:, h, j, :], st[:, j, h, :], start=False, stop=True)
                done("x", ins)
                dv("w8")
                prod("qt", b0, "f", "w")
                prod("q", a0, "w", "f")
                done("md", every_head(b2, lambda j, h: (mat["w"][hrow(h), j, :], const[hrow(h), cm:cm + CH])))
                dv("qt")
                ac("q")
                prod("q2", b0, "nt", "n")
                if not last:
                    pe.wait_ge(staged, i + 2)
                    ac("x")
                    done("g0", with_a_and_r(i + 1, 0, aux[:, 2:4, :]))
                ac("q2")
                dv("t1")
                prod("g1", a0, "n4", "n2t")
                if not last:
                    done("g2", with_a_and_r(i + 1, 1, main[:, 0:2, :]))
                ac("md")
                dv("g1")
                prod("mt", b2, "md", "n4t")
                if not last:
                    dv("gm0")
                    done("n", a_with_b(i + 1, a2))
                ac("mt")
                done("sa", every_head(a0, lambda j, h: (mat["n2"][hrow(h), j, :], xv[hrow(h), j, :])))
                if i:
                    dv("gr", 1)
                dv("sa")
                for j in range(8):
                    for h in range(2):
                        out = b2[h][hrow(h), j * CH:(j + 1) * CH]
                        nc.tensor.matmul(out, state[hrow(h), j, :], br[hrow(h), j, toks(i)], start=True, stop=False)
                        ins = nc.tensor.matmul(out, st[:, j, h, :], gr[:, h, j, :], start=False, stop=True)
                done("y", ins)
                if not last:
                    for j in range(8):
                        for h in range(2):
                            ins = nc.tensor.matmul(aux[hrow(h), 2, j * CH:(j + 1) * CH], bkt[:, j, hrow(h)], st[:, j, h, :],
                                                   start=True, stop=True)
                    done("s", ins)

            pe.wait_ge(core_dve, (NCH - 1) * len(DV) + DV["y"])
            def sum_heads(src, c):
                nc.tensor.matmul(aux[:, c, :], cst("hones"), src[:, 2 * c:2 * c + 2, :].rearrange("p j n -> p (j n)"),
                                 start=True, stop=True).then_inc(fin_mm, 1)

            def gate_block(j):
                cols = slice(j * P, (j + 1) * P)
                out = main[:, j // 2, (j % 2) * L:(j % 2 + 1) * L]
                nc.tensor.matmul(out, gup[:, 0, cols], sgl[:, 0, :], start=True, stop=False)
                nc.tensor.matmul(out, gup[0:32, 1, cols], sgl[0:32, 1, :], start=False, stop=True).then_inc(gu_mm, 1)

            for c in range(4):
                sum_heads(vr, c)
            pe.wait_ge(gup_loaded, 16)
            for j in range(2):
                gate_block(j)
            for c in range(4):
                pe.wait_ge(fin_act, c + 1)
                sum_heads(gnt, c)
            for j in range(2, 8):
                gate_block(j)
            pe.wait_ge(gate_sb, 4)
            n0, g0 = UNIT0["wout"], BLOCK0["wout"]
            with pe.Fori(0, 4) as i:
                for b in range(4):
                    n, g = At(n0 + 2 * b, 8, i), At(g0 + b, 4, i)
                    free(g)
                    unit(n, g, mxh, mxl, 0, 8, True, False)
                    unit(n + 1, g, mxh, mxl, 8, 8, False, True, (rwkv_ready, -4, 2) if b == 0 else None)
            n0, g0 = UNIT0["ffn"], BLOCK0["ffn"]
            for b in range(4):
                column(At(n0 + 2 * b), At(g0 + b), x3h, x3l, (in_ready, 2 * KB) if b == 0 else None)
                if b == 0:
                    norm_total(3, L)
            with pe.Fori(1, FB // 2) as i:
                for b in range(4):
                    column(At(n0 + 2 * b, 8, i), At(g0 + b, 4, i), x3h, x3l)
            n0, g0 = UNIT0["down"], BLOCK0["down"]
            pe.wait_ge(act_ready, FB)
            with pe.Fori(0, KB // 4) as i:
                for b in range(4):
                    g = At(g0 + b, 4, i)
                    free(g)
                    for u in range(6):
                        unit(At(n0 + 6 * b + u, 24, i), g, ah, al, 8 * u, down_width(u) // P, u == 0, u == 5)
            norm_total(4, L)


def _columns(w, cols):
    k = w.shape[0] // P
    return w[:, cols].reshape(k, P, P).transpose(1, 0, 2).reshape(P, k * P)


def _units(w, cols):
    return list(_columns(w, cols).reshape(P, -1, U).transpose(1, 0, 2))


def _rows(v):
    return np.asarray(v).reshape(-1, P).T


def _stream(w_in, w_out_a, w_glu, w_out_b, w_o, w_in_2, w_out_2, w_gate_up):
    def blk(start, j):
        return slice(start + j * P, start + (j + 1) * P)

    v, bg, cg, za, u, zb, ga, gb = (0, 2048, 4096, 6144, 8192, 9216, 10240, 12288)
    out = []
    for j in range(8):
        out += _units(w_in, blk(u, j))
    for j in range(8):
        out += _units(w_in, blk(zb, j))
    for j in range(16):
        for start in (za, v, cg, bg):
            out += _units(w_in, blk(start, j))
    for j in range(16):
        out += _units(w_in, blk(gb, j))
    for j in range(16):
        out += _units(w_in, blk(ga, j)) + _units(w_out_a, blk(0, j))
    for j in range(8):
        out += _units(w_glu, blk(0, j))
    for j in range(16):
        out += _units(w_out_b, blk(0, j))
    for j in range(16):
        out += _units(w_o, blk(0, j))
    z = 3 * 1024
    lo = np.concatenate([w_in_2[:, z + 3072:z + 3360], np.zeros((D, 96), np.float32)], axis=1)
    for j in range(3):
        out += _units(lo, blk(0, j))
    for j in range(24):
        out += _units(w_in_2, blk(z, j))
    for j in range(8):
        for start in (0, 1024, 2048):
            out += _units(w_in_2, blk(start, j))
    for j in range(16):
        out += _units(w_out_2, blk(0, j))
    for j in range(FB):
        out += _units(w_gate_up, blk(0, j)) + _units(w_gate_up, blk(FFN, j))
    assert len(out) == UNITS_MAIN
    return np.stack(out)


def _bucket(dist):
    if dist < 16:
        return dist
    big = 16 + int(np.float32(np.log(np.float32(dist) / np.float32(16))) / np.float32(math.log(2048 / 16)) * np.float32(16))
    return min(big, 31)


def _spans():
    q = np.arange(P)[:, None]
    return np.concatenate([q - np.arange(P)[None, :], q + P - np.arange(L)[None, :]], axis=1)


def _constants():
    c = np.zeros((P, NCONST), np.float32)

    def put(name, a):
        at, w = CCOLS[name]
        c[:a.shape[0], at:at + w] = a

    n, m = np.arange(P)[:, None], np.arange(P)[None, :]
    put("iota", np.tile(np.arange(L, dtype=np.float32), (P, 1)))
    put("inchunk", np.tile((np.arange(L) % CH > 0).astype(np.float32), (P, 1)))
    put("round", np.full((P, 1), ROUND))
    put("ones", np.ones((P, P)))
    put("hones", (n // 64 == m // 64).astype(np.float32))
    put("ident", np.eye(P))
    s, t = n % CH, m % CH
    put("maskg", np.where(m < CH, s < t, s <= t).astype(np.float32))
    n, m = np.arange(CH)[:, None], np.arange(CH)[None, :]
    put("mdiag", np.tile(((m < n) & (m // INV == n // INV)).astype(np.float32), (2, 1)))
    put("mdiagt", np.tile(((m > n) & (m // INV == n // INV)).astype(np.float32), (2, 1)))
    put("moff", np.tile((m // INV < n // INV).astype(np.float32), (2, 1)))
    put("eye64", np.tile(np.eye(CH), (2, 1)))
    d = _spans()
    count = (d >= 0).astype(int) * ((d <= 128).astype(int) + (d % 4 == 0) + (d % 16 == 0))
    put("lncount", np.where(count > 0, np.log(np.maximum(count, 1)), -1e30))
    put("halfpi", np.full((P, 1), math.pi / 2))
    put("eps", np.full((P, 1), EPS))
    put("gneps", np.full((P, 1), GN_EPS))
    return c


def _layout(a):
    f = {k: np.asarray(v) for k, v in a.items()}
    arrays = {}
    arrays["wmain"] = _stream(f["w_in"][0], f["w_out_a"][0], f["w_glu"][0], f["w_out_b"][0], f["w_o"][0],
                              f["w_in_2"][0], f["w_out_2"][0], f["w_gate_up_2"][0])
    arrays["wdown"] = np.stack([_columns(f["w_down_2"][0], slice(j * P, j * P + P)) for j in range(KB)])
    arrays["xt"] = np.ascontiguousarray(f["x"][0].T.reshape(KB, P, L).transpose(1, 0, 2))
    bst = np.zeros((SB, P, TPB, 2, P), np.float32)
    cs = np.zeros((P, 2, STATE_TILES, 32), np.float32)
    for r, (b, c) in enumerate(((f["b_re"][0], f["c_re"][0]), (f["b_im"][0], f["c_im"][0]))):
        for g in range(64):
            j, t, h = g // 8, g % 8 // 2, g % 2
            bst[j, (g % 8) * 16:(g % 8) * 16 + 16, t, r, h * 64:h * 64 + 64] = b[g].T
            cs[h * 64:h * 64 + 64, r, g // 2, h * 16:h * 16 + 16] = c[g].T
    arrays["bst"] = bst.reshape(SB, P, TPB * 2 * P)
    arrays["cs"] = cs
    par = np.zeros((P, NPAR), np.float32)

    def put(name, v):
        at, w = PCOLS[name]
        par[:, at:at + w] = _rows(v)

    put("norm_g", f["norm_g"][0])
    for k in range(3):
        put(f"conv{k}", f["conv_w"][0, k])
    put("final_g", f["final_g"])
    put("norm1", f["norm1_g_2"][0])
    put("norm2", f["norm2_g_2"][0])
    put("final2", f["final_g_2"])
    put("b_glu", f["b_glu"][0])
    put("d_skip", f["d_skip"][0])
    mixv = f["rwkv_shift_mix_2"][0]
    put("mix_rkv", mixv[:3072])
    put("mix_lo", np.concatenate([mixv[3072:], np.zeros(96, np.float32)]))
    for name, key in [("w0", "rwkv_w0_2"), ("a0", "rwkv_a0_2"), ("k_k", "rwkv_k_k_2"), ("k_a", "rwkv_k_a_2"),
                      ("r_k", "rwkv_r_k_2"), ("ln_w", "rwkv_ln_w_2"), ("ln_b", "rwkv_ln_b_2"),
                      ("a_re", "a_re"), ("a_im", "a_im")]:
        put(name, f[key][0])
    put("log_dt", np.repeat(f["log_dt"][0], 64))
    arrays["par"] = par
    arrays["consts"] = _constants()
    arrays["lora"] = np.concatenate([f["rwkv_w_up_2"][0], f["rwkv_a_up_2"][0]], axis=0)
    gup = np.zeros((P, 2, 1024), np.float32)
    gup[:, 0] = f["rwkv_g_up_2"][0][:P]
    gup[:32, 1] = f["rwkv_g_up_2"][0][P:]
    arrays["gup"] = gup
    which = np.vectorize(_bucket)(np.maximum(_spans(), 0))
    table = f["rel_bias_table_2"]
    bias = table[which]
    arrays["bias"] = np.ascontiguousarray(bias.reshape(P, 384, PAIRS, 2).transpose(2, 0, 3, 1)).reshape(PAIRS, P, 768)
    return arrays


_ORDER = ["wmain", "wdown", "bst", "cs", "par", "consts", "xt", "lora", "gup", "bias"]


def kernel(**inputs):
    import concourse.bacc as _bacc
    from concourse.bass_utils import run_bass_kernel_spmd as _run

    arrays = _layout(inputs)
    nc = _bacc.Bacc("TRN2", target_bir_lowering=False, num_devices=1)
    args = [nc.dram_tensor(n, arrays[n].shape, F32, kind="ExternalInput").ap() for n in _ORDER]
    out = nc.dram_tensor("out", (P, KB, L), F32, kind="ExternalOutput").ap()
    hybrid_kernel(nc, *args, out)
    r = _run(nc, [arrays], core_ids=[0])
    return r.results[0]["out"].transpose(2, 1, 0).reshape(1, L, D)
```
